# Optimizing a Trainium2 kernel written in Bass

```python
import math
import jax, jax.numpy as jnp
from jax import lax
import numpy as np

D_MODEL = 1024
BATCH = 1
SEQ = 256
DEPTH = 2

N_A = DEPTH // 2
N_B = DEPTH - N_A
D_FF = 2816
LRU_WIDTH = D_MODEL
LRU_BLOCKS = 4
LRU_BW = LRU_WIDTH // LRU_BLOCKS
CONV_W = 4
LRU_C = 8.0
N_HEADS = 16
HEAD_DIM = 64
D_ATTN = N_HEADS * HEAD_DIM
Q_BLOCK = 128
EPS = 1e-6


def rms_norm(x, gain):
    xf = x.astype(jnp.float32)
    y = xf * lax.rsqrt(jnp.mean(xf * xf, axis=-1, keepdims=True) + EPS)
    return (y * gain.astype(jnp.float32)).astype(x.dtype)

def swiglu(h, w13, w2):
    gate, up = jnp.split(h @ w13, 2, axis=-1)
    return (jax.nn.silu(gate) * up) @ w2

def causal_depthwise_conv(x, w, b):
    S = x.shape[1]
    xp = jnp.pad(x, ((0, 0), (CONV_W - 1, 0), (0, 0)))
    y = b
    for k in range(CONV_W):
        y = y + w[k] * xp[:, k:k + S]
    return y

def block_diag_linear(x, w, b):
    Bt, S, _ = x.shape
    xb = x.reshape(Bt, S, LRU_BLOCKS, LRU_BW)
    y = jnp.einsum('bsnc,ncd->bsnd', xb, w).reshape(Bt, S, LRU_WIDTH)
    return y + b

def linear_recurrence(a, u):
    def step(h, au):
        a_t, u_t = au
        h = a_t * h + u_t
        return h, h
    h0 = jnp.zeros((a.shape[0], a.shape[2]), jnp.float32)
    _, hs = lax.scan(step, h0, (jnp.swapaxes(a, 0, 1), jnp.swapaxes(u, 0, 1)))
    return jnp.swapaxes(hs, 0, 1)

def rglru_block(h, w_in, conv_w, conv_b, w_r, b_r, w_i, b_i, lam, w_out):
    gate_br, rec = jnp.split(h @ w_in, 2, axis=-1)
    gate_br = jax.nn.gelu(gate_br)
    xc = causal_depthwise_conv(rec, conv_w, conv_b)
    r = jax.nn.sigmoid(block_diag_linear(xc, w_r, b_r))
    i = jax.nn.sigmoid(block_diag_linear(xc, w_i, b_i))
    log_a = -LRU_C * r.astype(jnp.float32) * jax.nn.softplus(-lam.astype(jnp.float32))
    a = jnp.exp(log_a)
    mult = jnp.sqrt(-jnp.expm1(2.0 * log_a))
    u = mult * (i * xc).astype(jnp.float32)
    hs = linear_recurrence(a, u)
    y = hs.astype(h.dtype) * gate_br
    return y @ w_out

def heads(t):
    Bt, S, _ = t.shape
    return t.reshape(Bt, S, N_HEADS, HEAD_DIM).transpose(0, 2, 1, 3)

def shared_kv(x, kv_gain, w_kv, k_gain):
    hkv = rms_norm(x, kv_gain)
    k, v = jnp.split(hkv @ w_kv, 2, axis=-1)
    k = rms_norm(heads(k), k_gain)
    return k, heads(v)

def stick_breaking_attention(q, k, v):
    S = q.shape[2]
    scale = HEAD_DIM ** -0.5
    outs = []
    for blk in range(S // Q_BLOCK):
        q0 = blk * Q_BLOCK
        end = q0 + Q_BLOCK
        z = jnp.einsum('bhqd,bhkd->bhqk', q[:, :, q0:end], k[:, :, :end]).astype(jnp.float32) * scale
        t_pos = q0 + jnp.arange(Q_BLOCK)[:, None]
        s_pos = jnp.arange(end)[None, :]
        mask = s_pos < t_pos
        log_stay = jnp.where(mask, -jax.nn.softplus(z), 0.0)
        stay_after = lax.cumsum(log_stay, axis=3, reverse=True) - log_stay
        log_w = jax.nn.log_sigmoid(z) + stay_after
        w = jnp.where(mask, jnp.exp(log_w), 0.0)
        o = jnp.einsum('bhqk,bhkd->bhqd', w, v[:, :, :end].astype(jnp.float32))
        outs.append(o.astype(v.dtype))
    return jnp.concatenate(outs, axis=2)

def stick_breaking_block(h, k, v, w_q, q_gain, w_o):
    q = rms_norm(heads(h @ w_q), q_gain)
    o = stick_breaking_attention(q, k, v)
    Bt, _, S, _ = o.shape
    o = o.transpose(0, 2, 1, 3).reshape(Bt, S, D_ATTN)
    return o @ w_o

def first_inputs(seed: int = 0) -> dict:
    key = jax.random.key(seed)
    keys = jax.random.split(key, 32)
    counter = [0]
    f32 = jnp.float32

    def nk():
        k = keys[counter[0]]
        counter[0] += 1
        return k

    def w(shape, fan_in, scale=1.0):
        return jax.random.normal(nk(), shape, f32) * (scale * fan_in ** -0.5)

    def gain(shape):
        return 1.0 + 0.02 * jax.random.normal(nk(), shape, f32)

    def bias(shape):
        return 0.02 * jax.random.normal(nk(), shape, f32)

    a0 = jax.random.uniform(nk(), (N_A, LRU_WIDTH), f32, 0.9, 0.999)
    return {
        "x": jax.random.normal(nk(), (BATCH, SEQ, D_MODEL), f32),
        "ffn1_norm": gain((DEPTH, D_MODEL)),
        "ffn1_w13": w((DEPTH, D_MODEL, 2 * D_FF), D_MODEL),
        "ffn1_w2": w((DEPTH, D_FF, D_MODEL), D_FF, 0.5),
        "mix_norm": gain((DEPTH, D_MODEL)),
        "a_w_in": w((N_A, D_MODEL, 2 * LRU_WIDTH), D_MODEL),
        "a_conv_w": w((N_A, CONV_W, LRU_WIDTH), CONV_W),
        "a_conv_b": bias((N_A, LRU_WIDTH)),
        "a_w_r": w((N_A, LRU_BLOCKS, LRU_BW, LRU_BW), LRU_BW),
        "a_b_r": bias((N_A, LRU_WIDTH)),
        "a_w_i": w((N_A, LRU_BLOCKS, LRU_BW, LRU_BW), LRU_BW),
        "a_b_i": bias((N_A, LRU_WIDTH)),
        "a_lambda": jnp.log(a0) - jnp.log1p(-a0),
        "a_w_out": w((N_A, LRU_WIDTH, D_MODEL), LRU_WIDTH),
        "kv_norm": gain((D_MODEL,)),
        "w_kv": w((D_MODEL, 2 * D_ATTN), D_MODEL),
        "k_norm": gain((HEAD_DIM,)),
        "b_w_q": w((N_B, D_MODEL, D_ATTN), D_MODEL),
        "q_norm": gain((N_B, HEAD_DIM)),
        "b_w_o": w((N_B, D_ATTN, D_MODEL), D_ATTN),
        "ffn2_norm": gain((DEPTH, D_MODEL)),
        "ffn2_w13": w((DEPTH, D_MODEL, 2 * D_FF), D_MODEL),
        "ffn2_w2": w((DEPTH, D_FF, D_MODEL), D_FF, 0.5),
    }

def first_block(x, ffn1_norm, ffn1_w13, ffn1_w2, mix_norm, a_w_in, a_conv_w, a_conv_b,
              a_w_r, a_b_r, a_w_i, a_b_i, a_lambda, a_w_out, kv_norm, w_kv, k_norm,
              b_w_q, q_norm, b_w_o, ffn2_norm, ffn2_w13, ffn2_w2):
    k_shared = None
    v_shared = None
    for l in range(DEPTH):
        if l == N_A:
            k_shared, v_shared = shared_kv(x, kv_norm, w_kv, k_norm)
        x = x + 0.5 * swiglu(rms_norm(x, ffn1_norm[l]), ffn1_w13[l], ffn1_w2[l])
        h = rms_norm(x, mix_norm[l])
        if l < N_A:
            x = x + rglru_block(h, a_w_in[l], a_conv_w[l], a_conv_b[l], a_w_r[l], a_b_r[l],
                                a_w_i[l], a_b_i[l], a_lambda[l], a_w_out[l])
        else:
            j = l - N_A
            x = x + stick_breaking_block(h, k_shared, v_shared, b_w_q[j], q_norm[j], b_w_o[j])
        x = x + 0.5 * swiglu(rms_norm(x, ffn2_norm[l]), ffn2_w13[l], ffn2_w2[l])
    return x


GRID_W = 64
CTX_LEN = 256
FOUR_GROUPS = 4
FOUR_GC = D_MODEL // 8
FOUR_WIDTH = FOUR_GROUPS * FOUR_GC
NA_HEADS = 8
NA_HEAD_DIM = D_MODEL // 16
NA_WIDTH = NA_HEADS * NA_HEAD_DIM
NA_WIN_ROWS = 8
NA_WIN_COLS = 16
POOL_SIZES = (2, 4, 8, 16)
POOL_GC = D_MODEL // len(POOL_SIZES)
MLP_HIDDEN = 4 * D_MODEL
N_MOD = 6
RMS_EPS = 1e-6
N_EVEN = (DEPTH + 1) // 2
N_ODD = DEPTH // 2


def rms_norm_2(x, g):
    xf = x.astype(jnp.float32)
    y = xf * lax.rsqrt(jnp.mean(xf * xf, axis=-1, keepdims=True) + RMS_EPS)
    return (y * g.astype(jnp.float32)).astype(x.dtype)

def modulate(xn, shift, scale):
    return xn * (1.0 + scale) + shift

def sq_relu_mlp(u, w1, w2):
    a = jnp.maximum(u @ w1, 0.0)
    return (a * a) @ w2

def fourier_mix(f, w_four):
    B, N, _ = f.shape
    fg = f.reshape(B, N, FOUR_GROUPS, FOUR_GC).transpose(0, 2, 1, 3)
    mixed = jnp.fft.fft2(fg.astype(jnp.float32), norm="ortho").real.astype(f.dtype)
    out = jnp.einsum('bgnc,gcd->bngd', mixed, w_four)
    return out.reshape(B, N, FOUR_WIDTH)

def neighbourhood_attention(q, k, v, k_ctx, v_ctx, rpb):
    B, N, H, dh = q.shape
    rows = N // GRID_W
    wr = min(NA_WIN_ROWS, rows)

    def to_grid(a):
        return a.reshape(B, rows, GRID_W, H, dh).transpose(0, 3, 1, 2, 4)

    qg, kg, vg = to_grid(q), to_grid(k), to_grid(v)
    r = jnp.arange(rows)
    row_start = jnp.clip(r - wr // 2, 0, rows - wr)
    row_idx = row_start[:, None] + jnp.arange(wr)[None, :]
    kb = kg[:, :, row_idx]
    vb = vg[:, :, row_idx]
    cidx = jnp.arange(GRID_W)
    col_start = jnp.clip(cidx - NA_WIN_COLS // 2, 0, GRID_W - NA_WIN_COLS)
    col_mask = (cidx[None, :] >= col_start[:, None]) & (cidx[None, :] < col_start[:, None] + NA_WIN_COLS)
    dr = row_idx - r[:, None] + (NA_WIN_ROWS - 1)
    dc = jnp.clip(cidx[None, :] - cidx[:, None] + (NA_WIN_COLS - 1), 0, 2 * NA_WIN_COLS - 2)
    bias = rpb[:, dr[:, None, :, None], dc[None, :, None, :]]
    scale = dh ** -0.5
    s_win = jnp.einsum('bhrqd,bhrjkd->bhrqjk', qg, kb).astype(jnp.float32) * scale + bias.astype(jnp.float32)
    s_win = jnp.where(col_mask[:, None, :], s_win, -jnp.inf)
    s_win = s_win.reshape(B, H, rows, GRID_W, wr * GRID_W)
    s_ctx = jnp.einsum('bhrqd,blhd->bhrql', qg, k_ctx).astype(jnp.float32) * scale
    p = jax.nn.softmax(jnp.concatenate([s_win, s_ctx], axis=-1), axis=-1)
    p_win = p[..., :wr * GRID_W].reshape(B, H, rows, GRID_W, wr, GRID_W).astype(v.dtype)
    p_ctx = p[..., wr * GRID_W:].astype(v.dtype)
    o = jnp.einsum('bhrqjk,bhrjkd->bhrqd', p_win, vb) + jnp.einsum('bhrql,blhd->bhrqd', p_ctx, v_ctx)
    return o.transpose(0, 2, 3, 1, 4).reshape(B, N, H * dh)

def context_attention(qc, kc, vc):
    B, L, H, dh = qc.shape
    s = jnp.einsum('blhd,bmhd->bhlm', qc, kc).astype(jnp.float32) * (dh ** -0.5)
    p = jax.nn.softmax(s, axis=-1).astype(vc.dtype)
    return jnp.einsum('bhlm,bmhd->blhd', p, vc).reshape(B, L, H * dh)

def split_heads(a):
    return a.reshape(a.shape[0], a.shape[1], NA_HEADS, NA_HEAD_DIM)

def even_mixer(u, uc, w_in, w_four, q_g, k_g, rpb, w_out, update_ctx):
    p = u @ w_in
    f, q, k, v = jnp.split(p, [FOUR_WIDTH, FOUR_WIDTH + NA_WIDTH, FOUR_WIDTH + 2 * NA_WIDTH], axis=-1)
    q = rms_norm_2(split_heads(q), q_g)
    k = rms_norm_2(split_heads(k), k_g)
    v = split_heads(v)
    kvc = uc @ w_in[:, FOUR_WIDTH + NA_WIDTH:]
    kc, vc = jnp.split(kvc, [NA_WIDTH], axis=-1)
    kc = rms_norm_2(split_heads(kc), k_g)
    vc = split_heads(vc)
    o_four = fourier_mix(f, w_four)
    o_na = neighbourhood_attention(q, k, v, kc, vc, rpb)
    y = jnp.concatenate([o_four, o_na], axis=-1) @ w_out
    if not update_ctx:
        return y, None
    fc, qc = jnp.split(uc @ w_in[:, :FOUR_WIDTH + NA_WIDTH], [FOUR_WIDTH], axis=-1)
    qc = rms_norm_2(split_heads(qc), q_g)
    yc = jnp.concatenate([fourier_mix(fc, w_four), context_attention(qc, kc, vc)], axis=-1) @ w_out
    return y, yc

def multiscale_pool(u):
    N = u.shape[1]
    uf = u.astype(jnp.float32)
    zeros = jnp.zeros((uf.shape[0], 1, uf.shape[2]), jnp.float32)
    cs = jnp.concatenate([zeros, jnp.cumsum(uf, axis=1)], axis=1)
    t = jnp.arange(N)
    outs = []
    for gi, w in enumerate(POOL_SIZES):
        sl = slice(gi * POOL_GC, (gi + 1) * POOL_GC)
        lo = jnp.clip(t - w // 2, 0, N)
        hi = jnp.clip(t + w - w // 2, 0, N)
        csg = cs[..., sl]
        s = jnp.take(csg, hi, axis=1) - jnp.take(csg, lo, axis=1)
        cnt = (hi - lo).astype(jnp.float32)[None, :, None]
        outs.append(s / cnt - uf[..., sl])
    return jnp.concatenate(outs, axis=-1).astype(u.dtype)

def pool_mixer(u, w_pool, pool_scale):
    B, N, _ = u.shape
    pooled = multiscale_pool(u).reshape(B, N, len(POOL_SIZES), POOL_GC)
    y = jnp.einsum('bngc,gcd->bngd', pooled, w_pool).reshape(B, N, D_MODEL)
    return y * pool_scale

def second_inputs(seed: int = 0) -> dict:
    key = jax.random.key(seed)
    ks = jax.random.split(key, 20)
    f32 = jnp.float32
    n = lambda k, s: jax.random.normal(k, s, f32)
    return {
        "x": n(ks[0], (BATCH, SEQ, D_MODEL)),
        "c": n(ks[1], (BATCH, D_MODEL)),
        "ctx": n(ks[2], (BATCH, CTX_LEN, D_MODEL)),
        "c_ctx": n(ks[3], (D_MODEL,)),
        "w_mod": n(ks[4], (DEPTH, D_MODEL, N_MOD * D_MODEL)) * D_MODEL ** -0.5,
        "b_mod": n(ks[5], (DEPTH, N_MOD * D_MODEL)) * 0.02,
        "norm1_g": 1.0 + 0.02 * n(ks[6], (DEPTH, D_MODEL)),
        "norm2_g": 1.0 + 0.02 * n(ks[7], (DEPTH, D_MODEL)),
        "w_in_even": n(ks[8], (N_EVEN, D_MODEL, FOUR_WIDTH + 3 * NA_WIDTH)) * D_MODEL ** -0.5,
        "w_four": n(ks[9], (N_EVEN, FOUR_GROUPS, FOUR_GC, FOUR_GC)) * FOUR_GC ** -0.5,
        "q_norm_g": 1.0 + 0.02 * n(ks[10], (N_EVEN, NA_HEAD_DIM)),
        "k_norm_g": 1.0 + 0.02 * n(ks[11], (N_EVEN, NA_HEAD_DIM)),
        "rpb": 0.1 * n(ks[12], (N_EVEN, NA_HEADS, 2 * NA_WIN_ROWS - 1, 2 * NA_WIN_COLS - 1)),
        "w_out_even": n(ks[13], (N_EVEN, FOUR_WIDTH + NA_WIDTH, D_MODEL)) * (FOUR_WIDTH + NA_WIDTH) ** -0.5,
        "w_pool": n(ks[14], (N_ODD, len(POOL_SIZES), POOL_GC, POOL_GC)) * POOL_GC ** -0.5,
        "pool_scale": 1.0 + 0.1 * n(ks[15], (N_ODD, D_MODEL)),
        "w_mlp1": n(ks[16], (DEPTH, D_MODEL, MLP_HIDDEN)) * D_MODEL ** -0.5,
        "w_mlp2": n(ks[17], (DEPTH, MLP_HIDDEN, D_MODEL)) * MLP_HIDDEN ** -0.5,
    }

def second_block(x, c, ctx, c_ctx, w_mod, b_mod, norm1_g, norm2_g, w_in_even, w_four, q_norm_g, k_norm_g,
              rpb, w_out_even, w_pool, pool_scale, w_mlp1, w_mlp2):
    h, hc = x, ctx
    sc = jax.nn.silu(c)
    scc = jax.nn.silu(c_ctx)
    for l in range(DEPTH):
        update_ctx = any(j % 2 == 0 for j in range(l + 1, DEPTH))
        need_ctx_in = (l % 2 == 0) or update_ctx
        mod = (sc @ w_mod[l] + b_mod[l])[:, None, :]
        sh1, sc1, g1, sh2, sc2, g2 = jnp.split(mod, N_MOD, axis=-1)
        u = modulate(rms_norm_2(h, norm1_g[l]), sh1, sc1)
        if need_ctx_in:
            mod_c = scc @ w_mod[l] + b_mod[l]
            csh1, csc1, cg1, csh2, csc2, cg2 = jnp.split(mod_c, N_MOD, axis=-1)
            uc = modulate(rms_norm_2(hc, norm1_g[l]), csh1, csc1)
        if l % 2 == 0:
            e = l // 2
            y, yc = even_mixer(u, uc, w_in_even[e], w_four[e], q_norm_g[e], k_norm_g[e], rpb[e],
                               w_out_even[e], update_ctx)
        else:
            o = l // 2
            y = pool_mixer(u, w_pool[o], pool_scale[o])
            yc = pool_mixer(uc, w_pool[o], pool_scale[o]) if update_ctx else None
        h = h + g1 * y
        h = h + g2 * sq_relu_mlp(modulate(rms_norm_2(h, norm2_g[l]), sh2, sc2), w_mlp1[l], w_mlp2[l])
        if update_ctx:
            hc = hc + cg1 * yc
            hc = hc + cg2 * sq_relu_mlp(modulate(rms_norm_2(hc, norm2_g[l]), csh2, csc2), w_mlp1[l], w_mlp2[l])
    return h


def setup_inputs(seed=0):
    out = dict(first_inputs(seed))
    for name, value in second_inputs(seed + 1).items():
        if name != "x":
            out[name + "_2"] = value
    return out


def reference(
    x, ffn1_norm, ffn1_w13, ffn1_w2, mix_norm, a_w_in, a_conv_w, a_conv_b, a_w_r, a_b_r, a_w_i,
    a_b_i, a_lambda, a_w_out, kv_norm, w_kv, k_norm, b_w_q, q_norm, b_w_o, ffn2_norm, ffn2_w13,
    ffn2_w2, c_2, ctx_2, c_ctx_2, w_mod_2, b_mod_2, norm1_g_2, norm2_g_2, w_in_even_2, w_four_2,
    q_norm_g_2, k_norm_g_2, rpb_2, w_out_even_2, w_pool_2, pool_scale_2, w_mlp1_2, w_mlp2_2,
):
    x = first_block(
        x, ffn1_norm, ffn1_w13, ffn1_w2, mix_norm, a_w_in, a_conv_w, a_conv_b, a_w_r, a_b_r,
        a_w_i, a_b_i, a_lambda, a_w_out, kv_norm, w_kv, k_norm, b_w_q, q_norm, b_w_o, ffn2_norm,
        ffn2_w13, ffn2_w2,
    )
    return second_block(
        x, c_2, ctx_2, c_ctx_2, w_mod_2, b_mod_2, norm1_g_2, norm2_g_2, w_in_even_2, w_four_2,
        q_norm_g_2, k_norm_g_2, rpb_2, w_out_even_2, w_pool_2, pool_scale_2, w_mlp1_2, w_mlp2_2,
    )


_drawn_inputs = setup_inputs


def setup_inputs(seed=0):
    import zlib

    import numpy as np

    out = dict(_drawn_inputs(seed))
    spreads = {}
    factors = {'ffn1_norm': 8.0,
     'mix_norm': 4.568,
     'a_b_r': 8.0,
     'a_b_i': 8.0,
     'kv_norm': 5.112,
     'k_norm': 8.0,
     'q_norm': 8.0,
     'ffn2_norm': 8.0,
     'norm1_g_2': 7.466,
     'norm2_g_2': 14.7,
     'q_norm_g_2': 24.853,
     'k_norm_g_2': 8.0,
     'rpb_2': 64.0,
     'pool_scale_2': 28.168}
    for name, (base, spread) in spreads.items():
        noise = np.random.default_rng([zlib.crc32(name.encode()), seed]).standard_normal(out[name].shape)
        drawn = base * np.exp(spread * noise) if base else spread * noise
        out[name] = __import__('jax').numpy.asarray(drawn.astype(out[name].dtype))
    for name, factor in factors.items():
        out[name] = (out[name] * factor).astype(out[name].dtype)
    return out
```

```python
from contextlib import ExitStack

import numpy as np
from concourse import bass, mybir

F32 = mybir.dt.float32
F32R = mybir.dt.float32r
ALU = mybir.AluOpType
ACT = mybir.ActivationFunctionType
AX_X = mybir.AxisListType.X

P = 128
D = 1024
T = 256
NC = D // P
FF = 2816
FFS = FF // P
MLP = 4096
MLS = MLP // P // 2
CONV = 4
HD = 64
EPS = 1e-6
NMOD = 6
BIG = -1e30

UNIT = 1024
RING = 8
AHEAD = 5

FFU = 4 * FFS + 2
MODG = 6
PHASES = [("ffn0", FFU), ("rec", 8), ("gate", 8), ("r", 2), ("i", 2), ("wout", 8), ("ffn1", FFU),
          ("k", 8), ("v", 8), ("ffn2", FFU), ("q", 8), ("wo", 8), ("ffn3", FFU),
          ("fq2", 8), ("k2", 4), ("v2", 4), ("four", 2), ("woe", 8), ("mlp0", 4 * MLS),
          ("pool", 2), ("mlp1", 4 * MLS)]
AT = {}
_n = 0
for _name, _count in PHASES:
    AT[_name] = _n
    _n += _count
UNITS = _n
assert UNITS % RING == 0

SMALL = ["ffn1_0", "ffn1_1", "mix_0", "mix_1", "kv", "ffn2_0", "ffn2_1", "n1_0", "n1_1", "n2_0", "n2_1",
         "cw0", "cw1", "cw2", "cw3", "cb", "br", "bi", "lam", "pscale"]
COL = {n: NC * i for i, n in enumerate(SMALL)}
COL["cond"] = NC * len(SMALL)
COL["bmod"] = COL["cond"] + 2 * NC
COL["kg"] = COL["bmod"] + 2 * NMOD * NC
COL["qg"], COL["qg2"], COL["kg2"] = COL["kg"] + 1, COL["kg"] + 2, COL["kg"] + 3
NSMALL = COL["kg"] + 4

CC = {"ident": 0, "ones": 128, "tri": 256, "headsum": 384, "stick": 512, "colmask": 896, "headbc": 960}
NCONST = CC["headbc"] + NC * P
NLATE = 1024 + 2 * P
STICK = T + P
TABW = 4 * 6 * HD

TY = {n: NC * i for i, n in enumerate(["cond", "cond2", "negabs", "e", "den", "q", "q2", "poly", "sp8", "nsp8", "relu",
                                       "G1", "Gc", "G2", "H1", "H2", "Gp", "na"])}

OPS = {n: i for i, n in enumerate("ffn0 mix0 y ffn1 kv ffn2 mix1 att ffn3 even mixed mlp0 pooled mlp1".split())}
ACC = {n: i for i, n in enumerate("ffn0 rec gate r i wout ffn1 k v ffn2 q wo ffn3 fq2 k2 v2 woe mlp0 pool mlp1".split())}
RD = {n: i for i, n in enumerate("ffn0 rec gate wout ffn1 k v ffn2 q wo ffn3 fq2 k2 v2 woe mlp0 pool mlp1".split())}
NORMS = "start ffn0 wout ffn1 ctx ffn2 wo ffn3 woe mlp0 pool".split()
NRM = {n: i for i, n in enumerate(NORMS)}
HN = {"k": 0, "q": 1, "q2": 2, "k2": 3}
HNP = {"k": 0, "q": 4, "q2": 8, "k2": 10}
HEAD_BANK = {"k": 0, "q": 4, "q2": 4, "k2": 5}
STEPS = {"ffn0": 0, "ffn1": FFS, "ffn2": 2 * FFS, "ffn3": 3 * FFS, "mlp0": 4 * FFS, "mlp1": 4 * FFS + MLS}


class Signals:

    def __init__(self, sem):
        self.params_in = sem("params_in")
        self.consts_in = sem("consts_in")
        self.x_in = sem("x_in")
        self.ctx_in = sem("ctx_in")
        self.late_in = sem("late_in")
        self.cnt_in = sem("cnt_in")
        self.out_done = sem("out_done")
        self.hi_ready = sem("hi_ready")
        self.lo_ready = sem("lo_ready")
        self.unit_used = sem("unit_used")
        self.operand_hi = sem("operand_hi")
        self.operand_ready = sem("operand_ready")
        self.acc_ready = sem("acc_ready")
        self.acc_read = sem("acc_read")
        self.sq_ready = sem("sq_ready")
        self.pool_sum = sem("pool_sum")
        self.ssq_ready = sem("ssq_ready")
        self.ms_psum = sem("ms_psum")
        self.ms_ready = sem("ms_ready")
        self.root_ready = sem("root_ready")
        self.up_ready = sem("up_ready")
        self.up_scaled = sem("up_scaled")
        self.gated = sem("gated")
        self.hid_f32 = sem("hid_f32")
        self.hid_hi_ready = sem("hid_hi_ready")
        self.hid_ready = sem("hid_ready")
        self.cond_silu = sem("cond_silu")
        self.cond_hi_ready = sem("cond_hi_ready")
        self.cond_ready = sem("cond_ready")
        self.mod_rows = sem("mod_rows")
        self.mod_copied = sem("mod_copied")
        self.mod_turned = sem("mod_turned")
        self.mod_read = sem("mod_read")
        self.dve_chain = sem("dve_chain")
        self.lam_abs = sem("lam_abs")
        self.lam_exp = sem("lam_exp")
        self.lam_ready = sem("lam_ready")
        self.conv_first = sem("conv_first")
        self.conv_tap = sem("conv_tap")
        self.xc_hi = sem("xc_hi")
        self.xc_lo = sem("xc_lo")
        self.gelu_done = sem("gelu_done")
        self.gates_read = sem("gates_read")
        self.mixed_in = sem("mixed_in")
        self.lru_tanh = sem("lru_tanh")
        self.lru_decay = sem("lru_decay")
        self.lru_m2 = sem("lru_m2")
        self.lru_sqrt = sem("lru_sqrt")
        self.lru_y = sem("lru_y")
        self.head_sq = sem("head_sq")
        self.head_sum = sem("head_sum")
        self.head_ms = sem("head_ms")
        self.head_root = sem("head_root")
        self.head_rs = sem("head_rs")
        self.head_bc = sem("head_bc")
        self.normed = sem("normed")
        self.v_turned = sem("v_turned")
        self.v_out = sem("v_out")
        self.z_ready = sem("z_ready")
        self.z_masked = sem("z_masked")
        self.z_abs = sem("z_abs")
        self.e_ready = sem("e_ready")
        self.l_ready = sem("l_ready")
        self.sp_ready = sem("sp_ready")
        self.cum_ready = sem("cum_ready")
        self.w_arg = sem("w_arg")
        self.w_ready = sem("w_ready")
        self.o_ready = sem("o_ready")
        self.ctx_full = sem("ctx_full")
        self.ctx_hi = sem("ctx_hi")
        self.ctx_lo = sem("ctx_lo")
        self.full_ready = sem("full_ready")
        self.v2_turned = sem("v2_turned")
        self.v2_out = sem("v2_out")
        self.f_turned = sem("f_turned")
        self.f_out = sem("f_out")
        self.dft1 = sem("dft1")
        self.dft1_out = sem("dft1_out")
        self.dft2 = sem("dft2")
        self.mixed_hi = sem("mixed_hi")
        self.mixed_lo = sem("mixed_lo")
        self.dft3 = sem("dft3")
        self.pooled = sem("pooled")
        self.tab_ready = sem("tab_ready")
        self.na_z = sem("na_z")
        self.na_s = sem("na_s")
        self.na_max = sem("na_max")
        self.na_e = sem("na_e")
        self.na_p = sem("na_p")
        self.na_t = sem("na_t")
        self.na_tout = sem("na_tout")
        self.na_o = sem("na_o")


def build(nc, stream, x_in, ctx_in, small, consts, late, cnt, tab, out):
    with ExitStack() as es:
        def sb(name, cols, dt=F32):
            return es.enter_context(nc.sbuf_tensor(name, [P, cols], dt))

        raw = sb("raw", RING * UNIT)
        w_hi = sb("w_hi", RING * UNIT, F32R)
        w_lo = sb("w_lo", RING * UNIT, F32R)
        x_t = sb("x", NC * T)
        u_hi_t = sb("u_hi", NC * 2 * T, F32R)
        u_lo_t = sb("u_lo", NC * 2 * T, F32R)
        hid_hi_t = sb("hid_hi", 2 * 512, F32R)
        hid_lo_t = sb("hid_lo", 2 * 512, F32R)
        cond_t = sb("cond", 4 * NC, F32R)
        rstd = sb("rstd", T)
        nrm = sb("nrm", 1024)
        prm = sb("prm", NSMALL)
        cst = sb("cst", NCONST)
        mod_t = sb("mod", 2 * NMOD * NC * 2)
        tiny = sb("tiny", NC * len(TY))
        buf = [sb(f"buf{n}", 2048) for n in range(5)]
        buf5 = sb("buf5", NC * (T + CONV - 1))
        psum = es.enter_context(nc.psum_tensor("psum", [P, 8, 512], F32))

        x = x_t[:, :].rearrange("p (k t) -> p k t", k=NC)
        u_hi = u_hi_t[:, :].rearrange("p (k t) -> p k t", k=NC)
        u_lo = u_lo_t[:, :].rearrange("p (k t) -> p k t", k=NC)
        u_hif = u_hi_t[:, :].bitcast(F32).rearrange("p (k t) -> p k t", k=NC)
        hid_hi = hid_hi_t[:, :].rearrange("p (s t) -> p s t", s=2)
        hid_lo = hid_lo_t[:, :].rearrange("p (s t) -> p s t", s=2)
        hid_hif = hid_hi_t[:, :].bitcast(F32).rearrange("p (s t) -> p s t", s=2)
        cond = cond_t[:, :].rearrange("p (k c) -> p k c", c=4)
        condf = cond_t[:, :].bitcast(F32).rearrange("p (k c) -> p k c", c=4)
        mod = mod_t[:, :].rearrange("p (l j c) -> p l j c", l=2, c=2)
        pad = buf5[:, :].rearrange("p (k t) -> p k t", k=NC)
        t2, sil, h32 = buf5[:, 0:512], buf5[:, 512:768], buf5[:, 768:1280]
        mod_rows = buf5[0:4, 1280:1792]
        ms, root_t = nrm[:, 0:512], nrm[:, 512:1024]
        head_rs = buf5[:, 1536:2048]
        ident, ones, tri = (cst[:, CC[n]:CC[n] + P] for n in ("ident", "ones", "tri"))
        headsum = cst[:, CC["headsum"]:CC["headsum"] + P].rearrange("p (k h) -> p k h", k=NC)
        headbc = cst[0:16, CC["headbc"]:CC["headbc"] + NC * P].rearrange("p (k n) -> p k n", k=NC)
        stick = cst[:, CC["stick"]:CC["stick"] + STICK]
        colmask = cst[:, CC["colmask"]:CC["colmask"] + HD]
        inv_cnt = cst[:, CC["headbc"]:CC["headbc"] + 4 * T].rearrange("p (g t) -> p g t", g=4)

        def ck(t, k=NC):
            return t[:, :].rearrange("p (k t) -> p k t", k=k)

        def col(name, k=0, n=1):
            return prm[:, COL[name] + k:COL[name] + k + n]

        def ty(name, k=0, n=1):
            return tiny[:, TY[name] + k:TY[name] + k + n]

        def half(b):
            return slice(b * 512, (b + 1) * 512)

        def bank2(b):
            return psum[:, b, :].rearrange("p (k t) -> p k t", k=2)

        def over2(row):
            return row.unsqueeze(1).broadcast_to([P, 2, T])

        def sem(name):
            return es.enter_context(nc.semaphore(name))

        S = Signals(sem)
        raw_landed = [sem(f"raw_landed{n}") for n in range(RING // 2)]
        tab_in = [sem(f"tab_in{n}") for n in range(2)]
        block = es.enter_context(nc.Block())

        @block.sync
        def _(sp):
            sp.dma_start(prm[:, :], small).then_inc(S.params_in, 16)
            sp.dma_start(x_t[:, :], x_in).then_inc(S.x_in, 16)

            def load(pair, src, i=0):
                slot = pair % (RING // 2)
                sp.dma_start(raw[:, 2 * slot * UNIT:2 * (slot + 1) * UNIT], src).then_inc(raw_landed[slot], 16)

            for pair in range(RING // 2):
                load(pair, stream[pair])
                if pair == 0:
                    sp.dma_start(cst[:, :], consts).then_inc(S.consts_in, 16)
            with sp.Fori(1, UNITS // RING) as i:
                for slot in range(RING // 2):
                    sp.wait_ge(S.lo_ready, RING * i + 2 * slot + 2 - RING)
                    load(slot, stream[i * (RING // 2) + slot])
            sp.wait_ge(S.out_done, 4 * 16)

        @block.gpsimd
        def _(pool):
            gp = nc.gpsimd

            def sum_squares(n):
                for b in range(1, 4):
                    pool.wait_ge(S.sq_ready, 4 * n + b + 1)
                    if b > 1:
                        pool.wait_ge(S.pool_sum, 3 * n + b - 1)
                    a = buf[4][:, half(0)]
                    gp.tensor_tensor(a, a, buf[4][:, half(b)], ALU.add).then_inc(S.pool_sum, 1)
                pool.wait_ge(S.pool_sum, 3 * n + 3)
                gp.tensor_tensor(buf[4][:, 0:T], buf[4][:, 0:T], buf[4][:, T:2 * T], ALU.add).then_inc(S.ssq_ready, 1)

            for n, name in enumerate(NORMS):
                if name == "ctx":
                    pool.dma_start(buf[3][:, :], ctx_in).then_inc(S.ctx_in, 16)
                if name == "woe":
                    pool.wait_ge(S.acc_ready, 4 * ACC["ffn3"] + 4)
                    pool.dma_start(buf5[:, 0:NLATE], late).then_inc(S.late_in, 16)
                    pool.wait_ge(S.v2_turned, 4)
                    pool.dma_start(buf[2][:, 0:TABW], tab[0]).then_inc(tab_in[0], 16)
                    pool.wait_ge(S.mixed_lo, 4)
                    pool.dma_start(buf[4][:, 0:TABW], tab[1]).then_inc(tab_in[1], 16)
                    pool.wait_ge(S.normed, HNP["k2"] + 4)
                    pool.dma_start(cst[:, CC["headbc"]:CC["headbc"] + 4 * T], cnt).then_inc(S.cnt_in, 16)
                sum_squares(n)

        @block.scalar
        def _(act):
            sc = nc.scalar
            nxt = [0]

            def split_hi(c, i=0):
                slot = c % RING
                act.wait_ge(raw_landed[slot // 2], 16 * (c // RING + 1 + i))
                if c >= RING or not isinstance(i, int):
                    act.wait_ge(S.unit_used, RING * i + c - RING + 2)
                u = slice(slot * UNIT, (slot + 1) * UNIT)
                sc.activation(w_hi[:, u], raw[:, u], ACT.Copy).then_inc(S.hi_ready, 1)

            def pump_to(last):
                while nxt[0] <= min(last, UNITS - 1):
                    split_hi(nxt[0])
                    nxt[0] += 1

            def x_updated(name, b):
                if name == "start":
                    act.wait_ge(S.x_in, 16)
                    act.wait_ge(S.params_in, 16)
                else:
                    act.wait_ge(S.acc_read, 4 * RD[name] + b + 1)

            def square(n, src, b):
                if b == 0 and n:
                    act.wait_ge(S.ms_psum, n)
                sc.activation(buf[4][:, half(b)], src[:, half(b)], ACT.Square).then_inc(S.sq_ready, 1)

            def root(n):
                act.wait_ge(S.ms_ready, n + 1)
                sc.activation(root_t[:, 0:T], ms[:, 0:T], ACT.Sqrt).then_inc(S.root_ready, 1)

            def gain_operand(gain, name, norm=True):
                for b in range(4):
                    x_updated(name, b)
                    for k in (2 * b, 2 * b + 1):
                        sc.activation(u_hi[:, k, 0:T], x[:, k, :], ACT.Identity, scale=col(gain, k))\
                          .then_inc(S.operand_hi, 1)
                    if norm:
                        square(NRM[name], x_t, b)
                if norm:
                    root(NRM[name])

            def norm_only(name):
                for b in range(4):
                    x_updated(name, b)
                    square(NRM[name], x_t, b)
                root(NRM[name])

            def buffer_operand(src, ready, base=0):
                for b in range(4):
                    act.wait_ge(ready, base + b + 1)
                    sc.activation(u_hi[:, 2 * b:2 * b + 2, 0:T], ck(src)[:, 2 * b:2 * b + 2, :], ACT.Copy)\
                      .then_inc(S.operand_hi, 2)

            def swiglu(name):
                c0, h0, g0 = AT[name], STEPS[name], MODG * int(name[3])
                assert nxt[0] == c0 + AHEAD

                def copy_rows(g):
                    act.wait_ge(S.mod_rows, g + 1)
                    if not isinstance(g, int) or g:
                        act.wait_ge(S.mod_turned, g)
                    sc.activation(mod_rows, psum[0:4, 6, :], ACT.Copy).then_inc(S.mod_copied, 1)

                def hidden(j, par, c, i=0, n_units=4):
                    act.wait_ge(S.up_scaled, h0 + j + 1)
                    sc.activation(sil, t2[:, 0:T], ACT.Silu).then_inc(S.gated, 1)
                    split_hi(c, i)
                    if n_units > 1:
                        split_hi(c + 1, i)
                    act.wait_ge(S.hid_f32, h0 + j + 1)
                    sc.activation(hid_hi[:, par, 0:T], h32[:, 0:T], ACT.Copy).then_inc(S.hid_hi_ready, 1)
                    for n in range(2, n_units):
                        split_hi(c + n, i)

                for n in range(5):
                    split_hi(c0 + n + AHEAD)
                with act.Fori(0, (FFS - 2) // 4) as i:
                    for s in range(4):
                        hidden(4 * i + s, s % 2, c0 + 5 + 4 * s + AHEAD, 2 * i)
                        if s == 1:
                            copy_rows(g0 + i)
                hidden(FFS - 2, 0, c0 + FFU - 5 + AHEAD)
                hidden(FFS - 1, 1, c0 + FFU - 1 + AHEAD, n_units=1)
                copy_rows(g0 + MODG - 1)
                nxt[0] = c0 + FFU + AHEAD

            def sqrelu(name):
                c0, h0 = AT[name], STEPS[name]
                assert nxt[0] == c0 + AHEAD

                def hidden(j, par):
                    act.wait_ge(S.hid_f32, h0 + j + 1)
                    sc.activation(hid_hi[:, par, :], h32, ACT.Copy).then_inc(S.hid_hi_ready, 1)

                pump_to(c0 + 1 + AHEAD)
                with act.Fori(0, (MLS - 2) // 2) as i:
                    for s in range(2):
                        c = c0 + 2 + 4 * s + AHEAD
                        split_hi(c, i)
                        split_hi(c + 1, i)
                        hidden(2 * i + s, s)
                        split_hi(c + 2, i)
                        split_hi(c + 3, i)
                nxt[0] = c0 + 4 * MLS - 6 + AHEAD
                pump_to(c0 + 4 * MLS - 5 + AHEAD)
                hidden(MLS - 2, 0)
                pump_to(c0 + 4 * MLS - 3 + AHEAD)
                hidden(MLS - 1, 1)
                pump_to(c0 + 4 * MLS - 1 + AHEAD)

            def head_norm(name, t, pieces, w):
                for b in range(pieces):
                    act.wait_ge(S.acc_read, 4 * RD["fq2" if name == "q2" else name] + b + 1 + (2 if name == "q2" else 0))
                    sc.activation(buf[4][:, half(b)], t[:, half(b)], ACT.Square).then_inc(S.head_sq, 1)

            def head_root(name, w):
                act.wait_ge(S.head_ms, HN[name] + 1)
                sc.activation(root_t[0:16, 0:w], ms[0:16, 0:w], ACT.Sqrt).then_inc(S.head_root, 1)

            act.wait_ge(S.params_in, 16)
            sc.activation(ty("cond", n=16), col("cond", n=16), ACT.Silu).then_inc(S.cond_silu, 1)
            act.wait_ge(S.cond_silu, 1)
            sc.activation(cond[:, :, 0:2], ty("cond", n=16).rearrange("p (k c) -> p k c", c=2), ACT.Copy).then_inc(S.cond_hi_ready, 1)
            act.wait_ge(S.lam_abs, 1)
            sc.activation(ty("e", n=NC), ty("negabs", n=NC), ACT.Exp).then_inc(S.lam_exp, 1)
            for b in range(4):
                x_updated("start", b)
                for k in (2 * b, 2 * b + 1):
                    sc.activation(u_hi[:, k, 0:T], x[:, k, :], ACT.Identity, scale=col("ffn1_0", k))\
                      .then_inc(S.operand_hi, 1)
                square(0, x_t, b)
                pump_to(b)
            root(0)
            pump_to(AHEAD - 1)
            swiglu("ffn0")

            gain_operand("mix_0", "ffn0")
            pump_to(AT["rec"] + 7 + 3)
            xc = ck(buf[0])
            for b in range(4):
                act.wait_ge(S.acc_read, 4 * RD["rec"] + b + 1)
                for k in (2 * b, 2 * b + 1):
                    sc.activation(xc[:, k, :], pad[:, k, 0:T], ACT.Identity, bias=col("cb", k), scale=col("cw0", k))\
                      .then_inc(S.conv_first, 1)
            pump_to(AT["gate"] + 7)
            for b in range(4):
                act.wait_ge(S.conv_tap, NC * (CONV - 2) + 2 * b + 2)
                sc.activation(u_hi[:, 2 * b:2 * b + 2, T:2 * T], xc[:, 2 * b:2 * b + 2, :], ACT.Copy)\
                  .then_inc(S.xc_hi, 1)
            pump_to(AT["i"] + 1)
            for b in range(4):
                act.wait_ge(S.acc_read, 4 * RD["gate"] + b + 1)
                sc.activation(buf[1][:, half(b)], buf[1][:, half(b)], ACT.Gelu_apprx_tanh).then_inc(S.gelu_done, 1)
            r, ig, tn = ck(buf[2]), ck(buf[3]), ck(buf[4])
            for g, (dst, bias, name) in enumerate(((r, "br", "r"), (ig, "bi", "i"))):
                for k in range(NC):
                    act.wait_ge(S.acc_ready, 4 * ACC[name] + k // 2 + 1)
                    sc.activation(dst[:, k, :], bank2(4 * g + k // 2)[:, k % 2, :], ACT.Sigmoid, bias=col(bias, k))\
                      .then_inc(S.gates_read, 1)
            pump_to(AT["wout"] + 3)
            act.wait_ge(S.lam_ready, 2)
            act.wait_ge(S.ms_psum, NRM["ffn0"] + 1)
            act.wait_ge(S.gates_read, NC)
            for k in range(NC):
                sc.activation(tn[:, k, :], r[:, k, :], ACT.Tanh, scale=ty("sp8", k)).then_inc(S.lru_tanh, 1)
            act.wait_ge(S.lru_tanh, NC)
            for k in range(NC):
                sc.activation(r[:, k, :], r[:, k, :], ACT.Exp, scale=ty("nsp8", k)).then_inc(S.lru_decay, 1)
            for b in range(4):
                act.wait_ge(S.lru_m2, b + 1)
                sc.activation(buf[4][:, half(b)], buf[4][:, half(b)], ACT.Sqrt).then_inc(S.lru_sqrt, 1)
            buffer_operand(buf[1], S.lru_y)
            pump_to(AT["ffn1"] + AHEAD - 1)
            gain_operand("ffn2_0", "wout")
            swiglu("ffn1")

            gain_operand("kv", "ffn1")
            pump_to(AT["v"] + 4)
            act.wait_ge(S.ms_psum, NRM["ffn1"] + 1)
            head_norm("k", buf[1], 4, T)
            head_root("k", T)
            pump_to(AT["ffn2"] + AHEAD - 1)
            act.wait_ge(S.acc_ready, 4 * ACC["v"] + 4)
            gain_operand("ffn1_1", "ffn1", norm=False)
            act.wait_ge(S.ctx_in, 16)
            act.wait_ge(S.head_sum, HN["k"] + 1)
            for b in range(4):
                square(NRM["ctx"], buf[3], b)
            root(NRM["ctx"])
            for b in range(4):
                act.wait_ge(S.ctx_full, b + 1)
                sc.activation(u_hi[:, 2 * b:2 * b + 2, T:2 * T], ck(buf[3])[:, 2 * b:2 * b + 2, :], ACT.Copy)\
                  .then_inc(S.ctx_hi, 1)
            swiglu("ffn2")

            gain_operand("mix_1", "ffn2")
            pump_to(AT["q"] + 7 + 3)
            act.wait_ge(S.ms_psum, NRM["ffn2"] + 1)
            head_norm("q", buf[0], 4, T)
            head_root("q", T)
            pump_to(AT["wo"] + 4)
            zs = [buf[3], buf[4]]
            sp_t = buf5
            n_att = 4 * STICK

            def decay_terms(g):
                act.wait_ge(S.z_masked, g + 1)
                if g:
                    act.wait_ge(S.cum_ready, g)
                sc.activation(sp_t[:, 0:n_att], zs[g % 2][:, 0:n_att], ACT.Abs).then_inc(S.z_abs, 1)
                act.wait_ge(S.z_abs, g + 1)
                sc.activation(sp_t[:, 0:n_att], sp_t[:, 0:n_att], ACT.Exp, scale=-1.0).then_inc(S.e_ready, 1)
                act.wait_ge(S.e_ready, g + 1)
                sc.activation(sp_t[:, 0:n_att], sp_t[:, 0:n_att], ACT.Ln, bias=1.0).then_inc(S.l_ready, 1)

            sc.preload_act_table_set("natural_log_exp_and_others")
            decay_terms(0)
            for g in range(4):
                if g < 3:
                    decay_terms(g + 1)
                act.wait_ge(S.w_arg, g + 1)
                sc.activation(zs[g % 2][:, 0:n_att], zs[g % 2][:, 0:n_att], ACT.Exp).then_inc(S.w_ready, 1)
                act.wait_ge(S.o_ready, g + 1)
                sc.activation(u_hi[:, 2 * g:2 * g + 2, 0:T], bank2(4), ACT.Copy).then_inc(S.operand_hi, 2)
            pump_to(AT["ffn3"] + AHEAD - 1)
            gain_operand("ffn2_1", "wo")
            swiglu("ffn3")

            norm_only("ffn3")
            pump_to(AT["fq2"] + 3)
            buffer_operand(buf[3], S.full_ready, 0)
            pump_to(AT["k2"] + 2)
            act.wait_ge(S.ms_psum, NRM["ffn3"] + 1)
            head_norm("q2", buf[0][:, 1024:2048], 2, T)
            pump_to(AT["v2"] + 3)
            head_root("q2", T)
            act.wait_ge(S.head_sum, HN["q2"] + 1)
            head_norm("k2", buf[1], 4, 512)
            head_root("k2", 512)
            pump_to(AT["four"] + 1)
            for g in range(4):
                act.wait_ge(S.dft1, g + 1)
                if g >= 2:
                    act.wait_ge(S.dft2, g - 1)
                elif g == 0:
                    act.wait_ge(S.head_sum, HN["k2"] + 1)
                sc.activation(buf[4][:, 1024 + (g % 2) * 512:1536 + (g % 2) * 512], psum[:, 4 + g % 2, :], ACT.Copy)\
                  .then_inc(S.dft1_out, 1)
                act.wait_ge(S.dft2, g + 1)
                if g >= 2:
                    act.wait_ge(S.dft3, g - 1)
                sc.activation(hid_hi[:, g % 2, 0:T], psum[:, 6, 0:T], ACT.Copy).then_inc(S.mixed_hi, 1)
                act.wait_ge(S.dft3, g + 1)
                sc.activation(u_hi[:, g, 0:T], psum[:, 7, 0:T], ACT.Copy).then_inc(S.operand_hi, 1)
            pump_to(AT["woe"] + 4)
            pt = [buf[0][:, 0:1024], buf5[:, 1024:2048]]

            def na_exp(n):
                act.wait_ge(S.na_max, n + 1)
                e = buf5[:, (n % 2) * 512:(n % 2) * 512 + 512]
                sc.activation(e, e, ACT.Exp, bias=ty("na", 4 * (n % 2) + 1), accum_out=ty("na", 4 * (n % 2) + 2))\
                  .then_inc(S.na_e, 1)

            def na_turn(n):
                h, qt = n // 2, n % 2
                act.wait_ge(S.na_t, n + 1)
                if h >= 2:
                    act.wait_ge(S.na_o, h - 1)
                dst = pt[h % 2].rearrange("p (k q) -> p k q", k=4)[:, :, qt * P:(qt + 1) * P]
                sc.activation(dst, psum[:, 2 + qt, :].rearrange("p (k q) -> p k q", k=4), ACT.Copy)\
                  .then_inc(S.na_tout, 1)

            def na_hi(m):
                act.wait_ge(S.na_o, 2 * m + 2)
                sc.activation(u_hi[:, 4 + m, 0:T], psum[:, 4 + m % 2, 0:T], ACT.Copy).then_inc(S.operand_hi, 1)

            na_exp(0)
            for n in range(16):
                if n < 15:
                    na_exp(n + 1)
                na_turn(n)
                if n % 4 == 1 and n > 4:
                    na_hi(n // 4 - 1)
            na_hi(3)
            pump_to(AT["mlp0"] + AHEAD - 1)
            norm_only("woe")
            buffer_operand(buf[3], S.full_ready, 4)
            sqrelu("mlp0")

            norm_only("mlp0")
            for g in range(4):
                act.wait_ge(S.pooled, g + 1)
                sc.activation(u_hi[:, 2 * g:2 * g + 2, 0:T],
                              buf[g][:, 1088:1600].rearrange("p (k t) -> p k t", k=2), ACT.Copy)\
                  .then_inc(S.operand_hi, 2)
            pump_to(AT["mlp1"] + AHEAD - 1)
            norm_only("pool")
            buffer_operand(buf[3], S.full_ready, 8)
            sqrelu("mlp1")
            for b in range(4):
                act.wait_ge(S.acc_read, 4 * RD["mlp1"] + b + 1)
                act.dma_start(out[:, half(b)], x_t[:, half(b)]).then_inc(S.out_done, 16)

        @block.vector
        def _(dve):
            ve = nc.vector
            nxt = [0]
            chain = [0]

            def link(ins):
                chain[0] += 1
                ins.then_inc(S.dve_chain, 1)
                dve.wait_ge(S.dve_chain, chain[0])

            def split_lo(c, i=0):
                dve.wait_ge(S.hi_ready, RING * i + c + 1)
                u = slice((c % RING) * UNIT, (c % RING + 1) * UNIT)
                ve.tensor_tensor(w_lo[:, u], raw[:, u], w_hi[:, u].bitcast(F32), ALU.subtract).then_inc(S.lo_ready, 1)

            def pump_to(last):
                while nxt[0] <= min(last, UNITS - 1):
                    split_lo(nxt[0])
                    nxt[0] += 1

            def acc_ready(name, b):
                dve.wait_ge(S.acc_ready, 4 * ACC[name] + b + 1)

            def inverse_root(m, r, y):
                link(ve.reciprocal(y, r))
                link(ve.scalar_tensor_tensor(r, y, -0.5, m, ALU.mult, ALU.mult))
                link(ve.tensor_tensor(r, r, y, ALU.mult))
                return ve.scalar_tensor_tensor(y, r, 1.5, y, ALU.add, ALU.mult)

            def rms(name):
                n = NRM[name]
                dve.wait_ge(S.ms_psum, n + 1)
                ve.tensor_scalar(ms[:, 0:T], psum[:, 7, 0:T], 1.0 / D, EPS, ALU.mult, ALU.add).then_inc(S.ms_ready, 1)
                dve.wait_ge(S.root_ready, n + 1)
                link(inverse_root(ms[:, 0:T], root_t[:, 0:T], rstd[:, :]))

            def update_x(name, coef=None):
                for b in range(4):
                    acc_ready(name, b)
                    if coef is None or isinstance(coef, float):
                        ins = ve.scalar_tensor_tensor(x_t[:, half(b)], psum[:, b, :], coef or 1.0, x_t[:, half(b)],
                                                      ALU.mult, ALU.add)
                    else:
                        for k in (2 * b, 2 * b + 1):
                            ins = ve.scalar_tensor_tensor(x[:, k, :], bank2(b)[:, k % 2, :], coef(k), x[:, k, :],
                                                          ALU.mult, ALU.add)
                    ins.then_inc(S.acc_read, 1)

            def gain_operand_lo(op, gain, first=0):
                for k in range(first, NC):
                    dve.wait_ge(S.operand_hi, NC * OPS[op] + k + 1)
                    ve.scalar_tensor_tensor(u_lo[:, k, 0:T], x[:, k, :], col(gain, k), u_hif[:, k, 0:T],
                                            ALU.mult, ALU.subtract).then_inc(S.operand_ready, 1)

            def update_and_operand(name, op, gain, coef):
                for b in range(5):
                    if b < 4:
                        acc_ready(name, b)
                        ve.scalar_tensor_tensor(x_t[:, half(b)], psum[:, b, :], coef, x_t[:, half(b)],
                                                ALU.mult, ALU.add).then_inc(S.acc_read, 1)
                    if b:
                        for k in (2 * b - 2, 2 * b - 1):
                            dve.wait_ge(S.operand_hi, NC * OPS[op] + k + 1)
                            ve.scalar_tensor_tensor(u_lo[:, k, 0:T], x[:, k, :], col(gain, k), u_hif[:, k, 0:T],
                                                    ALU.mult, ALU.subtract).then_inc(S.operand_ready, 1)

            def buffer_operand_lo(op, src):
                for b in range(4):
                    dve.wait_ge(S.operand_hi, NC * OPS[op] + 2 * b + 2)
                    ve.tensor_tensor(u_lo[:, 2 * b:2 * b + 2, 0:T], ck(src)[:, 2 * b:2 * b + 2, :],
                                     u_hif[:, 2 * b:2 * b + 2, 0:T], ALU.subtract).then_inc(S.operand_ready, 2)

            def full_norm(src, dst, gain, shift, done):
                for b in range(4):
                    link(ve.tensor_tensor(ck(dst)[:, 2 * b:2 * b + 2, :], src[:, 2 * b:2 * b + 2, :],
                                          over2(rstd[:, :]), ALU.mult))
                    for k in (2 * b, 2 * b + 1):
                        ins = ve.tensor_scalar(ck(dst)[:, k, :], ck(dst)[:, k, :], gain(k), shift(k),
                                               ALU.mult, ALU.add)
                    ins.then_inc(done, 1)

            def swiglu(name):
                c0, h0, g0 = AT[name], STEPS[name], MODG * int(name[3])
                l, j0 = int(name[3]) // 2, 4 * MODG * (int(name[3]) % 2)
                assert nxt[0] == c0 + AHEAD, (name, nxt[0], c0)

                def hidden(j, par, c, i=0, n_units=4):
                    dve.wait_ge(S.up_ready, h0 + j + 1)
                    ve.tensor_tensor(t2.rearrange("p (k t) -> p k t", k=2), bank2(4 + par), over2(rstd[:, :]),
                                     ALU.mult).then_inc(S.up_scaled, 1)
                    split_lo(c, i)
                    dve.wait_ge(S.gated, h0 + j + 1)
                    ve.tensor_tensor(h32[:, 0:T], sil, t2[:, T:2 * T], ALU.mult).then_inc(S.hid_f32, 1)
                    if n_units > 1:
                        split_lo(c + 1, i)
                    dve.wait_ge(S.hid_hi_ready, h0 + j + 1)
                    ve.tensor_tensor(hid_lo[:, par, 0:T], h32[:, 0:T], hid_hif[:, par, 0:T], ALU.subtract)\
                      .then_inc(S.hid_ready, 1)
                    for n in range(2, n_units):
                        split_lo(c + n, i)

                for n in range(5):
                    split_lo(c0 + n + AHEAD)
                with dve.Fori(0, (FFS - 2) // 4) as i:
                    for s in range(4):
                        hidden(4 * i + s, s % 2, c0 + 5 + 4 * s + AHEAD, 2 * i)
                        if s == 2:
                            modulation(l, j0 + 4 * i, g0 + i)
                hidden(FFS - 2, 0, c0 + FFU - 5 + AHEAD)
                hidden(FFS - 1, 1, c0 + FFU - 1 + AHEAD, n_units=1)
                modulation(l, j0 + 4 * MODG - 4, g0 + MODG - 1)
                nxt[0] = c0 + FFU + AHEAD

            def modulation(l, j, g):
                dve.wait_ge(S.mod_turned, g + 1)
                where = bass.ds(j, 4) if not isinstance(j, int) else slice(j, j + 4)
                ve.tensor_reduce(mod[:, l, where, :], psum[:, 7, 0:16].rearrange("p (m t c) -> p m c t", m=4, t=2),
                                 AX_X, ALU.add).then_inc(S.mod_read, 1)

            def modulation_bias(l):
                dve.wait_ge(S.mod_read, 2 * MODG * (l + 1))
                bias = prm[:, COL["bmod"] + 48 * l:COL["bmod"] + 48 * (l + 1)].unsqueeze(2).broadcast_to([P, 48, 2])
                link(ve.tensor_tensor(mod[:, l, :, :], mod[:, l, :, :], bias, ALU.add))

            def part(l, n, k=None, c=0):
                if k is None:
                    return mod[:, l, NC * n:NC * (n + 1), c]
                return mod[:, l, NC * n + k, c:c + 1]

            def scale_gain(dst, l, n, gain, c=0):
                link(ve.scalar_tensor_tensor(ty(dst, n=NC), part(l, n, c=c), 1.0, col(gain, n=NC), ALU.add, ALU.mult))

            def sqrelu(name):
                c0, h0 = AT[name], STEPS[name]
                assert nxt[0] == c0 + AHEAD

                def hidden(j, par, c, i=0):
                    dve.wait_ge(S.up_ready, h0 + j + 1)
                    ve.tensor_scalar(t2, psum[:, 4 + par, :], 0.0, None, ALU.max).then_inc(S.up_scaled, 1)
                    dve.wait_ge(S.up_scaled, h0 + j + 1)
                    ve.tensor_tensor(h32, t2, t2, ALU.mult).then_inc(S.hid_f32, 1)
                    split(c, i)
                    split(c + 1, i)
                    dve.wait_ge(S.hid_hi_ready, h0 + j + 1)
                    ve.tensor_tensor(hid_lo[:, par, :], h32, hid_hif[:, par, :], ALU.subtract).then_inc(S.hid_ready, 1)
                    split(c + 2, i)
                    split(c + 3, i)

                last = min(c0 + 4 * MLS + AHEAD, UNITS)

                def split(c, i):
                    if not isinstance(i, int) or c < last:
                        split_lo(c, i)

                pump_to(c0 + 1 + AHEAD)
                with dve.Fori(0, (MLS - 2) // 2) as i:
                    for s in range(2):
                        hidden(2 * i + s, s, c0 + 2 + 4 * s + AHEAD, i)
                hidden(MLS - 2, 0, c0 + 4 * MLS - 6 + AHEAD)
                hidden(MLS - 1, 1, c0 + 4 * MLS - 2 + AHEAD)
                nxt[0] = last

            def head_norm(name, t, chunks, w, gain, b0):
                n = HN[name]
                dve.wait_ge(S.head_sum, n + 1)
                ve.tensor_scalar(ms[0:16, 0:w], psum[0:16, HEAD_BANK[name], 0:w], 1.0 / HD, EPS, ALU.mult, ALU.add)\
                  .then_inc(S.head_ms, 1)
                dve.wait_ge(S.head_root, n + 1)
                inverse_root(ms[0:16, 0:w], root_t[0:16, 0:w], head_rs[0:16, 0:w]).then_inc(S.head_rs, 1)
                for b in range(chunks * w // 512):
                    dve.wait_ge(S.head_bc, HNP[name] + b + 1)
                    ve.scalar_tensor_tensor(t[:, half(b)], t[:, half(b)], col(gain), psum[:, b0 + b, :],
                                            ALU.mult, ALU.mult).then_inc(S.normed, 1)

            dve.wait_ge(S.cond_hi_ready, 1)
            ve.tensor_tensor(cond[:, :, 2:4], ty("cond", n=16).rearrange("p (k c) -> p k c", c=2), condf[:, :, 0:2],
                             ALU.subtract)\
              .then_inc(S.cond_ready, 1)
            link(ve.tensor_scalar(ty("relu", n=NC), col("lam", n=NC), -1.0, 0.0, ALU.mult, ALU.max))
            link(ve.tensor_scalar(ty("q", n=NC), col("lam", n=NC), 0.0, None, ALU.max))
            link(ve.tensor_tensor(ty("negabs", n=NC), ty("relu", n=NC), ty("q", n=NC), ALU.add))
            ve.tensor_scalar(ty("negabs", n=NC), ty("negabs", n=NC), -1.0, None, ALU.mult).then_inc(S.lam_abs, 1)

            pump_to(0)
            gain_operand_lo("ffn0", "ffn1_0")
            pump_to(3)
            rms("start")
            pump_to(AHEAD - 1)
            dve.wait_ge(S.lam_exp, 1)
            e, den, q, q2, poly = (ty(n, n=NC) for n in ("e", "den", "q", "q2", "poly"))
            link(ve.tensor_scalar(den, e, 2.0, None, ALU.add))
            link(ve.reciprocal(den, den))
            link(ve.tensor_tensor(q, e, den, ALU.mult))
            link(ve.tensor_tensor(q2, q, q, ALU.mult))
            link(ve.tensor_scalar(poly, q2, 1.0 / 15, None, ALU.mult))
            for m in (13, 11, 9, 7, 5, 3):
                link(ve.scalar_tensor_tensor(poly, poly, 1.0 / m, q2, ALU.add, ALU.mult))
            link(ve.scalar_tensor_tensor(poly, poly, 1.0, q, ALU.add, ALU.mult))
            link(ve.scalar_tensor_tensor(poly, poly, 2.0, ty("relu", n=NC), ALU.mult, ALU.add))
            ve.tensor_scalar(ty("sp8", n=NC), poly, 8.0, None, ALU.mult).then_inc(S.lam_ready, 1)
            ve.tensor_scalar(ty("nsp8", n=NC), poly, -8.0, None, ALU.mult).then_inc(S.lam_ready, 1)
            swiglu("ffn0")

            update_and_operand("ffn0", "mix0", "mix_0", 0.5)
            link(ve.memset(pad[:, :, 0:CONV - 1], 0.0))
            rms("ffn0")
            pump_to(AT["rec"] + 7 + 3)
            for b in range(4):
                acc_ready("rec", b)
                ve.tensor_tensor(pad[:, 2 * b:2 * b + 2, CONV - 1:], bank2(b), over2(rstd[:, :]), ALU.mult)\
                  .then_inc(S.acc_read, 1)
            pump_to(AT["gate"] + 4)
            xc = ck(buf[0])
            for tap in range(1, CONV):
                for k in range(NC):
                    if tap == 1:
                        dve.wait_ge(S.conv_first, k + 1)
                    else:
                        dve.wait_ge(S.conv_tap, NC * (tap - 2) + k + 1)
                    ve.scalar_tensor_tensor(xc[:, k, :], pad[:, k, tap:tap + T], col(f"cw{tap}", k), xc[:, k, :],
                                            ALU.mult, ALU.add).then_inc(S.conv_tap, 1)
                if tap == 1:
                    pump_to(AT["gate"] + 7)
            for b in range(4):
                dve.wait_ge(S.xc_hi, b + 1)
                ve.tensor_tensor(u_lo[:, 2 * b:2 * b + 2, T:2 * T], xc[:, 2 * b:2 * b + 2, :],
                                 u_hif[:, 2 * b:2 * b + 2, T:2 * T], ALU.subtract).then_inc(S.xc_lo, 1)
            pump_to(AT["i"] + 1)
            for b in range(4):
                acc_ready("gate", b)
                ve.tensor_tensor(ck(buf[1])[:, 2 * b:2 * b + 2, :], bank2(4 + b), over2(rstd[:, :]), ALU.mult)\
                  .then_inc(S.acc_read, 1)
            pump_to(AT["wout"] + 3)
            for b in range(4):
                dve.wait_ge(S.gates_read, NC + 2 * b + 2)
                ve.tensor_tensor(buf[3][:, half(b)], buf[3][:, half(b)], buf[0][:, half(b)], ALU.mult)\
                  .then_inc(S.mixed_in, 1)
            for b in range(4):
                dve.wait_ge(S.lru_decay, 2 * b + 2)
                dve.wait_ge(S.mixed_in, b + 1)
                link(ve.tensor_tensor(buf[0][:, half(b)], buf[2][:, half(b)], buf[2][:, half(b)], ALU.mult))
                ve.scalar_tensor_tensor(buf[4][:, half(b)], buf[0][:, half(b)], 1.0, buf[4][:, half(b)],
                                        ALU.add, ALU.mult).then_inc(S.lru_m2, 1)
            a, hs = ck(buf[2]), ck(buf[0])
            for b in range(4):
                dve.wait_ge(S.lru_sqrt, b + 1)
                link(ve.tensor_tensor(buf[3][:, half(b)], buf[3][:, half(b)], buf[4][:, half(b)], ALU.mult))
                for k in (2 * b, 2 * b + 1):
                    ins = ve.tensor_tensor_scan(hs[:, k, :], a[:, k, :], ck(buf[3])[:, k, :], 0.0, ALU.mult, ALU.add)
                link(ins)
                dve.wait_ge(S.gelu_done, b + 1)
                ve.tensor_tensor(buf[1][:, half(b)], buf[0][:, half(b)], buf[1][:, half(b)], ALU.mult)\
                  .then_inc(S.lru_y, 1)
            buffer_operand_lo("y", buf[1])
            pump_to(AT["ffn1"] + AHEAD - 1)
            update_and_operand("wout", "ffn1", "ffn2_0", 1.0)
            rms("wout")
            swiglu("ffn1")

            update_and_operand("ffn1", "kv", "kv", 0.5)
            modulation_bias(0)
            rms("ffn1")
            for dst, n, gain, c in (("G1", 1, "n1_0", 0), ("Gc", 1, "n1_0", 1), ("G2", 4, "n2_0", 0)):
                scale_gain(dst, 0, n, gain, c)
            pump_to(AT["v"] + 4)
            for b in range(4):
                acc_ready("k", b)
                ve.tensor_tensor(ck(buf[1])[:, 2 * b:2 * b + 2, :], bank2(b), over2(rstd[:, :]), ALU.mult)\
                  .then_inc(S.acc_read, 1)
            head_norm("k", buf[1], NC, T, "kg", 0)
            pump_to(AT["ffn2"] + AHEAD - 1)
            for b in range(4):
                acc_ready("v", b)
                ve.tensor_tensor(ck(buf[0])[:, 2 * b:2 * b + 2, :], bank2(4 + b), over2(rstd[:, :]), ALU.mult)\
                  .then_inc(S.acc_read, 1)
            gain_operand_lo("ffn2", "ffn1_1")
            for b in range(4):
                dve.wait_ge(S.v_turned, b + 1)
                ve.tensor_copy(buf[2][:, half(b)], psum[:, b, :]).then_inc(S.v_out, 1)
            dve.wait_ge(S.ms_psum, NRM["ctx"] + 1)
            ve.tensor_scalar(ms[:, 0:T], psum[:, 7, 0:T], 1.0 / D, EPS, ALU.mult, ALU.add).then_inc(S.ms_ready, 1)
            dve.wait_ge(S.root_ready, NRM["ctx"] + 1)
            rc = ms[:, T:2 * T]
            link(inverse_root(ms[:, 0:T], root_t[:, 0:T], rc))
            for b in range(4):
                link(ve.tensor_tensor(ck(buf[3])[:, 2 * b:2 * b + 2, :], ck(buf[3])[:, 2 * b:2 * b + 2, :],
                                      over2(rc), ALU.mult))
                for k in (2 * b, 2 * b + 1):
                    ins = ve.tensor_scalar(ck(buf[3])[:, k, :], ck(buf[3])[:, k, :], ty("Gc", k), part(0, 0, k, 1),
                                           ALU.mult, ALU.add)
                ins.then_inc(S.ctx_full, 1)
            for b in range(4):
                dve.wait_ge(S.ctx_hi, b + 1)
                ve.tensor_tensor(u_lo[:, 2 * b:2 * b + 2, T:2 * T], ck(buf[3])[:, 2 * b:2 * b + 2, :],
                                 u_hif[:, 2 * b:2 * b + 2, T:2 * T], ALU.subtract).then_inc(S.ctx_lo, 1)
            swiglu("ffn2")

            update_and_operand("ffn2", "mix1", "mix_1", 0.5)
            rms("ffn2")
            pump_to(AT["q"] + 7 + 3)
            for b in range(4):
                acc_ready("q", b)
                ve.tensor_tensor(ck(buf[0])[:, 2 * b:2 * b + 2, :], bank2(b), over2(rstd[:, :]), ALU.mult)\
                  .then_inc(S.acc_read, 1)
            head_norm("q", buf[0], NC, T, "qg", 4)
            pump_to(AT["wo"] + 4)
            n_att = 4 * STICK
            zs, sp_t = [buf[3], buf[4]], buf5

            def heads4(t):
                return t[:, 0:n_att].rearrange("p (h c) -> p h c", h=4)

            def mask_scores(g):
                dve.wait_ge(S.z_ready, g + 1)
                if g >= 2:
                    dve.wait_ge(S.o_ready, g - 1)
                if g == 0:
                    dve.wait_ge(S.consts_in, 16)
                ve.scalar_tensor_tensor(heads4(zs[g % 2]), psum[:, 0:4, 0:STICK], HD ** -0.5,
                                        stick.unsqueeze(1).broadcast_to([P, 4, STICK]), ALU.mult, ALU.add)\
                  .then_inc(S.z_masked, 1)

            def softplus(g):
                dve.wait_ge(S.l_ready, g + 1)
                ve.scalar_tensor_tensor(sp_t[:, 0:n_att], zs[g % 2][:, 0:n_att], 0.0, sp_t[:, 0:n_att],
                                        ALU.max, ALU.add).then_inc(S.sp_ready, 1)

            mask_scores(0)
            softplus(0)
            for g in range(4):
                if g < 3:
                    mask_scores(g + 1)
                dve.wait_ge(S.cum_ready, g + 1)
                ve.tensor_tensor(heads4(zs[g % 2]), heads4(zs[g % 2]), psum[:, 4:8, 0:STICK], ALU.subtract)\
                  .then_inc(S.w_arg, 1)
                if g < 3:
                    softplus(g + 1)
                dve.wait_ge(S.operand_hi, NC * OPS["att"] + 2 * g + 2)
                ve.tensor_tensor(u_lo[:, 2 * g:2 * g + 2, 0:T], bank2(4), u_hif[:, 2 * g:2 * g + 2, 0:T],
                                 ALU.subtract).then_inc(S.operand_ready, 2)
            pump_to(AT["ffn3"] + AHEAD - 1)
            update_and_operand("wo", "ffn3", "ffn2_1", 1.0)
            rms("wo")
            swiglu("ffn3")

            update_x("ffn3", 0.5)
            modulation_bias(1)
            rms("ffn3")
            full_norm(x, buf[3], lambda k: ty("G1", k), lambda k: part(0, 0, k), S.full_ready)
            buffer_operand_lo("even", buf[3])
            for dst, n, gain in (("H1", 1, "n1_1"), ("H2", 4, "n2_1")):
                scale_gain(dst, 1, n, gain)
            link(ve.tensor_tensor(ty("Gp", n=NC), part(1, 2), col("pscale", n=NC), ALU.mult))
            pump_to(AT["fq2"] + 7 + 3)
            for b in range(4):
                acc_ready("fq2", b)
                ve.tensor_copy(buf[0][:, half(b)], psum[:, b, :]).then_inc(S.acc_read, 1)
            pump_to(AT["k2"] + 3 + 2)
            for b in range(4):
                acc_ready("k2", b)
                ve.tensor_copy(buf[1][:, half(b)], psum[:, 4 + b, :]).then_inc(S.acc_read, 1)
            pump_to(AT["v2"] + 3)
            q2 = buf[0][:, 1024:2048]
            head_norm("q2", q2, 4, T, "qg2", 6)
            for b in range(4):
                acc_ready("v2", b)
                ve.tensor_copy(buf[2][:, half(b)], psum[:, b, :]).then_inc(S.acc_read, 1)
            for qt in range(2):
                dve.wait_ge(S.f_turned, qt + 1)
                if qt == 0:
                    dve.wait_ge(S.head_sum, HN["k2"] + 1)
                ve.tensor_copy(buf[4][:, half(qt)], psum[:, 6 + qt, :]).then_inc(S.f_out, 1)
            for kt in range(4):
                dve.wait_ge(S.v2_turned, kt + 1)
                ve.tensor_copy(buf[3][:, half(kt)], psum[:, kt, :]).then_inc(S.v2_out, 1)
            head_norm("k2", buf[1], 4, 512, "kg2", 0)
            pump_to(AT["four"] + 1)
            for g in range(4):
                dve.wait_ge(S.mixed_hi, g + 1)
                ve.tensor_tensor(hid_lo[:, g % 2, 0:T], psum[:, 6, 0:T], hid_hif[:, g % 2, 0:T], ALU.subtract)\
                  .then_inc(S.mixed_lo, 1)
                dve.wait_ge(S.operand_hi, NC * OPS["mixed"] + g + 1)
                ve.tensor_tensor(u_lo[:, g, 0:T], psum[:, 7, 0:T], u_hif[:, g, 0:T], ALU.subtract)\
                  .then_inc(S.operand_ready, 1)
            pump_to(AT["woe"] + 4)
            tabs = [buf[2], buf[4]]
            for n in range(2):
                dve.wait_ge(tab_in[n], 16)
                w = tabs[n][:, 0:TABW].rearrange("p (e c) -> p e c", c=HD)
                ve.tensor_tensor(w, w, colmask.unsqueeze(1).broadcast_to([P, TABW // HD, HD]), ALU.add)\
                  .then_inc(S.tab_ready, 1)

            def na_scores(n):
                h, qt = n // 2, n % 2
                s = buf5[:, (n % 2) * 512:(n % 2) * 512 + 512]
                dve.wait_ge(S.na_z, n + 1)
                if n >= 2:
                    dve.wait_ge(S.na_t, n - 1)
                if h % 4 == 0:
                    dve.wait_ge(S.tab_ready, h // 4 + 1)
                at = (h % 4) * 6 * HD + (2 - 2 * qt) * HD
                ve.scalar_tensor_tensor(s[:, 0:T], psum[:, n % 2, 0:T], HD ** -0.5, tabs[h // 4][:, at:at + T],
                                        ALU.mult, ALU.add)
                ve.tensor_scalar(s[:, T:2 * T], psum[:, n % 2, T:2 * T], HD ** -0.5, None, ALU.mult)\
                  .then_inc(S.na_s, 1)
                dve.wait_ge(S.na_s, n + 1)
                a = 4 * (n % 2)
                link(ve.tensor_reduce(ty("na", a), s, AX_X, ALU.max))
                ve.tensor_scalar(ty("na", a + 1), ty("na", a), -1.0, None, ALU.mult).then_inc(S.na_max, 1)

            def na_normalise(n):
                s = buf5[:, (n % 2) * 512:(n % 2) * 512 + 512]
                a = 4 * (n % 2)
                dve.wait_ge(S.na_e, n + 1)
                link(ve.reciprocal(ty("na", a + 3), ty("na", a + 2)))
                ve.tensor_scalar(s, s, ty("na", a + 3), None, ALU.mult).then_inc(S.na_p, 1)

            def na_lo(m):
                dve.wait_ge(S.operand_hi, NC * OPS["mixed"] + 4 + m + 1)
                ve.tensor_tensor(u_lo[:, 4 + m, 0:T], psum[:, 4 + m % 2, 0:T], u_hif[:, 4 + m, 0:T],
                                 ALU.subtract).then_inc(S.operand_ready, 1)

            na_scores(0)
            for n in range(16):
                if n < 15:
                    na_scores(n + 1)
                na_normalise(n)
                if n % 4 == 1 and n > 4:
                    na_lo(n // 4 - 1)
            na_lo(3)
            pump_to(AT["mlp0"] + AHEAD - 1)
            update_x("woe", lambda k: part(0, 2, k))
            rms("woe")
            full_norm(x, buf[3], lambda k: ty("G2", k), lambda k: part(0, 3, k), S.full_ready)
            buffer_operand_lo("mlp0", buf[3])
            sqrelu("mlp0")

            update_x("mlp0", lambda k: part(0, 5, k))
            rms("mlp0")
            W = T + 16

            def pieces(g):
                return [buf[g][:, n * 2 * W:(n + 1) * 2 * W].rearrange("p (k t) -> p k t", k=2) for n in range(3)]

            for g in range(4):
                u = pieces(g)[0]
                ve.memset(u[:, :, 0:8], 0.0)
                ve.memset(u[:, :, T + 8:W], 0.0)
                link(ve.tensor_tensor(u[:, :, 8:8 + T], x[:, 2 * g:2 * g + 2, :], over2(rstd[:, :]), ALU.mult))
                for k in range(2):
                    ins = ve.tensor_scalar(u[:, k, 8:8 + T], u[:, k, 8:8 + T], ty("H1", 2 * g + k),
                                           part(1, 0, 2 * g + k), ALU.mult, ALU.add)
                link(ins)
            dve.wait_ge(S.cnt_in, 16)
            for g in range(4):
                u, a, b = pieces(g)
                src, dst, other = u, a, b
                size = W
                for level in range(g + 1):
                    step = 1 << level
                    size -= step
                    link(ve.tensor_tensor(dst[:, :, 0:size], src[:, :, 0:size], src[:, :, step:step + size], ALU.add))
                    src, dst, other = dst, other, dst
                at = 8 - (1 << g)
                link(ve.tensor_tensor(src[:, :, at:at + T], src[:, :, at:at + T], over2(inv_cnt[:, g, :]), ALU.mult))
                pooled = buf[g][:, 1088:1600].rearrange("p (k t) -> p k t", k=2)
                if g % 2:
                    link(ve.tensor_copy(a[:, :, at:at + T], src[:, :, at:at + T]))
                    src = a
                ve.tensor_tensor(pooled, src[:, :, at:at + T], u[:, :, 8:8 + T], ALU.subtract).then_inc(S.pooled, 1)
            for g in range(4):
                dve.wait_ge(S.operand_hi, NC * OPS["pooled"] + 2 * g + 2)
                ve.tensor_tensor(u_lo[:, 2 * g:2 * g + 2, 0:T],
                                 buf[g][:, 1088:1600].rearrange("p (k t) -> p k t", k=2),
                                 u_hif[:, 2 * g:2 * g + 2, 0:T], ALU.subtract).then_inc(S.operand_ready, 2)
            pump_to(AT["mlp1"] + AHEAD - 1)
            update_x("pool", lambda k: ty("Gp", k))
            rms("pool")
            full_norm(x, buf[3], lambda k: ty("H2", k), lambda k: part(1, 3, k), S.full_ready)
            buffer_operand_lo("mlp1", buf[3])
            sqrelu("mlp1")
            update_x("mlp1", lambda k: part(1, 5, k))

        @block.tensor
        def _(pe):
            te = nc.tensor

            def unit_ready(c, i=0):
                pe.wait_ge(S.lo_ready, RING * i + c + 1)

            def operand(name, k):
                pe.wait_ge(S.operand_ready, NC * OPS[name] + k + 1)

            def read(name, b):
                pe.wait_ge(S.acc_read, 4 * RD[name] + b + 1)

            def norm_sum(name):
                n = NRM[name]
                pe.wait_ge(S.ssq_ready, n + 1)
                if n == 0:
                    pe.wait_ge(S.consts_in, 16)
                te.matmul(psum[:, 7, 0:T], ones, buf[4][:, 0:T], start=True, stop=True).then_inc(S.ms_psum, 1)

            def product(dst, c, at, hi, lo, first, last):
                w = slice((c % RING) * UNIT + at, (c % RING) * UNIT + at + P)
                ins = te.matmul(dst, w_hi[:, w], hi, start=first, stop=False, skip_group_check=True)
                if begun[0] != c:
                    ins.then_inc(S.unit_used, 1)
                    begun[0] = c
                te.matmul(dst, w_hi[:, w], lo, start=False, stop=False, skip_group_check=True)
                return te.matmul(dst, w_lo[:, w], hi, start=False, stop=last, skip_group_check=True)

            begun = [-1]

            def all_k(c, i, dst, op=None):
                unit_ready(c, i)
                for k in range(NC):
                    if op:
                        operand(op, k)
                    ins = product(dst, c, k * P, u_hi[:, k, 0:T], u_lo[:, k, 0:T], k == 0, k == NC - 1)
                return ins

            def one_k(c, i, hi, lo, b0, first, last, free=None):
                unit_ready(c, i)
                for n in range(NC):
                    if free and n % 2 == 0:
                        free(n // 2)
                    ins = product(bank2(b0 + n // 2)[:, n % 2, :], c, n * P, hi, lo, first and n % 2 == 0, last)
                    if last and n % 2:
                        ins.then_inc(S.acc_ready, 1)

            def project(name, op, b0, free=None, hooks={}):
                for k in range(NC):
                    operand(op, k)
                    one_k(AT[name] + k, 0, u_hi[:, k, 0:T], u_lo[:, k, 0:T], b0, k == 0, k == NC - 1,
                          free if k == 0 else None)
                    if k in hooks:
                        hooks[k]()

            def block_diagonal(name, b0, t0, ready):
                for n in range(4):
                    c = AT[name] + n // 2
                    if n % 2 == 0:
                        unit_ready(c)
                    ready(n)
                    for kk in range(2):
                        for mo in range(2):
                            k = 2 * n + kk
                            ins = product(bank2(b0 + n)[:, mo, :], c, ((n % 2) * 4 + kk * 2 + mo) * P,
                                          u_hi[:, k, t0:t0 + T], u_lo[:, k, t0:t0 + T], kk == 0 and mo == 0, kk == 1)
                    ins.then_inc(S.acc_ready, 1)

            def modulate(c, i, q, g):
                unit_ready(c, i)
                if q == 0 and not (isinstance(g, int) and g == 0):
                    pe.wait_ge(S.mod_copied, g)
                if q == 0 and not isinstance(g, int):
                    pe.wait_ge(S.mod_read, g - 1)
                for kk in range(2):
                    at = slice((c % RING) * UNIT + kk * 512, (c % RING) * UNIT + (kk + 1) * 512)
                    k = 2 * q + kk
                    ins = te.matmul(psum[0:4, 6, :], cond[:, k, :], w_hi[:, at], start=k == 0, stop=False,
                                    skip_group_check=True)
                    if kk == 0:
                        ins.then_inc(S.unit_used, 1)
                    ins = te.matmul(psum[0:4, 6, :], cond[:, k, :], w_lo[:, at], start=False, stop=k == NC - 1,
                                    skip_group_check=True)
                if q == 3:
                    ins.then_inc(S.mod_rows, 1)

            def turn_modulation():
                for m in range(4):
                    ins = te.transpose(psum[:, 7, 4 * m:4 * m + 4], mod_rows[:, m * P:(m + 1) * P], ident[0:4, 0:4])
                ins.then_inc(S.mod_turned, 1)

            def up(c, i, j, par, h0, op=None):
                if not isinstance(j, int) or j >= 2:
                    pe.wait_ge(S.up_scaled, h0 + j - 1)
                all_k(c, i, bank2(4 + par)[:, 0, :], op)
                all_k(c + 1, i, bank2(4 + par)[:, 1, :]).then_inc(S.up_ready, 1)

            def swiglu(name, norm):
                c0, h0, g0 = AT[name], STEPS[name], MODG * int(name[3])

                def down(j, par, c, i=0, first=False, last=False):
                    pe.wait_ge(S.hid_ready, h0 + j + 1)
                    one_k(c, i, hid_hi[:, par, 0:T], hid_lo[:, par, 0:T], 0, first, last)

                if g0 == 0:
                    pe.wait_ge(S.cond_ready, 1)
                for q in range(2):
                    modulate(c0 + q, 0, q, g0)
                up(c0 + 2, 0, 0, 0, h0, name)
                norm_sum(norm)
                modulate(c0 + 4, 0, 2, g0)
                up(c0 + 5, 0, 1, 1, h0)
                modulate(c0 + 7, 0, 3, g0)
                pe.wait_ge(S.ms_ready, NRM[norm] + 1)
                down(0, 0, c0 + 8, first=True)
                with pe.Fori(0, (FFS - 2) // 4) as i:
                    for s in range(4):
                        j, c = 2 + 4 * i + s, c0 + 9 + 4 * s
                        up(c, 2 * i, j, s % 2, h0)
                        modulate(c + 2, 2 * i, s, g0 + i + 1)
                        if s == 0:
                            turn_modulation()
                        down(j - 1, 1 - s % 2, c + 3, 2 * i)
                pe.wait_ge(S.mod_copied, g0 + MODG)
                pe.wait_ge(S.mod_read, g0 + MODG - 1)
                turn_modulation()
                down(FFS - 1, 1, c0 + FFU - 1, last=True)

            def sqrelu(name):
                c0, h0 = AT[name], STEPS[name]

                def down(j, par, c, i=0, first=False, last=False):
                    pe.wait_ge(S.hid_ready, h0 + j + 1)
                    for n in range(2):
                        one_k(c + n, i, hid_hi[:, par, n * T:(n + 1) * T], hid_lo[:, par, n * T:(n + 1) * T], 0,
                              first and n == 0, last and n == 1)

                up(c0, 0, 0, 0, h0, name)
                up(c0 + 2, 0, 1, 1, h0)
                down(0, 0, c0 + 4, first=True)
                with pe.Fori(0, (MLS - 2) // 2) as i:
                    for s in range(2):
                        j, c = 2 + 2 * i + s, c0 + 6 + 4 * s
                        up(c, i, j, s, h0)
                        down(j - 1, 1 - s, c + 2, i)
                down(MLS - 1, 1, c0 + 4 * MLS - 2, last=True)

            def head_sums(name, sq, chunks, w, free):
                b = HEAD_BANK[name]
                free()
                for m in range(chunks):
                    pe.wait_ge(S.head_sq, HNP[name] + (m * w) // 512 + 1)
                    ins = te.matmul(psum[0:16, b, 0:w], headsum[:, m, :], sq[:, m * w:(m + 1) * w],
                                    start=m == 0, stop=m == chunks - 1)
                ins.then_inc(S.head_sum, 1)

            def head_spread(name, chunks, w, b0, free=lambda b: None):
                pe.wait_ge(S.head_rs, HN[name] + 1)
                per = 512 // w
                for m in range(chunks):
                    b = b0 + m // per
                    if m % per == 0:
                        free(m // per)
                    ins = te.matmul(psum[:, b, (m % per) * w:(m % per + 1) * w], headbc[:, m, :], head_rs[0:16, 0:w],
                                    start=m % per == 0, stop=True, skip_group_check=True)
                    if m % per == per - 1:
                        ins.then_inc(S.head_bc, 1)

            swiglu("ffn0", "start")

            project("rec", "mix0", 0, lambda b: read("ffn0", b), hooks={1: lambda: norm_sum("ffn0")})
            pe.wait_ge(S.ms_ready, NRM["ffn0"] + 1)
            project("gate", "mix0", 4)

            def xc_ready(n):
                pe.wait_ge(S.xc_lo, n + 1)

            def r_free(n):
                xc_ready(n)
                read("rec", n)

            def i_free(n):
                xc_ready(n)
                read("gate", n)

            block_diagonal("r", 0, T, r_free)
            block_diagonal("i", 4, T, i_free)
            pe.wait_ge(S.gates_read, NC)
            project("wout", "y", 0)
            swiglu("ffn1", "wout")

            def kv_norm():
                pe.wait_ge(S.mod_read, 2 * MODG)
                norm_sum("ffn1")

            def k_sums():
                head_sums("k", buf[4], NC, T, lambda: read("k", 0))

            def k_spread():
                head_spread("k", NC, T, 0, lambda b: read("k", b))

            project("k", "kv", 0, lambda b: read("ffn1", b), hooks={0: kv_norm})
            pe.wait_ge(S.ms_ready, NRM["ffn1"] + 1)
            project("v", "kv", 4, hooks={1: k_sums, 3: k_spread})
            v_raw = ck(buf[0])
            for b in range(4):
                pe.wait_ge(S.normed, HNP["k"] + b + 1)
                for m in range(4):
                    chunk = 4 * (b % 2) + m
                    read("v", chunk // 2)
                    ins = te.transpose(psum[:, b, m * P:(m + 1) * P], v_raw[:, chunk, (b // 2) * P:(b // 2 + 1) * P],
                                       ident)
                ins.then_inc(S.v_turned, 1)
            swiglu("ffn2", "ctx")

            project("q", "mix1", 0, lambda b: read("ffn2", b), hooks={1: lambda: norm_sum("ffn2")})
            qt_, kt_ = ck(buf[0]), ck(buf[1])
            pe.wait_ge(S.ms_ready, NRM["ffn2"] + 1)
            head_sums("q", buf[4], NC, T, lambda: None)
            head_spread("q", NC, T, 4)
            zs, sp_t = [buf[3], buf[4]], buf5

            def scores(g):
                pe.wait_ge(S.normed, HNP["q"] + g + 1)
                if g == 0:
                    read("q", 3)
                else:
                    pe.wait_ge(S.z_masked, g)
                for h in range(4):
                    m, p0 = (4 * g + h) // 2, HD * (h % 2)
                    te.matmul(psum[:, h, 0:T], kt_[p0:p0 + HD, m, 0:P], qt_[p0:p0 + HD, m, :], start=True, stop=True)
                    ins = te.matmul(psum[:, h, T:STICK], kt_[p0:p0 + HD, m, P:T], qt_[p0:p0 + HD, m, P:T],
                                    start=True, stop=True)
                ins.then_inc(S.z_ready, 1)

            def sums_after(g):
                pe.wait_ge(S.sp_ready, g + 1)
                if g == 0:
                    pe.wait_ge(S.normed, HNP["q"] + 4)
                else:
                    operand("att", 2 * g - 1)
                for h in range(4):
                    s = sp_t[:, h * STICK:(h + 1) * STICK]
                    te.matmul(psum[:, 4 + h, 0:T], tri, s[:, 0:T], start=True, stop=False, skip_group_check=True)
                    te.matmul(psum[:, 4 + h, P:T], ones, s[:, T:STICK], start=False, stop=False, skip_group_check=True)
                    ins = te.matmul(psum[:, 4 + h, T:STICK], tri, s[:, T:STICK], start=False, stop=True,
                                    skip_group_check=True)
                ins.then_inc(S.cum_ready, 1)

            def attend(g):
                pe.wait_ge(S.w_ready, g + 1)
                for h in range(4):
                    p0 = HD * (h % 2)
                    f = (4 * g + h) * HD
                    w = zs[g % 2][:, h * STICK:(h + 1) * STICK]
                    dst = bank2(4)[p0:p0 + HD, h // 2, :]
                    te.matmul(dst, buf[2][:, f:f + HD], w[:, 0:T], start=True, stop=False, skip_group_check=True)
                    ins = te.matmul(dst[:, P:T], buf[2][:, D + f:D + f + HD], w[:, T:STICK], start=False, stop=True,
                                    skip_group_check=True)
                ins.then_inc(S.o_ready, 1)

            scores(0)
            for g in range(4):
                if g < 3:
                    scores(g + 1)
                sums_after(g)
                attend(g)
            pe.wait_ge(S.z_masked, 4)
            project("wo", "att", 0)
            swiglu("ffn3", "wo")

            pe.wait_ge(S.mod_read, 4 * MODG)
            norm_sum("ffn3")
            project("fq2", "even", 0, lambda b: read("ffn3", b))

            def project_both(name, b0, free):
                for k in range(NC):
                    c = AT[name] + k // 2
                    if k % 2 == 0:
                        unit_ready(c)
                    for n in range(4):
                        if k == 0:
                            free(n)
                        ins = product(psum[:, b0 + n, :], c, ((k % 2) * 4 + n) * P, u_hi[:, k, :], u_lo[:, k, :],
                                      k == 0, k == NC - 1)
                        if k == NC - 1:
                            ins.then_inc(S.acc_ready, 1)

            pe.wait_ge(S.ctx_lo, 4)
            project_both("k2", 4, lambda n: None)
            project_both("v2", 0, lambda n: read("fq2", n))
            head_sums("q2", buf[4], 4, T, lambda: read("k2", 3))
            head_spread("q2", 4, T, 6)
            head_sums("k2", buf[4], 4, 512, lambda: None)
            pe.wait_ge(S.normed, HNP["q2"] + 2)
            f_raw = buf[0][:, 0:1024].rearrange("p (k t) -> p k t", k=4)
            for qt in range(2):
                for g in range(4):
                    ins = te.transpose(psum[:, 6 + qt, g * P:(g + 1) * P], f_raw[:, g, qt * P:(qt + 1) * P], ident)
                ins.then_inc(S.f_turned, 1)
            v2_raw = ck(buf[2], 4)
            read("v2", 3)
            for kt in range(4):
                for m in range(4):
                    ins = te.transpose(psum[:, kt, m * P:(m + 1) * P], v2_raw[:, m, kt * P:(kt + 1) * P], ident)
                ins.then_inc(S.v2_turned, 1)
            head_spread("k2", 4, 512, 0, lambda b: pe.wait_ge(S.v2_out, b + 1))

            dftc = buf5[:, 1024:1024 + 2 * P]

            def token_dft(g):
                if g == 0:
                    pe.wait_ge(S.late_in, 16)
                    pe.wait_ge(S.f_out, 2)
                if g < 2:
                    pe.wait_ge(S.head_ms, HN["q2"] + 1 + g)
                else:
                    pe.wait_ge(S.dft1_out, g - 1)
                for qt in range(2):
                    at = qt * 512
                    ins = te.matmul(psum[:, 4 + g % 2, :], buf[4][:, at + g * P:at + (g + 1) * P],
                                    buf5[:, at:at + 512], start=qt == 0, stop=qt == 1)
                ins.then_inc(S.dft1, 1)

            token_dft(0)
            for g in range(4):
                if g < 3:
                    token_dft(g + 1)
                ab = buf[4][:, 1024 + (g % 2) * 512:1536 + (g % 2) * 512]
                pe.wait_ge(S.dft1_out, g + 1)
                if g:
                    pe.wait_ge(S.mixed_lo, g)
                te.matmul(psum[:, 6, 0:T], dftc[:, 0:P], ab[:, 0:T], start=True, stop=False)
                te.matmul(psum[:, 6, 0:T], dftc[:, P:2 * P], ab[:, T:2 * T], start=False, stop=True)\
                  .then_inc(S.dft2, 1)
                pe.wait_ge(S.mixed_lo, g + 1)
                if g:
                    operand("mixed", g - 1)
                c = AT["four"] + g // 2
                unit_ready(c)
                product(psum[:, 7, 0:T], c, (g % 2) * P, hid_hi[:, g % 2, 0:T], hid_lo[:, g % 2, 0:T], True, True)\
                  .then_inc(S.dft3, 1)

            q2, k2 = ck(buf[0])[:, 4:8, :], ck(buf[1], 4)
            vt = ck(buf[3], 4)
            pt = [buf[0][:, 0:1024], buf5[:, 1024:2048]]

            def na_scores(n):
                h, qt = n // 2, n % 2
                m, p0 = h // 2, HD * (h % 2)
                if n == 0:
                    pe.wait_ge(S.normed, HNP["k2"] + 4)
                if n >= 2:
                    pe.wait_ge(S.na_s, n - 1)
                te.matmul(psum[:, n % 2, :], q2[p0:p0 + HD, m, qt * P:(qt + 1) * P], k2[p0:p0 + HD, m, :],
                          start=True, stop=True).then_inc(S.na_z, 1)

            def na_turn(n):
                qt = n % 2
                p = buf5[:, (n % 2) * 512:(n % 2) * 512 + 512]
                pe.wait_ge(S.na_p, n + 1)
                if n >= 2:
                    pe.wait_ge(S.na_tout, n - 1)
                for kt in range(4):
                    ins = te.transpose(psum[:, 2 + qt, kt * P:(kt + 1) * P], p[:, kt * P:(kt + 1) * P], ident)
                ins.then_inc(S.na_t, 1)

            def na_attend(h):
                m, p0 = h // 2, HD * (h % 2)
                pe.wait_ge(S.na_tout, 2 * h + 2)
                if m >= 2:
                    operand("mixed", 4 + m - 2)
                w = pt[h % 2].rearrange("p (k q) -> p k q", k=4)
                for kt in range(4):
                    ins = te.matmul(psum[p0:p0 + HD, 4 + m % 2, 0:T], vt[:, kt, h * HD:(h + 1) * HD], w[:, kt, :],
                                    start=kt == 0, stop=kt == 3)
                ins.then_inc(S.na_o, 1)

            na_scores(0)
            for n in range(16):
                if n < 15:
                    na_scores(n + 1)
                na_turn(n)
                if n % 2 and n > 1:
                    na_attend(n // 2 - 1)
            na_attend(7)
            project("woe", "mixed", 0)
            norm_sum("woe")
            sqrelu("mlp0")

            norm_sum("mlp0")
            block_diagonal("pool", 0, 0, lambda n: operand("pooled", 2 * n + 1))
            norm_sum("pool")
            sqrelu("mlp1")


def weight_stream(w):
    units = np.zeros((UNITS, P, UNIT), np.float32)

    def k_in(m):
        return m.reshape(-1, P, D)

    def n_out(m):
        return m.reshape(NC, P, -1, P).transpose(2, 1, 0, 3).reshape(-1, P, D)

    def blocks(m):
        return m.reshape(2, 2, 2, P, 2, P).transpose(0, 3, 1, 2, 4, 5).reshape(2, P, UNIT)

    def halves(m):
        return m.reshape(4, 2, P, 512).transpose(0, 2, 1, 3).reshape(4, P, UNIT)

    mods = w["w_mod_2"].reshape(2, 4, 2, P, 12, 512).transpose(0, 4, 1, 3, 2, 5).reshape(-1, P, UNIT)

    for f, (w13, w2) in enumerate([("ffn1_w13", "ffn1_w2"), ("ffn2_w13", "ffn2_w2")] * 2):
        l, c0 = f // 2, AT[f"ffn{f}"]
        u13, u2 = n_out(w[w13][l]), k_in(w[w2][l])
        m0 = 4 * MODG * f
        units[c0:c0 + 2] = mods[m0:m0 + 2]
        for j in range(FFS):
            c = c0 + 2 + 4 * j - (j > 0)
            units[c], units[c + 1], units[c + 2] = u13[j], u13[FFS + j], mods[m0 + 2 + j]
            if j:
                units[c + 3] = u2[j - 1]
        units[c0 + FFU - 1] = u2[FFS - 1]
    for m, name in enumerate(["mlp0", "mlp1"]):
        c0 = AT[name]
        u1, u2 = n_out(w["w_mlp1_2"][m]), k_in(w["w_mlp2_2"][m])
        for j in range(MLS):
            c = c0 + 4 * j - 2 * (j > 0)
            units[c:c + 2] = u1[2 * j:2 * j + 2]
            if j:
                units[c + 2:c + 4] = u2[2 * j - 2:2 * j]
        units[c0 + 4 * MLS - 2:c0 + 4 * MLS] = u2[2 * MLS - 2:]
    a_in, w_even, w_kv = w["a_w_in"][0], w["w_in_even_2"][0], w["w_kv"]
    whole = {"gate": a_in[:, :D], "rec": a_in[:, D:], "wout": w["a_w_out"][0], "k": w_kv[:, :D], "v": w_kv[:, D:],
             "q": w["b_w_q"][0], "wo": w["b_w_o"][0], "fq2": w_even[:, :D], "woe": w["w_out_even_2"][0]}
    for name, m in whole.items():
        units[AT[name]:AT[name] + 8] = k_in(m)
    for name, m in {"r": w["a_w_r"][0], "i": w["a_w_i"][0], "pool": w["w_pool_2"][0]}.items():
        units[AT[name]:AT[name] + 2] = blocks(m)
    units[AT["k2"]:AT["k2"] + 4] = halves(w_even[:, D:D + 512])
    units[AT["v2"]:AT["v2"] + 4] = halves(w_even[:, D + 512:])
    four = w["w_four_2"][0].transpose(1, 0, 2).reshape(P, 4 * P)
    units[AT["four"], :, :2 * P], units[AT["four"] + 1, :, :2 * P] = four[:, :2 * P], four[:, 2 * P:]
    return units.reshape(UNITS // 2, 2, P, UNIT).transpose(0, 2, 1, 3).reshape(UNITS // 2, P, 2 * UNIT)


def by_feature(v):
    return v.reshape(NC, P).T


def small_params(w):
    prm = np.zeros((P, NSMALL), np.float32)
    vectors = [w["ffn1_norm"][0], w["ffn1_norm"][1], w["mix_norm"][0], w["mix_norm"][1], w["kv_norm"],
               w["ffn2_norm"][0], w["ffn2_norm"][1], w["norm1_g_2"][0], w["norm1_g_2"][1], w["norm2_g_2"][0],
               w["norm2_g_2"][1], *w["a_conv_w"][0], w["a_conv_b"][0], w["a_b_r"][0], w["a_b_i"][0],
               w["a_lambda"][0], w["pool_scale_2"][0]]
    for n, v in enumerate(vectors):
        prm[:, NC * n:NC * (n + 1)] = by_feature(v)
    prm[:, COL["cond"]:COL["cond"] + 2 * NC:2] = by_feature(w["c_2"][0])
    prm[:, COL["cond"] + 1:COL["cond"] + 2 * NC:2] = by_feature(w["c_ctx_2"])
    prm[:, COL["bmod"]:COL["bmod"] + 96] = w["b_mod_2"].reshape(96, P).T
    for name, v in (("kg", w["k_norm"]), ("qg", w["q_norm"][0]), ("kg2", w["k_norm_g_2"][0]),
                    ("qg2", w["q_norm_g_2"][0])):
        prm[:HD, COL[name]] = v
        prm[HD:, COL[name]] = v
    return prm


def shape_constants():
    p = np.arange(P)
    cst = np.zeros((P, NCONST), np.float32)
    cst[:, CC["ident"]:CC["ident"] + P] = np.eye(P)
    cst[:, CC["ones"]:CC["ones"] + P] = 1.0
    cst[:, CC["tri"]:CC["tri"] + P] = p[:, None] >= p[None, :]
    for m in range(NC):
        for half in range(2):
            h = 2 * m + half
            cst[HD * half:HD * (half + 1), CC["headsum"] + 16 * m + h] = 1.0
            cst[h, CC["headbc"] + P * m + HD * half:CC["headbc"] + P * m + HD * (half + 1)] = 1.0
    diagonal = np.where(p[:, None] < p[None, :], 0.0, BIG)
    cst[:, CC["stick"]:CC["stick"] + P] = diagonal
    cst[:, CC["stick"] + T:CC["stick"] + STICK] = diagonal
    c = np.arange(64)
    start = np.clip(c - 8, 0, 48)
    window = (c[None, :] >= start[:, None]) & (c[None, :] < start[:, None] + 16)
    cst[:, CC["colmask"]:CC["colmask"] + HD] = np.tile(np.where(window, 0.0, BIG), (2, 1))
    late = np.zeros((P, NLATE), np.float32)
    t = np.arange(T)
    a = 2 * np.pi * (np.outer(t, t) % T) / T
    dft = np.concatenate([np.cos(a), np.sin(a)], 1)
    late[:, :1024] = dft.reshape(2, P, 512).transpose(1, 0, 2).reshape(P, 1024)
    a = 2 * np.pi * (np.outer(p, p) % P) / P
    late[:, 1024:] = np.concatenate([np.cos(a), -np.sin(a)], 1) / np.sqrt(T * P)
    cnt = np.zeros((4, T), np.float32)
    for g in range(4):
        w = 2 << g
        cnt[g] = 1.0 / (np.clip(t + w - w // 2, 0, T) - np.clip(t - w // 2, 0, T))
    return cst, late, np.broadcast_to(cnt.reshape(1, 4 * T), (P, 4 * T)).copy()


def bias_windows(rpb):
    wide = np.zeros((8, 15, 3 * 64), np.float32)
    wide[:, :, 64:64 + 31] = rpb
    tab = np.zeros((2, P, 4, 6, 64), np.float32)
    for c in range(64):
        at = 64 + 15 - c
        rows = wide[:, :, at:at + 64]
        tab[:, c] = rows[:, 5:11].reshape(2, 4, 6, 64)
        tab[:, 64 + c] = rows[:, 4:10].reshape(2, 4, 6, 64)
    return tab.reshape(2, P, TABW)


def kernel(**inputs):
    import concourse.bacc as bacc
    from concourse.bass_utils import run_bass_kernel_spmd

    w = {k: np.asarray(v) for k, v in inputs.items()}

    def tokens(v):
        return np.ascontiguousarray(v.reshape(T, NC, P).transpose(2, 1, 0).reshape(P, NC * T))

    cst, late, cnt = shape_constants()
    arrays = {"stream": weight_stream(w), "x_in": tokens(w["x"][0]), "ctx_in": tokens(w["ctx_2"][0]),
              "small": small_params(w), "consts": cst, "late": late, "cnt": cnt, "tab": bias_windows(w["rpb_2"][0])}
    nc = bacc.Bacc("TRN2", target_bir_lowering=False, num_devices=1)
    args = {}
    for name, a in arrays.items():
        arrays[name] = np.ascontiguousarray(a)
        args[name] = nc.dram_tensor(name, a.shape, mybir.dt.from_np(a.dtype), kind="ExternalInput").ap()
    out = nc.dram_tensor("out", (P, NC * T), F32, kind="ExternalOutput").ap()
    build(nc, out=out, **args)
    got = run_bass_kernel_spmd(nc, [arrays], core_ids=[0]).results[0]["out"]
    return got.reshape(P, NC, T).transpose(2, 1, 0).reshape(1, T, D)
```

```python
from contextlib import ExitStack

import numpy as np
from concourse import bass, mybir

F32 = mybir.dt.float32
F32R = mybir.dt.float32r
ALU = mybir.AluOpType
ACT = mybir.ActivationFunctionType
AX_X = mybir.AxisListType.X

P = 128
D = 1024
T = 256
NC = D // P
FF = 2816
FFS = FF // P
MLP = 4096
MLS = MLP // P // 2
CONV = 4
HD = 64
EPS = 1e-6
NMOD = 6
BIG = -1e30

UNIT = 1024
RING = 8
AHEAD = 6

FFU = 4 * FFS + 2
MODG = 6
PHASES = [("ffn0", FFU), ("rec", 8), ("gate", 8), ("r", 2), ("i", 2), ("wout", 8), ("ffn1", FFU),
          ("k", 8), ("v", 8), ("ffn2", FFU), ("q", 8), ("wo", 8), ("ffn3", FFU),
          ("fq2", 8), ("k2", 4), ("v2", 4), ("four", 2), ("woe", 8), ("mlp0", 4 * MLS),
          ("pool", 2), ("mlp1", 4 * MLS)]
AT = {}
_n = 0
for _name, _count in PHASES:
    AT[_name] = _n
    _n += _count
UNITS = _n
assert UNITS % RING == 0

SMALL = ["ffn1_0", "ffn1_1", "mix_0", "mix_1", "kv", "ffn2_0", "ffn2_1", "n1_0", "n1_1", "n2_0", "n2_1",
         "cw0", "cw1", "cw2", "cw3", "cb", "br", "bi", "lam", "pscale"]
COL = {n: NC * i for i, n in enumerate(SMALL)}
COL["cond"] = NC * len(SMALL)
COL["bmod"] = COL["cond"] + 2 * NC
COL["kg"] = COL["bmod"] + 2 * NMOD * NC
COL["qg"], COL["qg2"], COL["kg2"] = COL["kg"] + 1, COL["kg"] + 2, COL["kg"] + 3
NSMALL = COL["kg"] + 4

CC = {"ident": 0, "ones": 128, "tri": 256, "headsum": 384, "stick": 512, "colmask": 896, "headbc": 960}
NCONST = CC["headbc"] + NC * P
NLATE = 1024 + 2 * P
STICK = T + P
TABW = 4 * 6 * HD

TY = {n: NC * i for i, n in enumerate(["cond", "cond2", "negabs", "e", "den", "q", "q2", "poly", "sp8", "nsp8", "relu",
                                       "G1", "Gc", "G2", "H1", "H2", "Gp", "na", "na_rest"])}

OPS = {n: i for i, n in enumerate("ffn0 mix0 y ffn1 kv ffn2 mix1 att ffn3 even mixed mlp0 pooled mlp1".split())}
ACC = {n: i for i, n in enumerate("ffn0 rec gate r i wout ffn1 k v ffn2 q wo ffn3 fq2 k2 v2 woe mlp0 pool mlp1".split())}
RD = {n: i for i, n in enumerate("ffn0 rec gate wout ffn1 k v ffn2 q wo ffn3 fq2 k2 v2 woe mlp0 pool mlp1".split())}
NORMS = "start ffn0 wout ffn1 ctx ffn2 wo ffn3 woe mlp0 pool".split()
NRM = {n: i for i, n in enumerate(NORMS)}
HN = {"k": 0, "q": 1, "q2": 2, "k2": 3}
HNP = {"k": 0, "q": 4, "q2": 8, "k2": 10}
HEAD_BANK = {"k": 0, "q": 4, "q2": 4, "k2": 5}
STEPS = {"ffn0": 0, "ffn1": FFS, "ffn2": 2 * FFS, "ffn3": 3 * FFS, "mlp0": 4 * FFS, "mlp1": 4 * FFS + MLS}


class Signals:

    def __init__(self, sem):
        self.params_in = sem("params_in")
        self.consts_in = sem("consts_in")
        self.mixer_consts_in = sem("mixer_consts_in")
        self.x_in = sem("x_in")
        self.ctx_in = sem("ctx_in")
        self.late_in = sem("late_in")
        self.cnt_in = sem("cnt_in")
        self.out_done = sem("out_done")
        self.hi_ready = sem("hi_ready")
        self.lo_ready = sem("lo_ready")
        self.unit_used = sem("unit_used")
        self.operand_hi = sem("operand_hi")
        self.operand_ready = sem("operand_ready")
        self.acc_ready = sem("acc_ready")
        self.acc_read = sem("acc_read")
        self.sq_ready = sem("sq_ready")
        self.pool_sum = sem("pool_sum")
        self.ssq_ready = sem("ssq_ready")
        self.ms_psum = sem("ms_psum")
        self.ms_ready = sem("ms_ready")
        self.root_ready = sem("root_ready")
        self.up_ready = sem("up_ready")
        self.up_scaled = sem("up_scaled")
        self.gated = sem("gated")
        self.hid_f32 = sem("hid_f32")
        self.hid_hi_ready = sem("hid_hi_ready")
        self.hid_ready = sem("hid_ready")
        self.cond_silu = sem("cond_silu")
        self.cond_hi_ready = sem("cond_hi_ready")
        self.cond_ready = sem("cond_ready")
        self.mod_rows = sem("mod_rows")
        self.mod_copied = sem("mod_copied")
        self.mod_turned = sem("mod_turned")
        self.mod_read = sem("mod_read")
        self.dve_chain = sem("dve_chain")
        self.lam_abs = sem("lam_abs")
        self.lam_exp = sem("lam_exp")
        self.lam_ready = sem("lam_ready")
        self.conv_first = sem("conv_first")
        self.conv_tap = sem("conv_tap")
        self.xc_hi = sem("xc_hi")
        self.xc_lo = sem("xc_lo")
        self.gelu_done = sem("gelu_done")
        self.gates_read = sem("gates_read")
        self.mixed_in = sem("mixed_in")
        self.lru_tanh = sem("lru_tanh")
        self.lru_decay = sem("lru_decay")
        self.lru_m2 = sem("lru_m2")
        self.lru_sqrt = sem("lru_sqrt")
        self.lru_y = sem("lru_y")
        self.head_sq = sem("head_sq")
        self.head_sum = sem("head_sum")
        self.head_ms = sem("head_ms")
        self.head_root = sem("head_root")
        self.head_rs = sem("head_rs")
        self.head_bc = sem("head_bc")
        self.normed = sem("normed")
        self.v_turned = sem("v_turned")
        self.v_out = sem("v_out")
        self.z_ready = sem("z_ready")
        self.z_masked = sem("z_masked")
        self.z_abs = sem("z_abs")
        self.e_ready = sem("e_ready")
        self.l_ready = sem("l_ready")
        self.sp_ready = sem("sp_ready")
        self.cum_ready = sem("cum_ready")
        self.w_arg = sem("w_arg")
        self.w_ready = sem("w_ready")
        self.o_ready = sem("o_ready")
        self.ctx_full = sem("ctx_full")
        self.ctx_hi = sem("ctx_hi")
        self.ctx_lo = sem("ctx_lo")
        self.full_ready = sem("full_ready")
        self.v2_turned = sem("v2_turned")
        self.v2_out = sem("v2_out")
        self.f_turned = sem("f_turned")
        self.f_out = sem("f_out")
        self.dft1 = sem("dft1")
        self.dft1_out = sem("dft1_out")
        self.dft2 = sem("dft2")
        self.mixed_hi = sem("mixed_hi")
        self.mixed_lo = sem("mixed_lo")
        self.dft3 = sem("dft3")
        self.pooled = sem("pooled")
        self.tab_ready = sem("tab_ready")
        self.na_z = sem("na_z")
        self.na_s = sem("na_s")
        self.na_max = sem("na_max")
        self.na_e = sem("na_e")
        self.na_p = sem("na_p")
        self.na_t = sem("na_t")
        self.na_tout = sem("na_tout")
        self.na_o = sem("na_o")


def build(nc, stream, x_in, ctx_in, small, consts, late, cnt, tab, out):
    with ExitStack() as es:
        def sb(name, cols, dt=F32):
            return es.enter_context(nc.sbuf_tensor(name, [P, cols], dt))

        raw = sb("raw", RING * UNIT)
        w_hi = sb("w_hi", RING * UNIT, F32R)
        w_lo = sb("w_lo", RING * UNIT, F32R)
        x_t = sb("x", NC * T)
        u_hi_t = sb("u_hi", NC * 2 * T, F32R)
        u_lo_t = sb("u_lo", NC * 2 * T, F32R)
        hid_hi_t = sb("hid_hi", 2 * 512, F32R)
        hid_lo_t = sb("hid_lo", 2 * 512, F32R)
        cond_t = sb("cond", 4 * NC, F32R)
        rstd = sb("rstd", T)
        nrm = sb("nrm", 1024)
        prm = sb("prm", NSMALL)
        cst = sb("cst", NCONST)
        mod_t = sb("mod", 2 * NMOD * NC * 2)
        tiny = sb("tiny", NC * len(TY))
        buf = [sb(f"buf{n}", 2048) for n in range(5)]
        buf5 = sb("buf5", NC * (T + CONV - 1))
        psum = es.enter_context(nc.psum_tensor("psum", [P, 8, 512], F32))

        x = x_t[:, :].rearrange("p (k t) -> p k t", k=NC)
        u_hi = u_hi_t[:, :].rearrange("p (k t) -> p k t", k=NC)
        u_lo = u_lo_t[:, :].rearrange("p (k t) -> p k t", k=NC)
        u_hif = u_hi_t[:, :].bitcast(F32).rearrange("p (k t) -> p k t", k=NC)
        hid_hi = hid_hi_t[:, :].rearrange("p (s t) -> p s t", s=2)
        hid_lo = hid_lo_t[:, :].rearrange("p (s t) -> p s t", s=2)
        hid_hif = hid_hi_t[:, :].bitcast(F32).rearrange("p (s t) -> p s t", s=2)
        cond = cond_t[:, :].rearrange("p (k c) -> p k c", c=4)
        condf = cond_t[:, :].bitcast(F32).rearrange("p (k c) -> p k c", c=4)
        mod = mod_t[:, :].rearrange("p (l j c) -> p l j c", l=2, c=2)
        pad = buf5[:, :].rearrange("p (k t) -> p k t", k=NC)
        t2, sil, h32 = buf5[:, 0:512], buf5[:, 512:768], buf5[:, 768:1280]
        mod_rows = buf5[0:4, 1280:1792]
        ms, root_t = nrm[:, 0:512], nrm[:, 512:1024]
        head_rs = buf5[:, 1536:2048]
        n_att = 2 * STICK
        z_slots = [buf[3 + n // 2][:, (n % 2) * n_att:(n % 2 + 1) * n_att] for n in range(4)]
        sp_slots = [buf5[:, n * n_att:(n + 1) * n_att] for n in range(2)]
        na_slots = [buf5[:, 0:512], buf5[:, 512:1024], nrm[:, 0:512], nrm[:, 512:1024]]
        NA_BANKS = [0, 1, 6, 7]
        ident, ones, tri = (cst[:, CC[n]:CC[n] + P] for n in ("ident", "ones", "tri"))
        headsum = cst[:, CC["headsum"]:CC["headsum"] + P].rearrange("p (k h) -> p k h", k=NC)
        headbc = cst[0:16, CC["headbc"]:CC["headbc"] + NC * P].rearrange("p (k n) -> p k n", k=NC)
        stick = cst[:, CC["stick"]:CC["stick"] + STICK]
        colmask = cst[:, CC["colmask"]:CC["colmask"] + HD]
        inv_cnt = cst[:, CC["headbc"]:CC["headbc"] + 4 * T].rearrange("p (g t) -> p g t", g=4)

        def ck(t, k=NC):
            return t[:, :].rearrange("p (k t) -> p k t", k=k)

        def col(name, k=0, n=1):
            return prm[:, COL[name] + k:COL[name] + k + n]

        def ty(name, k=0, n=1):
            return tiny[:, TY[name] + k:TY[name] + k + n]

        def half(b):
            return slice(b * 512, (b + 1) * 512)

        def bank2(b):
            return psum[:, b, :].rearrange("p (k t) -> p k t", k=2)

        def over2(row):
            return row.unsqueeze(1).broadcast_to([P, 2, T])

        def sem(name):
            return es.enter_context(nc.semaphore(name))

        S = Signals(sem)
        raw_landed = [sem(f"raw_landed{n}") for n in range(RING // 2)]
        tab_in = [sem(f"tab_in{n}") for n in range(2)]
        block = es.enter_context(nc.Block())

        @block.sync
        def _(sp):
            sp.dma_start(prm[:, :], small).then_inc(S.params_in, 16)

            def load(pair, src, i=0):
                slot = pair % (RING // 2)
                sp.dma_start(raw[:, 2 * slot * UNIT:2 * (slot + 1) * UNIT], src).then_inc(raw_landed[slot], 16)

            for pair in range(RING // 2):
                load(pair, stream[pair])
                if pair == 0:
                    sp.dma_start(x_t[:, :], x_in).then_inc(S.x_in, 16)
                if pair == 1:
                    sp.dma_start(cst[:, 0:CC["tri"]], consts[:, 0:CC["tri"]]).then_inc(S.consts_in, 16)
            with sp.Fori(1, UNITS // RING) as i:
                for slot in range(RING // 2):
                    sp.wait_ge(S.lo_ready, RING * i + 2 * slot + 2 - RING)
                    load(slot, stream[i * (RING // 2) + slot])
            sp.wait_ge(S.out_done, 4 * 16)

        @block.gpsimd
        def _(pool):
            gp = nc.gpsimd

            def sum_squares(n):
                for b in range(1, 4):
                    pool.wait_ge(S.sq_ready, 4 * n + b + 1)
                    if b > 1:
                        pool.wait_ge(S.pool_sum, 3 * n + b - 1)
                    a = buf[4][:, half(0)]
                    gp.tensor_tensor(a, a, buf[4][:, half(b)], ALU.add).then_inc(S.pool_sum, 1)
                pool.wait_ge(S.pool_sum, 3 * n + 3)
                gp.tensor_tensor(buf[4][:, 0:T], buf[4][:, 0:T], buf[4][:, T:2 * T], ALU.add).then_inc(S.ssq_ready, 1)

            pool.wait_ge(S.hi_ready, 4)
            pool.dma_start(cst[:, CC["tri"]:], consts[:, CC["tri"]:]).then_inc(S.mixer_consts_in, 16)
            for n, name in enumerate(NORMS):
                if name == "ctx":
                    pool.dma_start(buf[3][:, :], ctx_in).then_inc(S.ctx_in, 16)
                if name == "woe":
                    pool.wait_ge(S.acc_ready, 4 * ACC["ffn3"] + 4)
                    pool.dma_start(buf5[:, 0:NLATE], late).then_inc(S.late_in, 16)
                    pool.wait_ge(S.v2_turned, 4)
                    pool.dma_start(buf[2][:, 0:TABW], tab[0]).then_inc(tab_in[0], 16)
                    pool.wait_ge(S.mixed_lo, 4)
                    pool.dma_start(buf[4][:, 0:TABW], tab[1]).then_inc(tab_in[1], 16)
                    pool.wait_ge(S.normed, HNP["k2"] + 4)
                    pool.dma_start(cst[:, CC["headbc"]:CC["headbc"] + 4 * T], cnt).then_inc(S.cnt_in, 16)
                sum_squares(n)

        @block.scalar
        def _(act):
            sc = nc.scalar
            nxt = [0]

            def split_hi(c, i=0):
                slot = c % RING
                act.wait_ge(raw_landed[slot // 2], 16 * (c // RING + 1 + i))
                if c >= RING or not isinstance(i, int):
                    act.wait_ge(S.unit_used, RING * i + c - RING + 2)
                u = slice(slot * UNIT, (slot + 1) * UNIT)
                sc.activation(w_hi[:, u], raw[:, u], ACT.Copy).then_inc(S.hi_ready, 1)

            def pump_to(last):
                while nxt[0] <= min(last, UNITS - 1):
                    split_hi(nxt[0])
                    nxt[0] += 1

            def x_updated(name, b):
                if name == "start":
                    act.wait_ge(S.x_in, 16)
                    act.wait_ge(S.params_in, 16)
                else:
                    act.wait_ge(S.acc_read, 4 * RD[name] + b + 1)

            def square(n, src, b):
                if b == 0 and n:
                    act.wait_ge(S.ms_psum, n)
                sc.activation(buf[4][:, half(b)], src[:, half(b)], ACT.Square).then_inc(S.sq_ready, 1)

            def root(n):
                act.wait_ge(S.ms_ready, n + 1)
                sc.activation(root_t[:, 0:T], ms[:, 0:T], ACT.Sqrt).then_inc(S.root_ready, 1)

            def gain_operand(gain, name, norm=True, early=0):
                for b in range(4):
                    x_updated(name, b)
                    for k in (2 * b, 2 * b + 1):
                        sc.activation(u_hi[:, k, 0:T], x[:, k, :], ACT.Identity, scale=col(gain, k))\
                          .then_inc(S.operand_hi, 1)
                    if norm:
                        square(NRM[name], x_t, b)
                pump_to(early - 1)
                if norm:
                    root(NRM[name])

            def norm_only(name):
                for b in range(4):
                    x_updated(name, b)
                    square(NRM[name], x_t, b)
                root(NRM[name])

            def buffer_operand(src, ready, base=0):
                for b in range(4):
                    act.wait_ge(ready, base + b + 1)
                    sc.activation(u_hi[:, 2 * b:2 * b + 2, 0:T], ck(src)[:, 2 * b:2 * b + 2, :], ACT.Copy)\
                      .then_inc(S.operand_hi, 2)

            def swiglu(name):
                c0, h0, g0 = AT[name], STEPS[name], MODG * int(name[3])

                def copy_rows(g):
                    act.wait_ge(S.mod_rows, g + 1)
                    if not isinstance(g, int) or g:
                        act.wait_ge(S.mod_turned, g)
                    sc.activation(mod_rows, psum[0:4, 6, :], ACT.Copy).then_inc(S.mod_copied, 1)

                def hidden(j, par, c, i=0, n_units=4, rows=None):
                    act.wait_ge(S.up_scaled, h0 + j + 1)
                    sc.activation(sil, t2[:, 0:T], ACT.Silu).then_inc(S.gated, 1)
                    for n in range(min(n_units, 2)):
                        split_hi(c + n, i)
                    act.wait_ge(S.hid_f32, h0 + j + 1)
                    sc.activation(hid_hi[:, par, 0:T], h32[:, 0:T], ACT.Copy).then_inc(S.hid_hi_ready, 1)
                    if rows is not None:
                        copy_rows(rows)
                    for n in range(2, n_units):
                        split_hi(c + n, i)

                pump_to(c0 + 7)
                with act.Fori(0, (FFS - 2) // 4) as i:
                    for s in range(4):
                        hidden(4 * i + s, s % 2, c0 + 8 + 4 * s, 2 * i, rows=g0 + i if s == 1 else None)
                hidden(FFS - 2, 0, c0 + FFU - 2)
                nxt[0] = c0 + FFU + 2
                pump_to(c0 + FFU + 3)
                hidden(FFS - 1, 1, None, n_units=0, rows=g0 + MODG - 1)
                pump_to(c0 + FFU - 1 + AHEAD)

            def sqrelu(name):
                c0, h0 = AT[name], STEPS[name]
                assert nxt[0] == c0 + AHEAD

                def hidden(j, par):
                    act.wait_ge(S.hid_f32, h0 + j + 1)
                    sc.activation(hid_hi[:, par, :], h32, ACT.Copy).then_inc(S.hid_hi_ready, 1)

                pump_to(c0 + 1 + AHEAD)
                with act.Fori(0, (MLS - 2) // 2) as i:
                    for s in range(2):
                        c = c0 + 2 + 4 * s + AHEAD
                        split_hi(c, i)
                        split_hi(c + 1, i)
                        hidden(2 * i + s, s)
                        split_hi(c + 2, i)
                        split_hi(c + 3, i)
                nxt[0] = c0 + 4 * MLS - 6 + AHEAD
                pump_to(c0 + 4 * MLS - 5 + AHEAD)
                hidden(MLS - 2, 0)
                pump_to(c0 + 4 * MLS - 3 + AHEAD)
                hidden(MLS - 1, 1)
                pump_to(c0 + 4 * MLS - 1 + AHEAD)

            def head_norm(name, t, pieces, w):
                for b in range(pieces):
                    act.wait_ge(S.acc_read, 4 * RD["fq2" if name == "q2" else name] + b + 1 + (2 if name == "q2" else 0))
                    sc.activation(buf[4][:, half(b)], t[:, half(b)], ACT.Square).then_inc(S.head_sq, 1)

            def head_root(name, w):
                act.wait_ge(S.head_ms, HN[name] + 1)
                sc.activation(root_t[0:16, 0:w], ms[0:16, 0:w], ACT.Sqrt).then_inc(S.head_root, 1)

            act.wait_ge(S.params_in, 16)
            sc.activation(ty("cond", n=16), col("cond", n=16), ACT.Silu).then_inc(S.cond_silu, 1)
            act.wait_ge(S.cond_silu, 1)
            sc.activation(cond[:, :, 0:2], ty("cond", n=16).rearrange("p (k c) -> p k c", c=2), ACT.Copy).then_inc(S.cond_hi_ready, 1)
            act.wait_ge(S.lam_abs, 1)
            sc.activation(ty("e", n=NC), ty("negabs", n=NC), ACT.Exp).then_inc(S.lam_exp, 1)
            pump_to(1)
            for b in range(4):
                x_updated("start", b)
                for k in (2 * b, 2 * b + 1):
                    sc.activation(u_hi[:, k, 0:T], x[:, k, :], ACT.Identity, scale=col("ffn1_0", k))\
                      .then_inc(S.operand_hi, 1)
                square(0, x_t, b)
                if b == 1:
                    pump_to(3)
            pump_to(AHEAD + 1)
            root(0)
            swiglu("ffn0")

            gain_operand("mix_0", "ffn0")
            pump_to(AT["rec"] + 7 + 3)
            xc = ck(buf[0])
            for b in range(4):
                act.wait_ge(S.acc_read, 4 * RD["rec"] + b + 1)
                for k in (2 * b, 2 * b + 1):
                    sc.activation(xc[:, k, :], pad[:, k, 0:T], ACT.Identity, bias=col("cb", k), scale=col("cw0", k))\
                      .then_inc(S.conv_first, 1)
            pump_to(AT["gate"] + 7)
            for b in range(4):
                act.wait_ge(S.conv_tap, NC * (CONV - 2) + 2 * b + 2)
                sc.activation(u_hi[:, 2 * b:2 * b + 2, T:2 * T], xc[:, 2 * b:2 * b + 2, :], ACT.Copy)\
                  .then_inc(S.xc_hi, 1)
            pump_to(AT["i"] + 1)
            for b in range(4):
                act.wait_ge(S.acc_read, 4 * RD["gate"] + b + 1)
                sc.activation(buf[1][:, half(b)], buf[1][:, half(b)], ACT.Gelu_apprx_tanh).then_inc(S.gelu_done, 1)
            r, ig, tn = ck(buf[2]), ck(buf[3]), ck(buf[4])
            for g, (dst, bias, name) in enumerate(((r, "br", "r"), (ig, "bi", "i"))):
                for k in range(NC):
                    act.wait_ge(S.acc_ready, 4 * ACC[name] + k // 2 + 1)
                    sc.activation(dst[:, k, :], bank2(4 * g + k // 2)[:, k % 2, :], ACT.Sigmoid, bias=col(bias, k))\
                      .then_inc(S.gates_read, 1)
            pump_to(AT["wout"] + 3)
            act.wait_ge(S.lam_ready, 2)
            act.wait_ge(S.ms_psum, NRM["ffn0"] + 1)
            act.wait_ge(S.gates_read, NC)
            for k in range(NC):
                sc.activation(tn[:, k, :], r[:, k, :], ACT.Tanh, scale=ty("sp8", k)).then_inc(S.lru_tanh, 1)
            act.wait_ge(S.lru_tanh, NC)
            for k in range(NC):
                sc.activation(r[:, k, :], r[:, k, :], ACT.Exp, scale=ty("nsp8", k)).then_inc(S.lru_decay, 1)
            for b in range(4):
                act.wait_ge(S.lru_m2, b + 1)
                sc.activation(buf[4][:, half(b)], buf[4][:, half(b)], ACT.Sqrt).then_inc(S.lru_sqrt, 1)
            buffer_operand(buf[1], S.lru_y)
            pump_to(AT["ffn1"] + AHEAD - 1)
            gain_operand("ffn2_0", "wout", early=AT["ffn1"] + 8)
            swiglu("ffn1")

            gain_operand("kv", "ffn1")
            pump_to(AT["v"] + 4)
            act.wait_ge(S.ms_psum, NRM["ffn1"] + 1)
            head_norm("k", buf[1], 4, T)
            head_root("k", T)
            pump_to(AT["ffn2"] + AHEAD - 1)
            act.wait_ge(S.acc_ready, 4 * ACC["v"] + 4)
            gain_operand("ffn1_1", "ffn1", norm=False)
            act.wait_ge(S.ctx_in, 16)
            act.wait_ge(S.head_sum, HN["k"] + 1)
            for b in range(4):
                square(NRM["ctx"], buf[3], b)
            pump_to(AT["ffn2"] + 7)
            act.wait_ge(S.ms_ready, NRM["ctx"] + 1)
            sc.activation(root_t[:, T:2 * T], ms[:, T:2 * T], ACT.Sqrt).then_inc(S.root_ready, 1)
            swiglu("ffn2")

            gain_operand("mix_1", "ffn2")
            pump_to(AT["q"] + 7)
            for b in range(4):
                act.wait_ge(S.ctx_full, b + 1)
                sc.activation(u_hi[:, 2 * b:2 * b + 2, T:2 * T], ck(buf[3])[:, 2 * b:2 * b + 2, :], ACT.Copy)\
                  .then_inc(S.ctx_hi, 1)
            pump_to(AT["q"] + 7 + 3)
            act.wait_ge(S.ms_psum, NRM["ffn2"] + 1)
            head_norm("q", buf[0], 4, T)
            head_root("q", T)
            pump_to(AT["wo"] + 4)

            def decay_terms(g):
                act.wait_ge(S.z_masked, g + 1)
                if g >= 2:
                    act.wait_ge(S.cum_ready, g - 1)
                d = sp_slots[g % 2]
                sc.activation(d, z_slots[g % 4], ACT.Abs).then_inc(S.z_abs, 1)
                act.wait_ge(S.z_abs, g + 1)
                sc.activation(d, d, ACT.Exp, scale=-1.0).then_inc(S.e_ready, 1)
                act.wait_ge(S.e_ready, g + 1)
                sc.activation(d, d, ACT.Ln, bias=1.0).then_inc(S.l_ready, 1)

            sc.preload_act_table_set("natural_log_exp_and_others")
            decay_terms(0)
            for g in range(NC + 1):
                if g:
                    act.wait_ge(S.w_arg, g)
                    z = z_slots[(g - 1) % 4]
                    sc.activation(z, z, ACT.Exp).then_inc(S.w_ready, 1)
                if g + 1 < NC:
                    decay_terms(g + 1)
                if g:
                    act.wait_ge(S.o_ready, g)
                    sc.activation(u_hi[:, g - 1, 0:T], psum[:, 4 + 2 * ((g - 1) % 2), 0:T], ACT.Copy)\
                      .then_inc(S.operand_hi, 1)
            pump_to(AT["ffn3"] + AHEAD - 1)
            gain_operand("ffn2_1", "wo", early=AT["ffn3"] + 8)
            swiglu("ffn3")

            norm_only("ffn3")
            pump_to(AT["fq2"] + 3)
            buffer_operand(buf[3], S.full_ready, 0)
            pump_to(AT["k2"] + 2)
            act.wait_ge(S.ms_psum, NRM["ffn3"] + 1)
            head_norm("q2", buf[0][:, 1024:2048], 2, T)
            pump_to(AT["v2"] + 3)
            head_root("q2", T)
            act.wait_ge(S.head_sum, HN["q2"] + 1)
            head_norm("k2", buf[1], 4, 512)
            head_root("k2", 512)
            pump_to(AT["four"] + 1)
            for g in range(4):
                act.wait_ge(S.dft1, g + 1)
                if g >= 2:
                    act.wait_ge(S.dft2, g - 1)
                elif g == 0:
                    act.wait_ge(S.head_sum, HN["k2"] + 1)
                sc.activation(buf[4][:, 1024 + (g % 2) * 512:1536 + (g % 2) * 512], psum[:, 4 + g % 2, :], ACT.Copy)\
                  .then_inc(S.dft1_out, 1)
                act.wait_ge(S.dft2, g + 1)
                if g >= 2:
                    act.wait_ge(S.dft3, g - 1)
                sc.activation(hid_hi[:, g % 2, 0:T], psum[:, 6, 0:T], ACT.Copy).then_inc(S.mixed_hi, 1)
                act.wait_ge(S.dft3, g + 1)
                sc.activation(u_hi[:, g, 0:T], psum[:, 7, 0:T], ACT.Copy).then_inc(S.operand_hi, 1)
            pump_to(AT["woe"] + 4)
            pt = [buf[0][:, 0:1024], buf5[:, 1024:2048]]

            def na_exp(n):
                act.wait_ge(S.na_max, n + 1)
                e = na_slots[n % 4]
                sc.activation(e, e, ACT.Exp, bias=ty("na", 4 * (n % 4) + 1), accum_out=ty("na", 4 * (n % 4) + 2))\
                  .then_inc(S.na_e, 1)

            def na_turn(n):
                h, qt = n // 2, n % 2
                act.wait_ge(S.na_t, n + 1)
                if h >= 2:
                    act.wait_ge(S.na_o, h - 1)
                dst = pt[h % 2].rearrange("p (k q) -> p k q", k=4)[:, :, qt * P:(qt + 1) * P]
                sc.activation(dst, psum[:, 2 + qt, :].rearrange("p (k q) -> p k q", k=4), ACT.Copy)\
                  .then_inc(S.na_tout, 1)

            def na_hi(m):
                act.wait_ge(S.na_o, 2 * m + 2)
                sc.activation(u_hi[:, 4 + m, 0:T], psum[:, 4 + m % 2, 0:T], ACT.Copy).then_inc(S.operand_hi, 1)

            na_exp(0)
            for n in range(16):
                if n < 15:
                    na_exp(n + 1)
                na_turn(n)
                if n % 4 == 0 and n:
                    na_hi(n // 4 - 1)
            na_hi(3)
            pump_to(AT["mlp0"] + AHEAD - 1)
            norm_only("woe")
            buffer_operand(buf[3], S.full_ready, 4)
            sqrelu("mlp0")

            norm_only("mlp0")
            for g in range(4):
                act.wait_ge(S.pooled, g + 1)
                sc.activation(u_hi[:, 2 * g:2 * g + 2, 0:T],
                              buf[g][:, 1088:1600].rearrange("p (k t) -> p k t", k=2), ACT.Copy)\
                  .then_inc(S.operand_hi, 2)
            pump_to(AT["mlp1"] + AHEAD - 1)
            norm_only("pool")
            buffer_operand(buf[3], S.full_ready, 8)
            sqrelu("mlp1")
            for b in range(4):
                act.wait_ge(S.acc_read, 4 * RD["mlp1"] + b + 1)
                act.dma_start(out[:, half(b)], x_t[:, half(b)]).then_inc(S.out_done, 16)

        @block.vector
        def _(dve):
            ve = nc.vector
            nxt = [0]
            chain = [0]

            def link(ins):
                chain[0] += 1
                ins.then_inc(S.dve_chain, 1)
                dve.wait_ge(S.dve_chain, chain[0])

            def split_lo(c, i=0):
                dve.wait_ge(S.hi_ready, RING * i + c + 1)
                u = slice((c % RING) * UNIT, (c % RING + 1) * UNIT)
                ve.tensor_tensor(w_lo[:, u], raw[:, u], w_hi[:, u].bitcast(F32), ALU.subtract).then_inc(S.lo_ready, 1)

            def pump_to(last):
                while nxt[0] <= min(last, UNITS - 1):
                    split_lo(nxt[0])
                    nxt[0] += 1

            def acc_ready(name, b):
                dve.wait_ge(S.acc_ready, 4 * ACC[name] + b + 1)

            def inverse_root(m, r, y):
                link(ve.reciprocal(y, r))
                link(ve.scalar_tensor_tensor(r, y, -0.5, m, ALU.mult, ALU.mult))
                link(ve.tensor_tensor(r, r, y, ALU.mult))
                return ve.scalar_tensor_tensor(y, r, 1.5, y, ALU.add, ALU.mult)

            def rms(name):
                n = NRM[name]
                dve.wait_ge(S.ms_psum, n + 1)
                ve.tensor_scalar(ms[:, 0:T], psum[:, 7, 0:T], 1.0 / D, EPS, ALU.mult, ALU.add).then_inc(S.ms_ready, 1)
                dve.wait_ge(S.root_ready, n + 1)
                link(inverse_root(ms[:, 0:T], root_t[:, 0:T], rstd[:, :]))

            def update_x(name, coef=None):
                for b in range(4):
                    acc_ready(name, b)
                    if coef is None or isinstance(coef, float):
                        ins = ve.scalar_tensor_tensor(x_t[:, half(b)], psum[:, b, :], coef or 1.0, x_t[:, half(b)],
                                                      ALU.mult, ALU.add)
                    else:
                        for k in (2 * b, 2 * b + 1):
                            ins = ve.scalar_tensor_tensor(x[:, k, :], bank2(b)[:, k % 2, :], coef(k), x[:, k, :],
                                                          ALU.mult, ALU.add)
                    ins.then_inc(S.acc_read, 1)

            def gain_operand_lo(op, gain, first=0, end=NC):
                for k in range(first, end):
                    dve.wait_ge(S.operand_hi, NC * OPS[op] + k + 1)
                    ve.scalar_tensor_tensor(u_lo[:, k, 0:T], x[:, k, :], col(gain, k), u_hif[:, k, 0:T],
                                            ALU.mult, ALU.subtract).then_inc(S.operand_ready, 1)

            def update_and_operand(name, op, gain, coef):
                for b in range(5):
                    if b < 4:
                        acc_ready(name, b)
                        ve.scalar_tensor_tensor(x_t[:, half(b)], psum[:, b, :], coef, x_t[:, half(b)],
                                                ALU.mult, ALU.add).then_inc(S.acc_read, 1)
                    if b:
                        for k in (2 * b - 2, 2 * b - 1):
                            dve.wait_ge(S.operand_hi, NC * OPS[op] + k + 1)
                            ve.scalar_tensor_tensor(u_lo[:, k, 0:T], x[:, k, :], col(gain, k), u_hif[:, k, 0:T],
                                                    ALU.mult, ALU.subtract).then_inc(S.operand_ready, 1)

            def buffer_operand_lo(op, src):
                for b in range(4):
                    dve.wait_ge(S.operand_hi, NC * OPS[op] + 2 * b + 2)
                    ve.tensor_tensor(u_lo[:, 2 * b:2 * b + 2, 0:T], ck(src)[:, 2 * b:2 * b + 2, :],
                                     u_hif[:, 2 * b:2 * b + 2, 0:T], ALU.subtract).then_inc(S.operand_ready, 2)

            def full_norm(src, dst, gain, shift, done):
                for b in range(4):
                    link(ve.tensor_tensor(ck(dst)[:, 2 * b:2 * b + 2, :], src[:, 2 * b:2 * b + 2, :],
                                          over2(rstd[:, :]), ALU.mult))
                    for k in (2 * b, 2 * b + 1):
                        ins = ve.tensor_scalar(ck(dst)[:, k, :], ck(dst)[:, k, :], gain(k), shift(k),
                                               ALU.mult, ALU.add)
                    ins.then_inc(done, 1)

            def swiglu(name):
                c0, h0, g0 = AT[name], STEPS[name], MODG * int(name[3])
                l, j0 = int(name[3]) // 2, 4 * MODG * (int(name[3]) % 2)

                def hidden(j, par, c, i=0, n_units=4):
                    dve.wait_ge(S.up_ready, h0 + j + 1)
                    ve.tensor_tensor(t2.rearrange("p (k t) -> p k t", k=2), bank2(4 + par), over2(rstd[:, :]),
                                     ALU.mult).then_inc(S.up_scaled, 1)
                    if n_units:
                        split_lo(c, i)
                    dve.wait_ge(S.gated, h0 + j + 1)
                    ve.tensor_tensor(h32[:, 0:T], sil, t2[:, T:2 * T], ALU.mult).then_inc(S.hid_f32, 1)
                    if n_units > 1:
                        split_lo(c + 1, i)
                    dve.wait_ge(S.hid_hi_ready, h0 + j + 1)
                    ve.tensor_tensor(hid_lo[:, par, 0:T], h32[:, 0:T], hid_hif[:, par, 0:T], ALU.subtract)\
                      .then_inc(S.hid_ready, 1)
                    for n in range(2, n_units):
                        split_lo(c + n, i)

                pump_to(c0 + 7)
                with dve.Fori(0, (FFS - 2) // 4) as i:
                    for s in range(4):
                        hidden(4 * i + s, s % 2, c0 + 8 + 4 * s, 2 * i)
                        if s == 2:
                            modulation(l, j0 + 4 * i, g0 + i)
                hidden(FFS - 2, 0, c0 + FFU - 2)
                nxt[0] = c0 + FFU + 2
                pump_to(c0 + FFU + 3)
                hidden(FFS - 1, 1, None, n_units=0)
                pump_to(c0 + FFU - 1 + AHEAD)

            def last_modulation(f):
                modulation(f // 2, 4 * MODG * (f % 2) + 4 * MODG - 4, MODG * (f + 1) - 1)

            def modulation(l, j, g):
                dve.wait_ge(S.mod_turned, g + 1)
                where = bass.ds(j, 4) if not isinstance(j, int) else slice(j, j + 4)
                ve.tensor_reduce(mod[:, l, where, :], psum[:, 7, 0:16].rearrange("p (m t c) -> p m c t", m=4, t=2),
                                 AX_X, ALU.add).then_inc(S.mod_read, 1)

            def modulation_bias(l):
                dve.wait_ge(S.mod_read, 2 * MODG * (l + 1))
                bias = prm[:, COL["bmod"] + 48 * l:COL["bmod"] + 48 * (l + 1)].unsqueeze(2).broadcast_to([P, 48, 2])
                link(ve.tensor_tensor(mod[:, l, :, :], mod[:, l, :, :], bias, ALU.add))

            def part(l, n, k=None, c=0):
                if k is None:
                    return mod[:, l, NC * n:NC * (n + 1), c]
                return mod[:, l, NC * n + k, c:c + 1]

            def scale_gain(dst, l, n, gain, c=0):
                link(ve.scalar_tensor_tensor(ty(dst, n=NC), part(l, n, c=c), 1.0, col(gain, n=NC), ALU.add, ALU.mult))

            def sqrelu(name):
                c0, h0 = AT[name], STEPS[name]
                assert nxt[0] == c0 + AHEAD

                def hidden(j, par, c, i=0, last_step=False):
                    dve.wait_ge(S.up_ready, h0 + j + 1)
                    ve.tensor_scalar(t2, psum[:, 4 + par, :], 0.0, None, ALU.max).then_inc(S.up_scaled, 1)
                    dve.wait_ge(S.up_scaled, h0 + j + 1)
                    ve.tensor_tensor(h32, t2, t2, ALU.mult).then_inc(S.hid_f32, 1)
                    if not last_step:
                        split(c, i)
                        split(c + 1, i)
                    dve.wait_ge(S.hid_hi_ready, h0 + j + 1)
                    ve.tensor_tensor(hid_lo[:, par, :], h32, hid_hif[:, par, :], ALU.subtract).then_inc(S.hid_ready, 1)
                    for n in range(0 if last_step else 2, 4):
                        split(c + n, i)

                last = min(c0 + 4 * MLS + AHEAD, UNITS)

                def split(c, i):
                    if not isinstance(i, int) or c < last:
                        split_lo(c, i)

                pump_to(c0 + 1 + AHEAD)
                with dve.Fori(0, (MLS - 2) // 2) as i:
                    for s in range(2):
                        hidden(2 * i + s, s, c0 + 2 + 4 * s + AHEAD, i)
                hidden(MLS - 2, 0, c0 + 4 * MLS - 6 + AHEAD)
                hidden(MLS - 1, 1, c0 + 4 * MLS - 2 + AHEAD, last_step=True)
                nxt[0] = last

            def head_norm(name, t, chunks, w, gain, b0):
                n = HN[name]
                dve.wait_ge(S.head_sum, n + 1)
                ve.tensor_scalar(ms[0:16, 0:w], psum[0:16, HEAD_BANK[name], 0:w], 1.0 / HD, EPS, ALU.mult, ALU.add)\
                  .then_inc(S.head_ms, 1)
                dve.wait_ge(S.head_root, n + 1)
                inverse_root(ms[0:16, 0:w], root_t[0:16, 0:w], head_rs[0:16, 0:w]).then_inc(S.head_rs, 1)
                for b in range(chunks * w // 512):
                    dve.wait_ge(S.head_bc, HNP[name] + b + 1)
                    ve.scalar_tensor_tensor(t[:, half(b)], t[:, half(b)], col(gain), psum[:, b0 + b, :],
                                            ALU.mult, ALU.mult).then_inc(S.normed, 1)

            dve.wait_ge(S.cond_hi_ready, 1)
            ve.tensor_tensor(cond[:, :, 2:4], ty("cond", n=16).rearrange("p (k c) -> p k c", c=2), condf[:, :, 0:2],
                             ALU.subtract)\
              .then_inc(S.cond_ready, 1)
            link(ve.tensor_scalar(ty("relu", n=NC), col("lam", n=NC), -1.0, 0.0, ALU.mult, ALU.max))
            link(ve.tensor_scalar(ty("q", n=NC), col("lam", n=NC), 0.0, None, ALU.max))
            link(ve.tensor_tensor(ty("negabs", n=NC), ty("relu", n=NC), ty("q", n=NC), ALU.add))
            ve.tensor_scalar(ty("negabs", n=NC), ty("negabs", n=NC), -1.0, None, ALU.mult).then_inc(S.lam_abs, 1)

            pump_to(1)
            gain_operand_lo("ffn0", "ffn1_0", 0, 4)
            pump_to(3)
            gain_operand_lo("ffn0", "ffn1_0", 4)
            pump_to(AHEAD + 1)
            rms("start")
            swiglu("ffn0")

            update_and_operand("ffn0", "mix0", "mix_0", 0.5)
            last_modulation(0)
            link(ve.memset(pad[:, :, 0:CONV - 1], 0.0))
            rms("ffn0")
            pump_to(AT["rec"] + 7 + 3)
            dve.wait_ge(S.lam_exp, 1)
            e, den, q, q2, poly = (ty(n, n=NC) for n in ("e", "den", "q", "q2", "poly"))
            link(ve.tensor_scalar(den, e, 2.0, None, ALU.add))
            link(ve.reciprocal(den, den))
            link(ve.tensor_tensor(q, e, den, ALU.mult))
            link(ve.tensor_tensor(q2, q, q, ALU.mult))
            link(ve.tensor_scalar(poly, q2, 1.0 / 15, None, ALU.mult))
            for m in (13, 11, 9, 7, 5, 3):
                link(ve.scalar_tensor_tensor(poly, poly, 1.0 / m, q2, ALU.add, ALU.mult))
            link(ve.scalar_tensor_tensor(poly, poly, 1.0, q, ALU.add, ALU.mult))
            link(ve.scalar_tensor_tensor(poly, poly, 2.0, ty("relu", n=NC), ALU.mult, ALU.add))
            ve.tensor_scalar(ty("sp8", n=NC), poly, 8.0, None, ALU.mult).then_inc(S.lam_ready, 1)
            ve.tensor_scalar(ty("nsp8", n=NC), poly, -8.0, None, ALU.mult).then_inc(S.lam_ready, 1)
            for b in range(4):
                acc_ready("rec", b)
                ve.tensor_tensor(pad[:, 2 * b:2 * b + 2, CONV - 1:], bank2(b), over2(rstd[:, :]), ALU.mult)\
                  .then_inc(S.acc_read, 1)
            pump_to(AT["gate"] + 4)
            xc = ck(buf[0])
            for tap in range(1, CONV):
                for k in range(NC):
                    if tap == 1:
                        dve.wait_ge(S.conv_first, k + 1)
                    else:
                        dve.wait_ge(S.conv_tap, NC * (tap - 2) + k + 1)
                    ve.scalar_tensor_tensor(xc[:, k, :], pad[:, k, tap:tap + T], col(f"cw{tap}", k), xc[:, k, :],
                                            ALU.mult, ALU.add).then_inc(S.conv_tap, 1)
                if tap == 1:
                    pump_to(AT["gate"] + 7)
            for b in range(4):
                dve.wait_ge(S.xc_hi, b + 1)
                ve.tensor_tensor(u_lo[:, 2 * b:2 * b + 2, T:2 * T], xc[:, 2 * b:2 * b + 2, :],
                                 u_hif[:, 2 * b:2 * b + 2, T:2 * T], ALU.subtract).then_inc(S.xc_lo, 1)
            pump_to(AT["i"] + 1)
            for b in range(4):
                acc_ready("gate", b)
                ve.tensor_tensor(ck(buf[1])[:, 2 * b:2 * b + 2, :], bank2(4 + b), over2(rstd[:, :]), ALU.mult)\
                  .then_inc(S.acc_read, 1)
            pump_to(AT["wout"] + 3)
            for b in range(4):
                dve.wait_ge(S.gates_read, NC + 2 * b + 2)
                ve.tensor_tensor(buf[3][:, half(b)], buf[3][:, half(b)], buf[0][:, half(b)], ALU.mult)\
                  .then_inc(S.mixed_in, 1)
            for b in range(4):
                dve.wait_ge(S.lru_decay, 2 * b + 2)
                dve.wait_ge(S.mixed_in, b + 1)
                link(ve.tensor_tensor(buf[0][:, half(b)], buf[2][:, half(b)], buf[2][:, half(b)], ALU.mult))
                ve.scalar_tensor_tensor(buf[4][:, half(b)], buf[0][:, half(b)], 1.0, buf[4][:, half(b)],
                                        ALU.add, ALU.mult).then_inc(S.lru_m2, 1)
            a, hs = ck(buf[2]), ck(buf[0])
            for b in range(4):
                dve.wait_ge(S.lru_sqrt, b + 1)
                link(ve.tensor_tensor(buf[3][:, half(b)], buf[3][:, half(b)], buf[4][:, half(b)], ALU.mult))
                for k in (2 * b, 2 * b + 1):
                    ins = ve.tensor_tensor_scan(hs[:, k, :], a[:, k, :], ck(buf[3])[:, k, :], 0.0, ALU.mult, ALU.add)
                link(ins)
                dve.wait_ge(S.gelu_done, b + 1)
                ve.tensor_tensor(buf[1][:, half(b)], buf[0][:, half(b)], buf[1][:, half(b)], ALU.mult)\
                  .then_inc(S.lru_y, 1)
            buffer_operand_lo("y", buf[1])
            pump_to(AT["ffn1"] + AHEAD - 1)
            update_and_operand("wout", "ffn1", "ffn2_0", 1.0)
            pump_to(AT["ffn1"] + 7)
            rms("wout")
            swiglu("ffn1")

            update_and_operand("ffn1", "kv", "kv", 0.5)
            last_modulation(1)
            modulation_bias(0)
            rms("ffn1")
            for dst, n, gain, c in (("G1", 1, "n1_0", 0), ("Gc", 1, "n1_0", 1), ("G2", 4, "n2_0", 0)):
                scale_gain(dst, 0, n, gain, c)
            pump_to(AT["v"] + 4)
            for b in range(4):
                acc_ready("k", b)
                ve.tensor_tensor(ck(buf[1])[:, 2 * b:2 * b + 2, :], bank2(b), over2(rstd[:, :]), ALU.mult)\
                  .then_inc(S.acc_read, 1)
            head_norm("k", buf[1], NC, T, "kg", 0)
            pump_to(AT["ffn2"] + AHEAD - 1)
            for b in range(4):
                acc_ready("v", b)
                ve.tensor_tensor(ck(buf[0])[:, 2 * b:2 * b + 2, :], bank2(4 + b), over2(rstd[:, :]), ALU.mult)\
                  .then_inc(S.acc_read, 1)
            gain_operand_lo("ffn2", "ffn1_1")
            for b in range(4):
                dve.wait_ge(S.v_turned, b + 1)
                ve.tensor_copy(buf[2][:, half(b)], psum[:, b, :]).then_inc(S.v_out, 1)
            pump_to(AT["ffn2"] + 7)
            dve.wait_ge(S.ms_psum, NRM["ctx"] + 1)
            ve.tensor_scalar(ms[:, T:2 * T], psum[:, 7, 0:T], 1.0 / D, EPS, ALU.mult, ALU.add).then_inc(S.ms_ready, 1)
            swiglu("ffn2")

            update_and_operand("ffn2", "mix1", "mix_1", 0.5)
            last_modulation(2)
            rms("ffn2")
            pump_to(AT["q"] + 7)
            dve.wait_ge(S.root_ready, NRM["ctx"] + 1)
            rc = buf5[:, 1792:2048]
            link(inverse_root(ms[:, T:2 * T], root_t[:, T:2 * T], rc))
            for b in range(4):
                link(ve.tensor_tensor(ck(buf[3])[:, 2 * b:2 * b + 2, :], ck(buf[3])[:, 2 * b:2 * b + 2, :],
                                      over2(rc), ALU.mult))
                for k in (2 * b, 2 * b + 1):
                    ins = ve.tensor_scalar(ck(buf[3])[:, k, :], ck(buf[3])[:, k, :], ty("Gc", k), part(0, 0, k, 1),
                                           ALU.mult, ALU.add)
                ins.then_inc(S.ctx_full, 1)
            for b in range(4):
                dve.wait_ge(S.ctx_hi, b + 1)
                ve.tensor_tensor(u_lo[:, 2 * b:2 * b + 2, T:2 * T], ck(buf[3])[:, 2 * b:2 * b + 2, :],
                                 u_hif[:, 2 * b:2 * b + 2, T:2 * T], ALU.subtract).then_inc(S.ctx_lo, 1)
            pump_to(AT["q"] + 7 + 3)
            for b in range(4):
                acc_ready("q", b)
                ve.tensor_tensor(ck(buf[0])[:, 2 * b:2 * b + 2, :], bank2(b), over2(rstd[:, :]), ALU.mult)\
                  .then_inc(S.acc_read, 1)
            head_norm("q", buf[0], NC, T, "qg", 4)
            pump_to(AT["wo"] + 4)

            def by_head(t):
                return t.rearrange("p (h c) -> p h c", h=2)

            def mask_scores(g):
                dve.wait_ge(S.z_ready, g + 1)
                if g >= 4:
                    dve.wait_ge(S.o_ready, g - 3)
                if g == 0:
                    dve.wait_ge(S.mixer_consts_in, 16)
                b = 2 * (g % 2)
                ve.scalar_tensor_tensor(by_head(z_slots[g % 4]), psum[:, b:b + 2, 0:STICK], HD ** -0.5,
                                        stick.unsqueeze(1).broadcast_to([P, 2, STICK]), ALU.mult, ALU.add)\
                  .then_inc(S.z_masked, 1)

            def softplus(g):
                dve.wait_ge(S.l_ready, g + 1)
                d = sp_slots[g % 2]
                ve.scalar_tensor_tensor(d, z_slots[g % 4], 0.0, d, ALU.max, ALU.add).then_inc(S.sp_ready, 1)

            mask_scores(0)
            mask_scores(1)
            softplus(0)
            for g in range(NC + 1):
                if g:
                    dve.wait_ge(S.cum_ready, g)
                    z, b = by_head(z_slots[(g - 1) % 4]), 4 + 2 * ((g - 1) % 2)
                    ve.tensor_tensor(z, z, psum[:, b:b + 2, 0:STICK], ALU.subtract).then_inc(S.w_arg, 1)
                if g + 2 < NC:
                    mask_scores(g + 2)
                if g + 1 < NC:
                    softplus(g + 1)
                if g:
                    dve.wait_ge(S.operand_hi, NC * OPS["att"] + g)
                    ve.tensor_tensor(u_lo[:, g - 1, 0:T], psum[:, b, 0:T], u_hif[:, g - 1, 0:T], ALU.subtract)\
                      .then_inc(S.operand_ready, 1)
            pump_to(AT["ffn3"] + AHEAD - 1)
            update_and_operand("wo", "ffn3", "ffn2_1", 1.0)
            pump_to(AT["ffn3"] + 7)
            rms("wo")
            swiglu("ffn3")

            update_x("ffn3", 0.5)
            last_modulation(3)
            modulation_bias(1)
            rms("ffn3")
            full_norm(x, buf[3], lambda k: ty("G1", k), lambda k: part(0, 0, k), S.full_ready)
            buffer_operand_lo("even", buf[3])
            for dst, n, gain in (("H1", 1, "n1_1"), ("H2", 4, "n2_1")):
                scale_gain(dst, 1, n, gain)
            link(ve.tensor_tensor(ty("Gp", n=NC), part(1, 2), col("pscale", n=NC), ALU.mult))
            pump_to(AT["fq2"] + 7 + 3)
            for b in range(4):
                acc_ready("fq2", b)
                ve.tensor_copy(buf[0][:, half(b)], psum[:, b, :]).then_inc(S.acc_read, 1)
            pump_to(AT["k2"] + 3 + 2)
            for b in range(4):
                acc_ready("k2", b)
                ve.tensor_copy(buf[1][:, half(b)], psum[:, 4 + b, :]).then_inc(S.acc_read, 1)
            pump_to(AT["v2"] + 3)
            q2 = buf[0][:, 1024:2048]
            head_norm("q2", q2, 4, T, "qg2", 6)
            for b in range(4):
                acc_ready("v2", b)
                ve.tensor_copy(buf[2][:, half(b)], psum[:, b, :]).then_inc(S.acc_read, 1)
            for qt in range(2):
                dve.wait_ge(S.f_turned, qt + 1)
                if qt == 0:
                    dve.wait_ge(S.head_sum, HN["k2"] + 1)
                ve.tensor_copy(buf[4][:, half(qt)], psum[:, 6 + qt, :]).then_inc(S.f_out, 1)
            for kt in range(4):
                dve.wait_ge(S.v2_turned, kt + 1)
                ve.tensor_copy(buf[3][:, half(kt)], psum[:, kt, :]).then_inc(S.v2_out, 1)
            head_norm("k2", buf[1], 4, 512, "kg2", 0)
            pump_to(AT["four"] + 1)
            for g in range(4):
                dve.wait_ge(S.mixed_hi, g + 1)
                ve.tensor_tensor(hid_lo[:, g % 2, 0:T], psum[:, 6, 0:T], hid_hif[:, g % 2, 0:T], ALU.subtract)\
                  .then_inc(S.mixed_lo, 1)
                dve.wait_ge(S.operand_hi, NC * OPS["mixed"] + g + 1)
                ve.tensor_tensor(u_lo[:, g, 0:T], psum[:, 7, 0:T], u_hif[:, g, 0:T], ALU.subtract)\
                  .then_inc(S.operand_ready, 1)
            pump_to(AT["woe"] + 4)
            tabs = [buf[2], buf[4]]
            for n in range(2):
                dve.wait_ge(tab_in[n], 16)
                w = tabs[n][:, 0:TABW].rearrange("p (e c) -> p e c", c=HD)
                ve.tensor_tensor(w, w, colmask.unsqueeze(1).broadcast_to([P, TABW // HD, HD]), ALU.add)\
                  .then_inc(S.tab_ready, 1)

            def na_scores(n):
                h, qt = n // 2, n % 2
                s, z = na_slots[n % 4], NA_BANKS[n % 4]
                dve.wait_ge(S.na_z, n + 1)
                if n >= 4:
                    dve.wait_ge(S.na_t, n - 3)
                if h % 4 == 0:
                    dve.wait_ge(S.tab_ready, h // 4 + 1)
                at = (h % 4) * 6 * HD + (2 - 2 * qt) * HD
                ve.scalar_tensor_tensor(s[:, 0:T], psum[:, z, 0:T], HD ** -0.5, tabs[h // 4][:, at:at + T],
                                        ALU.mult, ALU.add)
                ve.tensor_scalar(s[:, T:2 * T], psum[:, z, T:2 * T], HD ** -0.5, None, ALU.mult)\
                  .then_inc(S.na_s, 1)
                dve.wait_ge(S.na_s, n + 1)
                a = 4 * (n % 4)
                link(ve.tensor_reduce(ty("na", a), s, AX_X, ALU.max))
                ve.tensor_scalar(ty("na", a + 1), ty("na", a), -1.0, None, ALU.mult).then_inc(S.na_max, 1)

            def na_normalise(n):
                s, a = na_slots[n % 4], 4 * (n % 4)
                dve.wait_ge(S.na_e, n + 1)
                link(ve.reciprocal(ty("na", a + 3), ty("na", a + 2)))
                ve.tensor_scalar(s, s, ty("na", a + 3), None, ALU.mult).then_inc(S.na_p, 1)

            def na_lo(m):
                dve.wait_ge(S.operand_hi, NC * OPS["mixed"] + 4 + m + 1)
                ve.tensor_tensor(u_lo[:, 4 + m, 0:T], psum[:, 4 + m % 2, 0:T], u_hif[:, 4 + m, 0:T],
                                 ALU.subtract).then_inc(S.operand_ready, 1)

            na_scores(0)
            na_scores(1)
            for n in range(16):
                if n < 14:
                    na_scores(n + 2)
                na_normalise(n)
                if n % 4 == 1 and n > 4:
                    na_lo(n // 4 - 1)
            na_lo(3)
            pump_to(AT["mlp0"] + AHEAD - 1)
            update_x("woe", lambda k: part(0, 2, k))
            rms("woe")
            full_norm(x, buf[3], lambda k: ty("G2", k), lambda k: part(0, 3, k), S.full_ready)
            buffer_operand_lo("mlp0", buf[3])
            sqrelu("mlp0")

            update_x("mlp0", lambda k: part(0, 5, k))
            rms("mlp0")
            W = T + 16

            def pieces(g):
                return [buf[g][:, n * 2 * W:(n + 1) * 2 * W].rearrange("p (k t) -> p k t", k=2) for n in range(3)]

            for g in range(4):
                u = pieces(g)[0]
                ve.memset(u[:, :, 0:8], 0.0)
                ve.memset(u[:, :, T + 8:W], 0.0)
                link(ve.tensor_tensor(u[:, :, 8:8 + T], x[:, 2 * g:2 * g + 2, :], over2(rstd[:, :]), ALU.mult))
                for k in range(2):
                    ins = ve.tensor_scalar(u[:, k, 8:8 + T], u[:, k, 8:8 + T], ty("H1", 2 * g + k),
                                           part(1, 0, 2 * g + k), ALU.mult, ALU.add)
                link(ins)
            dve.wait_ge(S.cnt_in, 16)
            for g in range(4):
                u, a, b = pieces(g)
                src, dst, other = u, a, b
                size = W
                for level in range(g + 1):
                    step = 1 << level
                    size -= step
                    link(ve.tensor_tensor(dst[:, :, 0:size], src[:, :, 0:size], src[:, :, step:step + size], ALU.add))
                    src, dst, other = dst, other, dst
                at = 8 - (1 << g)
                link(ve.tensor_tensor(src[:, :, at:at + T], src[:, :, at:at + T], over2(inv_cnt[:, g, :]), ALU.mult))
                pooled = buf[g][:, 1088:1600].rearrange("p (k t) -> p k t", k=2)
                if g % 2:
                    link(ve.tensor_copy(a[:, :, at:at + T], src[:, :, at:at + T]))
                    src = a
                ve.tensor_tensor(pooled, src[:, :, at:at + T], u[:, :, 8:8 + T], ALU.subtract).then_inc(S.pooled, 1)
            for g in range(4):
                dve.wait_ge(S.operand_hi, NC * OPS["pooled"] + 2 * g + 2)
                ve.tensor_tensor(u_lo[:, 2 * g:2 * g + 2, 0:T],
                                 buf[g][:, 1088:1600].rearrange("p (k t) -> p k t", k=2),
                                 u_hif[:, 2 * g:2 * g + 2, 0:T], ALU.subtract).then_inc(S.operand_ready, 2)
            pump_to(AT["mlp1"] + AHEAD - 1)
            update_x("pool", lambda k: ty("Gp", k))
            rms("pool")
            full_norm(x, buf[3], lambda k: ty("H2", k), lambda k: part(1, 3, k), S.full_ready)
            buffer_operand_lo("mlp1", buf[3])
            sqrelu("mlp1")
            update_x("mlp1", lambda k: part(1, 5, k))

        @block.tensor
        def _(pe):
            te = nc.tensor

            def unit_ready(c, i=0):
                pe.wait_ge(S.lo_ready, RING * i + c + 1)

            def operand(name, k):
                pe.wait_ge(S.operand_ready, NC * OPS[name] + k + 1)

            def read(name, b):
                pe.wait_ge(S.acc_read, 4 * RD[name] + b + 1)

            def norm_sum(name):
                n = NRM[name]
                pe.wait_ge(S.ssq_ready, n + 1)
                if n == 0:
                    pe.wait_ge(S.consts_in, 16)
                if name[:3] == "ffn":
                    pe.wait_ge(S.mod_read, MODG * (int(name[3]) + 1))
                te.matmul(psum[:, 7, 0:T], ones, buf[4][:, 0:T], start=True, stop=True).then_inc(S.ms_psum, 1)

            def product(dst, c, at, hi, lo, first, last):
                w = slice((c % RING) * UNIT + at, (c % RING) * UNIT + at + P)
                ins = te.matmul(dst, w_hi[:, w], hi, start=first, stop=False, skip_group_check=True)
                if begun[0] != c:
                    ins.then_inc(S.unit_used, 1)
                    begun[0] = c
                te.matmul(dst, w_hi[:, w], lo, start=False, stop=False, skip_group_check=True)
                return te.matmul(dst, w_lo[:, w], hi, start=False, stop=last, skip_group_check=True)

            begun = [-1]

            def all_k(c, i, dst, op=None):
                unit_ready(c, i)
                for k in range(NC):
                    if op:
                        operand(op, k)
                    ins = product(dst, c, k * P, u_hi[:, k, 0:T], u_lo[:, k, 0:T], k == 0, k == NC - 1)
                return ins

            def one_k(c, i, hi, lo, b0, first, last, free=None):
                unit_ready(c, i)
                for n in range(NC):
                    if free and n % 2 == 0:
                        free(n // 2)
                    ins = product(bank2(b0 + n // 2)[:, n % 2, :], c, n * P, hi, lo, first and n % 2 == 0, last)
                    if last and n % 2:
                        ins.then_inc(S.acc_ready, 1)

            def project(name, op, b0, free=None, hooks={}):
                for k in range(NC):
                    operand(op, k)
                    one_k(AT[name] + k, 0, u_hi[:, k, 0:T], u_lo[:, k, 0:T], b0, k == 0, k == NC - 1,
                          free if k == 0 else None)
                    if k in hooks:
                        hooks[k]()

            def block_diagonal(name, b0, t0, ready):
                for n in range(4):
                    c = AT[name] + n // 2
                    if n % 2 == 0:
                        unit_ready(c)
                    ready(n)
                    for kk in range(2):
                        for mo in range(2):
                            k = 2 * n + kk
                            ins = product(bank2(b0 + n)[:, mo, :], c, ((n % 2) * 4 + kk * 2 + mo) * P,
                                          u_hi[:, k, t0:t0 + T], u_lo[:, k, t0:t0 + T], kk == 0 and mo == 0, kk == 1)
                    ins.then_inc(S.acc_ready, 1)

            def modulate(c, i, q, g):
                unit_ready(c, i)
                if q == 0 and not (isinstance(g, int) and g == 0):
                    pe.wait_ge(S.mod_copied, g)
                if q == 0 and not isinstance(g, int):
                    pe.wait_ge(S.mod_read, g - 1)
                for kk in range(2):
                    at = slice((c % RING) * UNIT + kk * 512, (c % RING) * UNIT + (kk + 1) * 512)
                    k = 2 * q + kk
                    ins = te.matmul(psum[0:4, 6, :], cond[:, k, :], w_hi[:, at], start=k == 0, stop=False,
                                    skip_group_check=True)
                    if kk == 0:
                        ins.then_inc(S.unit_used, 1)
                    ins = te.matmul(psum[0:4, 6, :], cond[:, k, :], w_lo[:, at], start=False, stop=k == NC - 1,
                                    skip_group_check=True)
                if q == 3:
                    ins.then_inc(S.mod_rows, 1)

            def turn_modulation():
                for m in range(4):
                    ins = te.transpose(psum[:, 7, 4 * m:4 * m + 4], mod_rows[:, m * P:(m + 1) * P], ident[0:4, 0:4])
                ins.then_inc(S.mod_turned, 1)

            def up(c, i, j, par, h0, op=None, between=lambda: None):
                if not isinstance(j, int) or j >= 2:
                    pe.wait_ge(S.up_scaled, h0 + j - 1)
                all_k(c, i, bank2(4 + par)[:, 0, :], op)
                between()
                all_k(c + 1, i, bank2(4 + par)[:, 1, :]).then_inc(S.up_ready, 1)

            def swiglu(name, norm):
                c0, h0, g0 = AT[name], STEPS[name], MODG * int(name[3])

                def down(j, par, c, i=0, first=False, last=False):
                    pe.wait_ge(S.hid_ready, h0 + j + 1)
                    one_k(c, i, hid_hi[:, par, 0:T], hid_lo[:, par, 0:T], 0, first, last)

                if g0 == 0:
                    pe.wait_ge(S.cond_ready, 1)
                for q in range(4):
                    modulate(c0 + q, 0, q, g0)
                up(c0 + 4, 0, 0, 0, h0, name, between=lambda: norm_sum(norm))
                up(c0 + 6, 0, 1, 1, h0)
                pe.wait_ge(S.ms_ready, NRM[norm] + 1)
                down(0, 0, c0 + 8, first=True)
                with pe.Fori(0, (FFS - 2) // 4) as i:
                    for s in range(4):
                        j, c = 2 + 4 * i + s, c0 + 9 + 4 * s
                        up(c, 2 * i, j, s % 2, h0)
                        modulate(c + 2, 2 * i, s, g0 + i + 1)
                        if s == 0:
                            turn_modulation()
                        down(j - 1, 1 - s % 2, c + 3, 2 * i)
                down(FFS - 1, 1, c0 + FFU - 1, last=True)
                pe.wait_ge(S.mod_copied, g0 + MODG)
                pe.wait_ge(S.mod_read, g0 + MODG - 1)
                turn_modulation()

            def sqrelu(name):
                c0, h0 = AT[name], STEPS[name]

                def down(j, par, c, i=0, first=False, last=False):
                    pe.wait_ge(S.hid_ready, h0 + j + 1)
                    for n in range(2):
                        one_k(c + n, i, hid_hi[:, par, n * T:(n + 1) * T], hid_lo[:, par, n * T:(n + 1) * T], 0,
                              first and n == 0, last and n == 1)

                up(c0, 0, 0, 0, h0, name)
                up(c0 + 2, 0, 1, 1, h0)
                down(0, 0, c0 + 4, first=True)
                with pe.Fori(0, (MLS - 2) // 2) as i:
                    for s in range(2):
                        j, c = 2 + 2 * i + s, c0 + 6 + 4 * s
                        up(c, i, j, s, h0)
                        down(j - 1, 1 - s, c + 2, i)
                down(MLS - 1, 1, c0 + 4 * MLS - 2, last=True)

            def head_sums(name, sq, chunks, w, free):
                b = HEAD_BANK[name]
                free()
                if name == "k":
                    pe.wait_ge(S.mixer_consts_in, 16)
                for m in range(chunks):
                    pe.wait_ge(S.head_sq, HNP[name] + (m * w) // 512 + 1)
                    ins = te.matmul(psum[0:16, b, 0:w], headsum[:, m, :], sq[:, m * w:(m + 1) * w],
                                    start=m == 0, stop=m == chunks - 1)
                ins.then_inc(S.head_sum, 1)

            def head_spread(name, chunks, w, b0, free=lambda b: None):
                pe.wait_ge(S.head_rs, HN[name] + 1)
                per = 512 // w
                for m in range(chunks):
                    b = b0 + m // per
                    if m % per == 0:
                        free(m // per)
                    ins = te.matmul(psum[:, b, (m % per) * w:(m % per + 1) * w], headbc[:, m, :], head_rs[0:16, 0:w],
                                    start=m % per == 0, stop=True, skip_group_check=True)
                    if m % per == per - 1:
                        ins.then_inc(S.head_bc, 1)

            swiglu("ffn0", "start")

            project("rec", "mix0", 0, lambda b: read("ffn0", b), hooks={1: lambda: norm_sum("ffn0")})
            pe.wait_ge(S.ms_ready, NRM["ffn0"] + 1)
            project("gate", "mix0", 4)

            def xc_ready(n):
                pe.wait_ge(S.xc_lo, n + 1)

            def r_free(n):
                xc_ready(n)
                read("rec", n)

            def i_free(n):
                xc_ready(n)
                read("gate", n)

            block_diagonal("r", 0, T, r_free)
            block_diagonal("i", 4, T, i_free)
            pe.wait_ge(S.gates_read, NC)
            project("wout", "y", 0)
            swiglu("ffn1", "wout")

            def k_sums():
                head_sums("k", buf[4], NC, T, lambda: read("k", 0))

            def k_spread():
                head_spread("k", NC, T, 0, lambda b: read("k", b))

            project("k", "kv", 0, lambda b: read("ffn1", b), hooks={0: lambda: norm_sum("ffn1")})
            pe.wait_ge(S.ms_ready, NRM["ffn1"] + 1)
            project("v", "kv", 4, hooks={1: k_sums, 3: k_spread})
            v_raw = ck(buf[0])
            for b in range(4):
                pe.wait_ge(S.normed, HNP["k"] + b + 1)
                for m in range(4):
                    chunk = 4 * (b % 2) + m
                    read("v", chunk // 2)
                    ins = te.transpose(psum[:, b, m * P:(m + 1) * P], v_raw[:, chunk, (b // 2) * P:(b // 2 + 1) * P],
                                       ident)
                ins.then_inc(S.v_turned, 1)
            swiglu("ffn2", "ctx")

            project("q", "mix1", 0, lambda b: read("ffn2", b), hooks={1: lambda: norm_sum("ffn2")})
            qt_, kt_ = ck(buf[0]), ck(buf[1])
            pe.wait_ge(S.ms_ready, NRM["ffn2"] + 1)
            head_sums("q", buf[4], NC, T, lambda: None)
            head_spread("q", NC, T, 4)

            def scores(g):
                pe.wait_ge(S.normed, HNP["q"] + g // 2 + 1)
                if g < 2:
                    read("q", 3)
                else:
                    pe.wait_ge(S.z_masked, g - 1)
                for h in range(2):
                    b, p0 = 2 * (g % 2) + h, HD * h
                    te.matmul(psum[:, b, 0:T], kt_[p0:p0 + HD, g, 0:P], qt_[p0:p0 + HD, g, :], start=True, stop=True)
                    ins = te.matmul(psum[:, b, T:STICK], kt_[p0:p0 + HD, g, P:T], qt_[p0:p0 + HD, g, P:T],
                                    start=True, stop=True)
                ins.then_inc(S.z_ready, 1)

            def sums_after(g):
                pe.wait_ge(S.sp_ready, g + 1)
                if g < 2:
                    pe.wait_ge(S.normed, HNP["q"] + 4)
                else:
                    operand("att", g - 2)
                for h in range(2):
                    b, s = 4 + 2 * (g % 2) + h, sp_slots[g % 2][:, h * STICK:(h + 1) * STICK]
                    te.matmul(psum[:, b, 0:T], tri, s[:, 0:T], start=True, stop=False, skip_group_check=True)
                    te.matmul(psum[:, b, P:T], ones, s[:, T:STICK], start=False, stop=False, skip_group_check=True)
                    ins = te.matmul(psum[:, b, T:STICK], tri, s[:, T:STICK], start=False, stop=True,
                                    skip_group_check=True)
                ins.then_inc(S.cum_ready, 1)

            def attend(g):
                pe.wait_ge(S.w_ready, g + 1)
                for h in range(2):
                    p0, f = HD * h, (2 * g + h) * HD
                    w = z_slots[g % 4][:, h * STICK:(h + 1) * STICK]
                    dst = psum[p0:p0 + HD, 4 + 2 * (g % 2), 0:T]
                    te.matmul(dst, buf[2][:, f:f + HD], w[:, 0:T], start=True, stop=False, skip_group_check=True)
                    ins = te.matmul(dst[:, P:T], buf[2][:, D + f:D + f + HD], w[:, T:STICK], start=False, stop=True,
                                    skip_group_check=True)
                ins.then_inc(S.o_ready, 1)

            scores(0)
            scores(1)
            for g in range(NC + 1):
                if g + 2 < NC:
                    scores(g + 2)
                if g < NC:
                    sums_after(g)
                if g:
                    attend(g - 1)
            pe.wait_ge(S.z_masked, NC)
            project("wo", "att", 0)
            swiglu("ffn3", "wo")

            norm_sum("ffn3")
            project("fq2", "even", 0, lambda b: read("ffn3", b))

            def project_both(name, b0, free):
                for k in range(NC):
                    c = AT[name] + k // 2
                    if k % 2 == 0:
                        unit_ready(c)
                    for n in range(4):
                        if k == 0:
                            free(n)
                        ins = product(psum[:, b0 + n, :], c, ((k % 2) * 4 + n) * P, u_hi[:, k, :], u_lo[:, k, :],
                                      k == 0, k == NC - 1)
                        if k == NC - 1:
                            ins.then_inc(S.acc_ready, 1)

            pe.wait_ge(S.ctx_lo, 4)
            project_both("k2", 4, lambda n: None)
            project_both("v2", 0, lambda n: read("fq2", n))
            head_sums("q2", buf[4], 4, T, lambda: read("k2", 3))
            head_spread("q2", 4, T, 6)
            head_sums("k2", buf[4], 4, 512, lambda: None)
            pe.wait_ge(S.normed, HNP["q2"] + 2)
            f_raw = buf[0][:, 0:1024].rearrange("p (k t) -> p k t", k=4)
            for qt in range(2):
                for g in range(4):
                    ins = te.transpose(psum[:, 6 + qt, g * P:(g + 1) * P], f_raw[:, g, qt * P:(qt + 1) * P], ident)
                ins.then_inc(S.f_turned, 1)
            v2_raw = ck(buf[2], 4)
            read("v2", 3)
            for kt in range(4):
                for m in range(4):
                    ins = te.transpose(psum[:, kt, m * P:(m + 1) * P], v2_raw[:, m, kt * P:(kt + 1) * P], ident)
                ins.then_inc(S.v2_turned, 1)
            head_spread("k2", 4, 512, 0, lambda b: pe.wait_ge(S.v2_out, b + 1))

            dftc = buf5[:, 1024:1024 + 2 * P]

            def token_dft(g):
                if g == 0:
                    pe.wait_ge(S.late_in, 16)
                    pe.wait_ge(S.f_out, 2)
                if g < 2:
                    pe.wait_ge(S.head_ms, HN["q2"] + 1 + g)
                else:
                    pe.wait_ge(S.dft1_out, g - 1)
                for qt in range(2):
                    at = qt * 512
                    ins = te.matmul(psum[:, 4 + g % 2, :], buf[4][:, at + g * P:at + (g + 1) * P],
                                    buf5[:, at:at + 512], start=qt == 0, stop=qt == 1)
                ins.then_inc(S.dft1, 1)

            token_dft(0)
            for g in range(4):
                if g < 3:
                    token_dft(g + 1)
                ab = buf[4][:, 1024 + (g % 2) * 512:1536 + (g % 2) * 512]
                pe.wait_ge(S.dft1_out, g + 1)
                if g:
                    pe.wait_ge(S.mixed_lo, g)
                te.matmul(psum[:, 6, 0:T], dftc[:, 0:P], ab[:, 0:T], start=True, stop=False)
                te.matmul(psum[:, 6, 0:T], dftc[:, P:2 * P], ab[:, T:2 * T], start=False, stop=True)\
                  .then_inc(S.dft2, 1)
                pe.wait_ge(S.mixed_lo, g + 1)
                if g:
                    operand("mixed", g - 1)
                c = AT["four"] + g // 2
                unit_ready(c)
                product(psum[:, 7, 0:T], c, (g % 2) * P, hid_hi[:, g % 2, 0:T], hid_lo[:, g % 2, 0:T], True, True)\
                  .then_inc(S.dft3, 1)

            q2, k2 = ck(buf[0])[:, 4:8, :], ck(buf[1], 4)
            vt = ck(buf[3], 4)
            pt = [buf[0][:, 0:1024], buf5[:, 1024:2048]]

            def na_scores(n):
                h, qt = n // 2, n % 2
                m, p0 = h // 2, HD * (h % 2)
                if n == 0:
                    pe.wait_ge(S.normed, HNP["k2"] + 4)
                if n == 2:
                    operand("mixed", 3)
                if n >= 4:
                    pe.wait_ge(S.na_s, n - 3)
                te.matmul(psum[:, NA_BANKS[n % 4], :], q2[p0:p0 + HD, m, qt * P:(qt + 1) * P], k2[p0:p0 + HD, m, :],
                          start=True, stop=True).then_inc(S.na_z, 1)

            def na_turn(n):
                qt = n % 2
                p = na_slots[n % 4]
                pe.wait_ge(S.na_p, n + 1)
                if n >= 2:
                    pe.wait_ge(S.na_tout, n - 1)
                for kt in range(4):
                    ins = te.transpose(psum[:, 2 + qt, kt * P:(kt + 1) * P], p[:, kt * P:(kt + 1) * P], ident)
                ins.then_inc(S.na_t, 1)

            def na_attend(h):
                m, p0 = h // 2, HD * (h % 2)
                pe.wait_ge(S.na_tout, 2 * h + 2)
                if m >= 2:
                    operand("mixed", 4 + m - 2)
                w = pt[h % 2].rearrange("p (k q) -> p k q", k=4)
                for kt in range(4):
                    ins = te.matmul(psum[p0:p0 + HD, 4 + m % 2, 0:T], vt[:, kt, h * HD:(h + 1) * HD], w[:, kt, :],
                                    start=kt == 0, stop=kt == 3)
                ins.then_inc(S.na_o, 1)

            for n in range(3):
                na_scores(n)
            for n in range(16):
                if n < 13:
                    na_scores(n + 3)
                na_turn(n)
                if n % 2 == 0 and n:
                    na_attend(n // 2 - 1)
            na_attend(7)
            project("woe", "mixed", 0)
            norm_sum("woe")
            sqrelu("mlp0")

            norm_sum("mlp0")
            block_diagonal("pool", 0, 0, lambda n: operand("pooled", 2 * n + 1))
            norm_sum("pool")
            sqrelu("mlp1")


def weight_stream(w):
    units = np.zeros((UNITS, P, UNIT), np.float32)

    def k_in(m):
        return m.reshape(-1, P, D)

    def n_out(m):
        return m.reshape(NC, P, -1, P).transpose(2, 1, 0, 3).reshape(-1, P, D)

    def blocks(m):
        return m.reshape(2, 2, 2, P, 2, P).transpose(0, 3, 1, 2, 4, 5).reshape(2, P, UNIT)

    def halves(m):
        return m.reshape(4, 2, P, 512).transpose(0, 2, 1, 3).reshape(4, P, UNIT)

    mods = w["w_mod_2"].reshape(2, 4, 2, P, 12, 512).transpose(0, 4, 1, 3, 2, 5).reshape(-1, P, UNIT)

    for f, (w13, w2) in enumerate([("ffn1_w13", "ffn1_w2"), ("ffn2_w13", "ffn2_w2")] * 2):
        l, c0 = f // 2, AT[f"ffn{f}"]
        u13, u2 = n_out(w[w13][l]), k_in(w[w2][l])
        m0 = 4 * MODG * f
        units[c0:c0 + 4] = mods[m0:m0 + 4]
        for j in range(FFS):
            c = c0 + 4 + 2 * j if j < 2 else c0 + 4 * j + 1
            units[c], units[c + 1] = u13[j], u13[FFS + j]
            if j > 1:
                units[c + 2] = mods[m0 + 2 + j]
            if j:
                units[c + (2 if j == 1 else 3)] = u2[j - 1]
        units[c0 + FFU - 1] = u2[FFS - 1]
    for m, name in enumerate(["mlp0", "mlp1"]):
        c0 = AT[name]
        u1, u2 = n_out(w["w_mlp1_2"][m]), k_in(w["w_mlp2_2"][m])
        for j in range(MLS):
            c = c0 + 4 * j - 2 * (j > 0)
            units[c:c + 2] = u1[2 * j:2 * j + 2]
            if j:
                units[c + 2:c + 4] = u2[2 * j - 2:2 * j]
        units[c0 + 4 * MLS - 2:c0 + 4 * MLS] = u2[2 * MLS - 2:]
    a_in, w_even, w_kv = w["a_w_in"][0], w["w_in_even_2"][0], w["w_kv"]
    whole = {"gate": a_in[:, :D], "rec": a_in[:, D:], "wout": w["a_w_out"][0], "k": w_kv[:, :D], "v": w_kv[:, D:],
             "q": w["b_w_q"][0], "wo": w["b_w_o"][0], "fq2": w_even[:, :D], "woe": w["w_out_even_2"][0]}
    for name, m in whole.items():
        units[AT[name]:AT[name] + 8] = k_in(m)
    for name, m in {"r": w["a_w_r"][0], "i": w["a_w_i"][0], "pool": w["w_pool_2"][0]}.items():
        units[AT[name]:AT[name] + 2] = blocks(m)
    units[AT["k2"]:AT["k2"] + 4] = halves(w_even[:, D:D + 512])
    units[AT["v2"]:AT["v2"] + 4] = halves(w_even[:, D + 512:])
    four = w["w_four_2"][0].transpose(1, 0, 2).reshape(P, 4 * P)
    units[AT["four"], :, :2 * P], units[AT["four"] + 1, :, :2 * P] = four[:, :2 * P], four[:, 2 * P:]
    return units.reshape(UNITS // 2, 2, P, UNIT).transpose(0, 2, 1, 3).reshape(UNITS // 2, P, 2 * UNIT)


def by_feature(v):
    return v.reshape(NC, P).T


def small_params(w):
    prm = np.zeros((P, NSMALL), np.float32)
    vectors = [w["ffn1_norm"][0], w["ffn1_norm"][1], w["mix_norm"][0], w["mix_norm"][1], w["kv_norm"],
               w["ffn2_norm"][0], w["ffn2_norm"][1], w["norm1_g_2"][0], w["norm1_g_2"][1], w["norm2_g_2"][0],
               w["norm2_g_2"][1], *w["a_conv_w"][0], w["a_conv_b"][0], w["a_b_r"][0], w["a_b_i"][0],
               w["a_lambda"][0], w["pool_scale_2"][0]]
    for n, v in enumerate(vectors):
        prm[:, NC * n:NC * (n + 1)] = by_feature(v)
    prm[:, COL["cond"]:COL["cond"] + 2 * NC:2] = by_feature(w["c_2"][0])
    prm[:, COL["cond"] + 1:COL["cond"] + 2 * NC:2] = by_feature(w["c_ctx_2"])
    prm[:, COL["bmod"]:COL["bmod"] + 96] = w["b_mod_2"].reshape(96, P).T
    for name, v in (("kg", w["k_norm"]), ("qg", w["q_norm"][0]), ("kg2", w["k_norm_g_2"][0]),
                    ("qg2", w["q_norm_g_2"][0])):
        prm[:HD, COL[name]] = v
        prm[HD:, COL[name]] = v
    return prm


def shape_constants():
    p = np.arange(P)
    cst = np.zeros((P, NCONST), np.float32)
    cst[:, CC["ident"]:CC["ident"] + P] = np.eye(P)
    cst[:, CC["ones"]:CC["ones"] + P] = 1.0
    cst[:, CC["tri"]:CC["tri"] + P] = p[:, None] >= p[None, :]
    for m in range(NC):
        for half in range(2):
            h = 2 * m + half
            cst[HD * half:HD * (half + 1), CC["headsum"] + 16 * m + h] = 1.0
            cst[h, CC["headbc"] + P * m + HD * half:CC["headbc"] + P * m + HD * (half + 1)] = 1.0
    diagonal = np.where(p[:, None] < p[None, :], 0.0, BIG)
    cst[:, CC["stick"]:CC["stick"] + P] = diagonal
    cst[:, CC["stick"] + T:CC["stick"] + STICK] = diagonal
    c = np.arange(64)
    start = np.clip(c - 8, 0, 48)
    window = (c[None, :] >= start[:, None]) & (c[None, :] < start[:, None] + 16)
    cst[:, CC["colmask"]:CC["colmask"] + HD] = np.tile(np.where(window, 0.0, BIG), (2, 1))
    late = np.zeros((P, NLATE), np.float32)
    t = np.arange(T)
    a = 2 * np.pi * (np.outer(t, t) % T) / T
    dft = np.concatenate([np.cos(a), np.sin(a)], 1)
    late[:, :1024] = dft.reshape(2, P, 512).transpose(1, 0, 2).reshape(P, 1024)
    a = 2 * np.pi * (np.outer(p, p) % P) / P
    late[:, 1024:] = np.concatenate([np.cos(a), -np.sin(a)], 1) / np.sqrt(T * P)
    cnt = np.zeros((4, T), np.float32)
    for g in range(4):
        w = 2 << g
        cnt[g] = 1.0 / (np.clip(t + w - w // 2, 0, T) - np.clip(t - w // 2, 0, T))
    return cst, late, np.broadcast_to(cnt.reshape(1, 4 * T), (P, 4 * T)).copy()


def bias_windows(rpb):
    wide = np.zeros((8, 15, 3 * 64), np.float32)
    wide[:, :, 64:64 + 31] = rpb
    tab = np.zeros((2, P, 4, 6, 64), np.float32)
    for c in range(64):
        at = 64 + 15 - c
        rows = wide[:, :, at:at + 64]
        tab[:, c] = rows[:, 5:11].reshape(2, 4, 6, 64)
        tab[:, 64 + c] = rows[:, 4:10].reshape(2, 4, 6, 64)
    return tab.reshape(2, P, TABW)


def kernel(**inputs):
    import concourse.bacc as bacc
    from concourse.bass_utils import run_bass_kernel_spmd

    w = {k: np.asarray(v) for k, v in inputs.items()}

    def tokens(v):
        return np.ascontiguousarray(v.reshape(T, NC, P).transpose(2, 1, 0).reshape(P, NC * T))

    cst, late, cnt = shape_constants()
    arrays = {"stream": weight_stream(w), "x_in": tokens(w["x"][0]), "ctx_in": tokens(w["ctx_2"][0]),
              "small": small_params(w), "consts": cst, "late": late, "cnt": cnt, "tab": bias_windows(w["rpb_2"][0])}
    nc = bacc.Bacc("TRN2", target_bir_lowering=False, num_devices=1)
    args = {}
    for name, a in arrays.items():
        arrays[name] = np.ascontiguousarray(a)
        args[name] = nc.dram_tensor(name, a.shape, mybir.dt.from_np(a.dtype), kind="ExternalInput").ap()
    out = nc.dram_tensor("out", (P, NC * T), F32, kind="ExternalOutput").ap()
    build(nc, out=out, **args)
    got = run_bass_kernel_spmd(nc, [arrays], core_ids=[0]).results[0]["out"]
    return got.reshape(P, NC, T).transpose(2, 1, 0).reshape(1, T, D)
```

```python
from contextlib import ExitStack

import numpy as np
from concourse import bass, mybir

F32 = mybir.dt.float32
F32R = mybir.dt.float32r
ALU = mybir.AluOpType
ACT = mybir.ActivationFunctionType
AX_X = mybir.AxisListType.X

P = 128
D = 1024
T = 256
NC = D // P
FF = 2816
FFS = FF // P
MLP = 4096
MLS = MLP // P // 2
CONV = 4
HD = 64
EPS = 1e-6
NMOD = 6
BIG = -1e30

UNIT = 1024
RING = 8
AHEAD = 6

FFU = 4 * FFS + 2
MODG = 6
PHASES = [("ffn0", FFU), ("rec", 8), ("gate", 6), ("r", 2), ("i", 2), ("gate_end", 2), ("wout", 8), ("ffn1", FFU),
          ("k", 8), ("v", 8), ("ffn2", FFU), ("q", 8), ("wo", 8), ("ffn3", FFU),
          ("k2", 4), ("fq2", 8), ("v2", 4), ("four", 2), ("woe", 8), ("mlp0", 4 * MLS),
          ("pool", 2), ("mlp1", 4 * MLS)]
AT = {}
_n = 0
for _name, _count in PHASES:
    AT[_name] = _n
    _n += _count
UNITS = _n
assert UNITS % RING == 0

SMALL = ["ffn1_0", "ffn1_1", "mix_0", "mix_1", "kv", "ffn2_0", "ffn2_1", "n1_0", "n1_1", "n2_0", "n2_1",
         "cw0", "cw1", "cw2", "cw3", "cb", "br", "bi", "lam", "pscale"]
COL = {n: NC * i for i, n in enumerate(SMALL)}
COL["cond"] = NC * len(SMALL)
COL["bmod"] = COL["cond"] + 2 * NC
COL["kg"] = COL["bmod"] + 2 * NMOD * NC
COL["qg"], COL["qg2"], COL["kg2"] = COL["kg"] + 1, COL["kg"] + 2, COL["kg"] + 3
NSMALL = COL["kg"] + 4

CC = {"ident": 0, "ones": 128, "tri": 256, "headsum": 384, "stick": 512, "colmask": 896, "headbc": 960}
NCONST = CC["headbc"] + NC * P
NLATE = 1024 + 2 * P
STICK = T + P
TABW = 4 * 6 * HD

TY = {n: NC * i for i, n in enumerate(["cond", "cond2", "negabs", "e", "den", "q", "q2", "poly", "sp8", "nsp8", "relu",
                                       "G1", "Gc", "G2", "H1", "H2", "Gp", "s", "na", "na_rest"])}

OPS = {n: i for i, n in enumerate("ffn0 mix0 y ffn1 kv ffn2 mix1 att ffn3 even mixed mlp0 mlp1".split())}
ACC = {n: i for i, n in enumerate("ffn0 rec r i gate wout ffn1 k v ffn2 q wo ffn3 k2 fq2 v2 woe mlp0 pool mlp1".split())}
RD = {n: i for i, n in enumerate("ffn0 rec gate wout ffn1 k v ffn2 q wo ffn3 k2 fq2 v2 woe mlp0 pool mlp1".split())}
NORMS = "start ffn0 wout ffn1 ctx ffn2 wo ffn3 woe mlp0 pool".split()
NRM = {n: i for i, n in enumerate(NORMS)}
NORM_BANK = {"ffn3": 0}
PE_SUMS = ["ffn3", "mlp0"]
POOL_SUMS = {n: i for i, n in enumerate(n for n in NORMS if n not in PE_SUMS)}
TS = T + 2
HN = {"k": 0, "q": 1, "q2": 2, "k2": 3}
HNP = {"k": 0, "q": 4, "q2": 8, "k2": 10}
HEAD_BANK = {"k": 0, "q": 4, "q2": 4, "k2": 5}
STEPS = {"ffn0": 0, "ffn1": FFS, "ffn2": 2 * FFS, "ffn3": 3 * FFS, "mlp0": 4 * FFS, "mlp1": 4 * FFS + MLS}


class Signals:

    def __init__(self, sem):
        self.params_in = sem("params_in")
        self.consts_in = sem("consts_in")
        self.mixer_consts_in = sem("mixer_consts_in")
        self.x_in = sem("x_in")
        self.ctx_in = sem("ctx_in")
        self.late_in = sem("late_in")
        self.poolmat_in = sem("poolmat_in")
        self.out_done = sem("out_done")
        self.hi_ready = sem("hi_ready")
        self.lo_ready = sem("lo_ready")
        self.unit_used = sem("unit_used")
        self.operand_hi = sem("operand_hi")
        self.operand_ready = sem("operand_ready")
        self.acc_ready = sem("acc_ready")
        self.acc_read = sem("acc_read")
        self.sq_ready = sem("sq_ready")
        self.pool_sum = sem("pool_sum")
        self.ssq_ready = sem("ssq_ready")
        self.ms_psum = sem("ms_psum")
        self.ms_ready = sem("ms_ready")
        self.root_ready = sem("root_ready")
        self.up_ready = sem("up_ready")
        self.up_scaled = sem("up_scaled")
        self.gated = sem("gated")
        self.relu_done = sem("relu_done")
        self.shift_hi = sem("shift_hi")
        self.shift_lo = sem("shift_lo")
        self.hid_f32 = sem("hid_f32")
        self.hid_hi_ready = sem("hid_hi_ready")
        self.hid_ready = sem("hid_ready")
        self.cond_silu = sem("cond_silu")
        self.cond_hi_ready = sem("cond_hi_ready")
        self.cond_ready = sem("cond_ready")
        self.mod_rows = sem("mod_rows")
        self.mod_copied = sem("mod_copied")
        self.mod_turned = sem("mod_turned")
        self.mod_read = sem("mod_read")
        self.dve_chain = sem("dve_chain")
        self.lam_abs = sem("lam_abs")
        self.lam_exp = sem("lam_exp")
        self.lam_ready = sem("lam_ready")
        self.conv_first = sem("conv_first")
        self.conv_tap = sem("conv_tap")
        self.xc_hi = sem("xc_hi")
        self.xc_lo = sem("xc_lo")
        self.gelu_done = sem("gelu_done")
        self.gates_read = sem("gates_read")
        self.mixed_in = sem("mixed_in")
        self.lru_tanh = sem("lru_tanh")
        self.lru_decay = sem("lru_decay")
        self.lru_m2 = sem("lru_m2")
        self.lru_sqrt = sem("lru_sqrt")
        self.lru_y = sem("lru_y")
        self.head_sq = sem("head_sq")
        self.head_sum = sem("head_sum")
        self.head_ms = sem("head_ms")
        self.head_root = sem("head_root")
        self.head_rs = sem("head_rs")
        self.head_bc = sem("head_bc")
        self.normed = sem("normed")
        self.v_turned = sem("v_turned")
        self.v_out = sem("v_out")
        self.z_ready = sem("z_ready")
        self.z_masked = sem("z_masked")
        self.z_abs = sem("z_abs")
        self.e_ready = sem("e_ready")
        self.l_ready = sem("l_ready")
        self.sp_ready = sem("sp_ready")
        self.cum_ready = sem("cum_ready")
        self.w_arg = sem("w_arg")
        self.w_ready = sem("w_ready")
        self.o_ready = sem("o_ready")
        self.ctx_full = sem("ctx_full")
        self.ctx_hi = sem("ctx_hi")
        self.ctx_lo = sem("ctx_lo")
        self.full_ready = sem("full_ready")
        self.v2_turned = sem("v2_turned")
        self.v2_out = sem("v2_out")
        self.f_turned = sem("f_turned")
        self.f_out = sem("f_out")
        self.dft1 = sem("dft1")
        self.dft1_out = sem("dft1_out")
        self.dft2 = sem("dft2")
        self.mixed_hi = sem("mixed_hi")
        self.mixed_lo = sem("mixed_lo")
        self.dft3 = sem("dft3")
        self.pool_norm = sem("pool_norm")
        self.pool_u = sem("pool_u")
        self.pool_turned = sem("pool_turned")
        self.pool_tok = sem("pool_tok")
        self.pooled = sem("pooled")
        self.pooled_hi = sem("pooled_hi")
        self.pooled_lo = sem("pooled_lo")
        self.tab_ready = sem("tab_ready")
        self.na_z = sem("na_z")
        self.na_s = sem("na_s")
        self.na_max = sem("na_max")
        self.na_e = sem("na_e")
        self.na_p = sem("na_p")
        self.na_t = sem("na_t")
        self.na_tout = sem("na_tout")
        self.na_o = sem("na_o")


def build(nc, stream, x_in, ctx_in, small, consts, late, poolmat, tab, out):
    with ExitStack() as es:
        def sb(name, cols, dt=F32):
            return es.enter_context(nc.sbuf_tensor(name, [P, cols], dt))

        raw = sb("raw", RING * UNIT)
        w_hi = sb("w_hi", RING * UNIT, F32R)
        w_lo = sb("w_lo", RING * UNIT, F32R)
        x_t = sb("x", NC * T)
        u_hi_t = sb("u_hi", NC * 2 * T, F32R)
        u_lo_t = sb("u_lo", NC * 2 * T, F32R)
        hid_hi_t = sb("hid_hi", 2 * 512, F32R)
        hid_lo_t = sb("hid_lo", 2 * 512, F32R)
        cond_t = sb("cond", 4 * NC, F32R)
        rstd = sb("rstd", T)
        nrm = sb("nrm", 1024)
        prm = sb("prm", NSMALL)
        cst = sb("cst", NCONST)
        mod_t = sb("mod", 2 * NMOD * NC * 2)
        tiny = sb("tiny", NC * len(TY))
        buf = [sb(f"buf{n}", 2048) for n in range(5)]
        buf5 = sb("buf5", NC * (T + CONV - 1))
        psum = es.enter_context(nc.psum_tensor("psum", [P, 8, 512], F32))

        x = x_t[:, :].rearrange("p (k t) -> p k t", k=NC)
        u_hi = u_hi_t[:, :].rearrange("p (k t) -> p k t", k=NC)
        u_lo = u_lo_t[:, :].rearrange("p (k t) -> p k t", k=NC)
        u_hif = u_hi_t[:, :].bitcast(F32).rearrange("p (k t) -> p k t", k=NC)
        hid_hi = hid_hi_t[:, :].rearrange("p (s t) -> p s t", s=2)
        hid_lo = hid_lo_t[:, :].rearrange("p (s t) -> p s t", s=2)
        hid_hif = hid_hi_t[:, :].bitcast(F32).rearrange("p (s t) -> p s t", s=2)
        cond = cond_t[:, :].rearrange("p (k c) -> p k c", c=4)
        condf = cond_t[:, :].bitcast(F32).rearrange("p (k c) -> p k c", c=4)
        mod = mod_t[:, :].rearrange("p (l j c) -> p l j c", l=2, c=2)
        pad = buf5[:, :].rearrange("p (k t) -> p k t", k=NC)
        t2, sil, h32 = buf5[:, 0:512], buf5[:, 512:768], buf5[:, 768:1280]
        mod_rows = buf5[0:4, 1280:1792]
        ms, root_t = nrm[:, 0:512], nrm[:, 512:1024]
        head_rs = buf5[:, 1536:2048]
        n_att = 2 * STICK
        z_slots = [buf[3 + n // 2][:, (n % 2) * n_att:(n % 2 + 1) * n_att] for n in range(4)]
        sp_slots = [buf5[:, n * n_att:(n + 1) * n_att] for n in range(2)]
        na_slots = [buf5[:, 0:512], buf5[:, 512:1024], nrm[:, 0:512], nrm[:, 512:1024]]
        NA_BANKS = [0, 1, 6, 7]
        ident, ones, tri = (cst[:, CC[n]:CC[n] + P] for n in ("ident", "ones", "tri"))
        headsum = cst[:, CC["headsum"]:CC["headsum"] + P].rearrange("p (k h) -> p k h", k=NC)
        headbc = cst[0:16, CC["headbc"]:CC["headbc"] + NC * P].rearrange("p (k n) -> p k n", k=NC)
        stick = cst[:, CC["stick"]:CC["stick"] + STICK]
        colmask = cst[:, CC["colmask"]:CC["colmask"] + HD]

        def ck(t, k=NC):
            return t[:, :].rearrange("p (k t) -> p k t", k=k)

        def col(name, k=0, n=1):
            return prm[:, COL[name] + k:COL[name] + k + n]

        def ty(name, k=0, n=1):
            return tiny[:, TY[name] + k:TY[name] + k + n]

        def part(l, n, k=None, c=0):
            if k is None:
                return mod[:, l, NC * n:NC * (n + 1), c]
            return mod[:, l, NC * n + k, c:c + 1]

        def half(b):
            return slice(b * 512, (b + 1) * 512)

        def bank2(b):
            return psum[:, b, :].rearrange("p (k t) -> p k t", k=2)

        def over2(row):
            return row.unsqueeze(1).broadcast_to([P, 2, T])

        def sem(name):
            return es.enter_context(nc.semaphore(name))

        S = Signals(sem)
        raw_landed = [sem(f"raw_landed{n}") for n in range(RING // 2)]
        tab_in = [sem(f"tab_in{n}") for n in range(2)]
        block = es.enter_context(nc.Block())

        @block.sync
        def _(sp):
            sp.dma_start(prm[:, :], small).then_inc(S.params_in, 16)

            def load(pair, src, i=0):
                slot = pair % (RING // 2)
                sp.dma_start(raw[:, 2 * slot * UNIT:2 * (slot + 1) * UNIT], src).then_inc(raw_landed[slot], 16)

            for pair in range(RING // 2):
                load(pair, stream[pair])
                if pair == 0:
                    sp.dma_start(x_t[:, :], x_in).then_inc(S.x_in, 16)
                if pair == 1:
                    sp.dma_start(cst[:, 0:CC["tri"]], consts[:, 0:CC["tri"]]).then_inc(S.consts_in, 16)
            with sp.Fori(1, UNITS // RING) as i:
                for slot in range(RING // 2):
                    sp.wait_ge(S.lo_ready, RING * i + 2 * slot + 2 - RING)
                    load(slot, stream[i * (RING // 2) + slot])
            sp.wait_ge(S.out_done, 4 * 16)

        @block.gpsimd
        def _(pool):
            gp = nc.gpsimd

            def sum_squares(n):
                m = POOL_SUMS[NORMS[n]]
                for b in range(1, 4):
                    pool.wait_ge(S.sq_ready, 4 * n + b + 1)
                    if b > 1:
                        pool.wait_ge(S.pool_sum, 3 * m + b - 1)
                    a = buf[4][:, half(0)]
                    gp.tensor_tensor(a, a, buf[4][:, half(b)], ALU.add).then_inc(S.pool_sum, 1)
                pool.wait_ge(S.pool_sum, 3 * m + 3)
                gp.tensor_tensor(buf[4][:, 0:T], buf[4][:, 0:T], buf[4][:, T:2 * T], ALU.add).then_inc(S.ssq_ready, 1)

            pool.wait_ge(S.hi_ready, 4)
            pool.dma_start(cst[:, CC["tri"]:], consts[:, CC["tri"]:]).then_inc(S.mixer_consts_in, 16)
            for n, name in enumerate(NORMS):
                if name == "ctx":
                    pool.dma_start(buf[3][:, :], ctx_in).then_inc(S.ctx_in, 16)
                if name == "woe":
                    pool.wait_ge(S.acc_ready, 4 * ACC["ffn3"] + 4)
                    pool.dma_start(buf5[:, 0:NLATE], late).then_inc(S.late_in, 16)
                    pool.wait_ge(S.v2_turned, 4)
                    pool.dma_start(buf[2][:, 0:TABW], tab[0]).then_inc(tab_in[0], 16)
                    pool.wait_ge(S.mixed_lo, 4)
                    pool.dma_start(buf[4][:, 0:TABW], tab[1]).then_inc(tab_in[1], 16)
                if name == "mlp0":
                    pool.wait_ge(S.na_s, 16)
                    pool.dma_start(buf[2][:, :], poolmat).then_inc(S.poolmat_in, 16)
                if name not in PE_SUMS:
                    sum_squares(n)

        @block.scalar
        def _(act):
            sc = nc.scalar
            nxt = [0]

            def split_hi(c, i=0):
                slot = c % RING
                act.wait_ge(raw_landed[slot // 2], 16 * (c // RING + 1 + i))
                if c >= RING or not isinstance(i, int):
                    act.wait_ge(S.unit_used, RING * i + c - RING + 2)
                u = slice(slot * UNIT, (slot + 1) * UNIT)
                sc.activation(w_hi[:, u], raw[:, u], ACT.Copy).then_inc(S.hi_ready, 1)

            def pump_to(last):
                while nxt[0] <= min(last, UNITS - 1):
                    split_hi(nxt[0])
                    nxt[0] += 1

            def x_updated(name, b):
                if name == "start":
                    act.wait_ge(S.x_in, 16)
                    act.wait_ge(S.params_in, 16)
                else:
                    act.wait_ge(S.acc_read, 4 * RD[name] + b + 1)

            def square(n, src, b):
                if b == 0 and n:
                    act.wait_ge(S.ms_psum, n)
                sc.activation(buf[4][:, half(b)], src[:, half(b)], ACT.Square).then_inc(S.sq_ready, 1)

            def root(n):
                act.wait_ge(S.ms_ready, n + 1)
                sc.activation(root_t[:, 0:T], ms[:, 0:T], ACT.Sqrt).then_inc(S.root_ready, 1)

            def gain_operand(gain, name, norm=True, early=0):
                for b in range(4):
                    x_updated(name, b)
                    for k in (2 * b, 2 * b + 1):
                        sc.activation(u_hi[:, k, 0:T], x[:, k, :], ACT.Identity, scale=col(gain, k))\
                          .then_inc(S.operand_hi, 1)
                    if norm:
                        square(NRM[name], x_t, b)
                pump_to(early - 1)
                if norm:
                    root(NRM[name])

            def norm_only(name, early=0):
                for b in range(4):
                    x_updated(name, b)
                    square(NRM[name], x_t, b)
                pump_to(early - 1)
                root(NRM[name])

            def normed_operand(n, shift):
                for k in range(NC):
                    act.wait_ge(S.full_ready, NC * n + k + 1)
                    sc.activation(u_hi[:, k, 0:T], ck(buf[3])[:, k, :], ACT.Identity, bias=shift(k))\
                      .then_inc(S.operand_hi, 1)

            def swiglu(name):
                c0, h0, g0 = AT[name], STEPS[name], MODG * int(name[3])

                def copy_rows(g):
                    act.wait_ge(S.mod_rows, g + 1)
                    if not isinstance(g, int) or g:
                        act.wait_ge(S.mod_turned, g)
                    sc.activation(mod_rows, psum[0:4, 6, :], ACT.Copy).then_inc(S.mod_copied, 1)

                def hidden(j, par, c, i=0, n_units=4, rows=None):
                    act.wait_ge(S.up_scaled, h0 + j + 1)
                    sc.activation(sil, t2[:, 0:T], ACT.Silu).then_inc(S.gated, 1)
                    act.wait_ge(S.hid_f32, h0 + j + 1)
                    sc.activation(hid_hi[:, par, 0:T], h32[:, 0:T], ACT.Copy).then_inc(S.hid_hi_ready, 1)
                    if rows is not None:
                        copy_rows(rows)
                    for n in range(n_units):
                        split_hi(c + n, i)

                pump_to(c0 + 7)
                with act.Fori(0, (FFS - 2) // 4) as i:
                    for s in range(4):
                        hidden(4 * i + s, s % 2, c0 + 8 + 4 * s, 2 * i, rows=g0 + i if s == 1 else None)
                hidden(FFS - 2, 0, c0 + FFU - 2)
                nxt[0] = c0 + FFU + 2
                pump_to(c0 + FFU + 3)
                hidden(FFS - 1, 1, None, n_units=0, rows=g0 + MODG - 1)

            def shift_operand(l):
                sc.activation(u_hi[:, :, T:TS], part(l, 3).unsqueeze(2).broadcast_to([P, NC, 2]), ACT.Copy)\
                  .then_inc(S.shift_hi, 1)

            def mlp_operand(name, gain, b):
                x_updated(name, b)
                for k in (2 * b, 2 * b + 1):
                    sc.activation(u_hi[:, k, 0:T], x[:, k, :], ACT.Identity, scale=ty(gain, k)).then_inc(S.operand_hi, 1)
                square(NRM[name], x_t, b)

            def sqrelu(name):
                c0, h0 = AT[name], STEPS[name]
                assert nxt[0] == c0 + AHEAD + 2
                last = min(c0 + 4 * MLS - 2 + AHEAD, UNITS)

                def split(c, i):
                    if not isinstance(i, int) or c < last:
                        split_hi(c, i)

                def hidden(j, par, c, i=0):
                    act.wait_ge(S.up_scaled, h0 + j + 1)
                    for n in range(2):
                        h = t2[:, n * T:(n + 1) * T]
                        ins = sc.activation(h, h, ACT.Relu, bias=ty("s", n))
                    ins.then_inc(S.relu_done, 1)
                    act.wait_ge(S.hid_f32, h0 + j + 1)
                    sc.activation(hid_hi[:, par, :], h32, ACT.Copy).then_inc(S.hid_hi_ready, 1)
                    for n in range(4):
                        split(c + n, i)

                with act.Fori(0, (MLS - 2) // 2) as i:
                    for s in range(2):
                        hidden(2 * i + s, s, c0 + 2 + 4 * s + AHEAD, i)
                hidden(MLS - 2, 0, c0 + 4 * MLS - 6 + AHEAD)
                hidden(MLS - 1, 1, c0 + 4 * MLS - 2 + AHEAD)
                nxt[0] = last

            def head_norm(name, t, pieces, w):
                for b in range(pieces):
                    act.wait_ge(S.acc_read, 4 * RD["fq2" if name == "q2" else name] + b + 1 + (2 if name == "q2" else 0))
                    sc.activation(buf[4][:, half(b)], t[:, half(b)], ACT.Square).then_inc(S.head_sq, 1)

            def head_root(name, w):
                act.wait_ge(S.head_ms, HN[name] + 1)
                sc.activation(root_t[0:16, 0:w], ms[0:16, 0:w], ACT.Sqrt).then_inc(S.head_root, 1)

            act.wait_ge(S.params_in, 16)
            sc.activation(ty("cond", n=16), col("cond", n=16), ACT.Silu).then_inc(S.cond_silu, 1)
            act.wait_ge(S.cond_silu, 1)
            sc.activation(cond[:, :, 0:2], ty("cond", n=16).rearrange("p (k c) -> p k c", c=2), ACT.Copy).then_inc(S.cond_hi_ready, 1)
            act.wait_ge(S.lam_abs, 1)
            sc.activation(ty("e", n=NC), ty("negabs", n=NC), ACT.Exp).then_inc(S.lam_exp, 1)
            pump_to(1)
            for b in range(4):
                x_updated("start", b)
                for k in (2 * b, 2 * b + 1):
                    sc.activation(u_hi[:, k, 0:T], x[:, k, :], ACT.Identity, scale=col("ffn1_0", k))\
                      .then_inc(S.operand_hi, 1)
                square(0, x_t, b)
                if b == 1:
                    pump_to(3)
            pump_to(AHEAD + 1)
            root(0)
            swiglu("ffn0")

            gain_operand("mix_0", "ffn0", early=AT["rec"] + AHEAD)
            pump_to(AT["rec"] + 7 + 3)
            xc = ck(buf[0])
            for b in range(4):
                act.wait_ge(S.acc_read, 4 * RD["rec"] + b + 1)
                for k in (2 * b, 2 * b + 1):
                    sc.activation(xc[:, k, :], pad[:, k, 0:T], ACT.Identity, bias=col("cb", k), scale=col("cw0", k))\
                      .then_inc(S.conv_first, 1)
            pump_to(AT["gate"] + 5)
            for b in range(4):
                act.wait_ge(S.conv_tap, 2 * (CONV - 1) * (b + 1))
                sc.activation(u_hi[:, 2 * b:2 * b + 2, T:2 * T], xc[:, 2 * b:2 * b + 2, :], ACT.Copy)\
                  .then_inc(S.xc_hi, 1)
                pump_to(AT["gate"] + 5 + b)
            pump_to(AT["wout"] - 1)
            r, ig, tn = ck(buf[2]), ck(buf[3]), ck(buf[4])

            def gate_sigmoid(dst, bias, name):
                for k in range(NC):
                    act.wait_ge(S.acc_ready, 4 * ACC[name] + k // 2 + 1)
                    sc.activation(dst[:, k, :], bank2(k // 2)[:, k % 2, :], ACT.Sigmoid, bias=col(bias, k))\
                      .then_inc(S.gates_read, 1)

            gate_sigmoid(r, "br", "r")
            act.wait_ge(S.lam_ready, 2)
            act.wait_ge(S.ms_psum, NRM["ffn0"] + 1)
            act.wait_ge(S.gates_read, NC)
            for k in range(NC):
                sc.activation(tn[:, k, :], r[:, k, :], ACT.Tanh, scale=ty("sp8", k)).then_inc(S.lru_tanh, 1)
            pump_to(AT["wout"] + 1)
            gate_sigmoid(ig, "bi", "i")
            act.wait_ge(S.lru_tanh, NC)
            for k in range(NC):
                sc.activation(r[:, k, :], r[:, k, :], ACT.Exp, scale=ty("nsp8", k)).then_inc(S.lru_decay, 1)

            def mult_root(b):
                act.wait_ge(S.lru_m2, b + 1)
                sc.activation(buf[4][:, half(b)], buf[4][:, half(b)], ACT.Sqrt).then_inc(S.lru_sqrt, 1)

            def gelu(b):
                act.wait_ge(S.acc_read, 4 * RD["gate"] + b + 1)
                sc.activation(buf[1][:, half(b)], buf[1][:, half(b)], ACT.Gelu_apprx_tanh).then_inc(S.gelu_done, 1)

            def y_hi(b):
                act.wait_ge(S.lru_y, b + 1)
                sc.activation(u_hi[:, 2 * b:2 * b + 2, 0:T], ck(buf[1])[:, 2 * b:2 * b + 2, :], ACT.Copy)\
                  .then_inc(S.operand_hi, 2)

            mult_root(0)
            mult_root(1)
            gelu(0)
            gelu(1)
            y_hi(0)
            mult_root(2)
            mult_root(3)
            pump_to(AT["wout"] + 3)
            y_hi(1)
            gelu(2)
            gelu(3)
            pump_to(AT["wout"] + 5)
            y_hi(2)
            y_hi(3)
            pump_to(AT["ffn1"] + AHEAD - 1)
            gain_operand("ffn2_0", "wout", early=AT["ffn1"] + 8)
            swiglu("ffn1")

            gain_operand("kv", "ffn1", early=AT["k"] + AHEAD)
            pump_to(AT["v"] + 4)
            act.wait_ge(S.ms_psum, NRM["ffn1"] + 1)
            head_norm("k", buf[1], 4, T)
            head_root("k", T)
            pump_to(AT["ffn2"] + AHEAD - 1)
            act.wait_ge(S.acc_ready, 4 * ACC["v"] + 4)
            gain_operand("ffn1_1", "ffn1", norm=False)
            act.wait_ge(S.ctx_in, 16)
            act.wait_ge(S.head_sum, HN["k"] + 1)
            for b in range(4):
                square(NRM["ctx"], buf[3], b)
            pump_to(AT["ffn2"] + 7)
            act.wait_ge(S.ms_ready, NRM["ctx"] + 1)
            sc.activation(root_t[:, T:2 * T], ms[:, T:2 * T], ACT.Sqrt).then_inc(S.root_ready, 1)
            swiglu("ffn2")

            gain_operand("mix_1", "ffn2", early=AT["q"] + AHEAD)
            pump_to(AT["q"] + 7)
            for k in range(NC):
                act.wait_ge(S.ctx_full, k + 1)
                sc.activation(u_hi[:, k, T:2 * T], ck(buf[3])[:, k, :], ACT.Identity, bias=part(0, 0, k, 1))\
                  .then_inc(S.ctx_hi, 1)
            pump_to(AT["q"] + 7 + 3)
            act.wait_ge(S.ms_psum, NRM["ffn2"] + 1)
            head_norm("q", buf[0], 4, T)
            head_root("q", T)
            pump_to(AT["wo"] + 4)

            def decay_terms(g):
                act.wait_ge(S.z_masked, g + 1)
                if g >= 2:
                    act.wait_ge(S.cum_ready, g - 1)
                d = sp_slots[g % 2]
                sc.activation(d, z_slots[g % 4], ACT.Abs).then_inc(S.z_abs, 1)
                act.wait_ge(S.z_abs, g + 1)
                sc.activation(d, d, ACT.Exp, scale=-1.0).then_inc(S.e_ready, 1)
                act.wait_ge(S.e_ready, g + 1)
                sc.activation(d, d, ACT.Ln, bias=1.0).then_inc(S.l_ready, 1)

            sc.preload_act_table_set("natural_log_exp_and_others")
            decay_terms(0)
            for g in range(NC + 1):
                if g:
                    act.wait_ge(S.w_arg, g)
                    z = z_slots[(g - 1) % 4]
                    sc.activation(z, z, ACT.Exp).then_inc(S.w_ready, 1)
                if g + 1 < NC:
                    decay_terms(g + 1)
                if g:
                    act.wait_ge(S.o_ready, g)
                    sc.activation(u_hi[:, g - 1, 0:T], psum[:, 4 + 2 * ((g - 1) % 2), 0:T], ACT.Copy)\
                      .then_inc(S.operand_hi, 1)
            pump_to(AT["ffn3"] + AHEAD - 1)
            gain_operand("ffn2_1", "wo", early=AT["ffn3"] + 8)
            swiglu("ffn3")

            norm_only("ffn3", early=AT["k2"] + AHEAD)
            normed_operand(0, lambda k: part(0, 0, k))
            pump_to(AT["v2"] + 2)
            act.wait_ge(S.ms_psum, NRM["ffn3"] + 1)
            head_norm("q2", buf[0][:, 1024:2048], 2, T)
            pump_to(AT["v2"] + 3)
            head_root("q2", T)
            act.wait_ge(S.head_sum, HN["q2"] + 1)
            head_norm("k2", buf[1], 4, 512)
            head_root("k2", 512)
            for qt in range(2):
                act.wait_ge(S.f_turned, qt + 1)
                if qt == 0:
                    act.wait_ge(S.head_sum, HN["k2"] + 1)
                sc.activation(buf[4][:, half(qt)], psum[:, 6 + qt, :], ACT.Copy).then_inc(S.f_out, 1)
            for kt in range(4):
                act.wait_ge(S.v2_turned, kt + 1)
                sc.activation(buf[3][:, half(kt)], psum[:, kt, :], ACT.Copy).then_inc(S.v2_out, 1)
            pump_to(AT["four"] + 1)
            for g in range(4):
                act.wait_ge(S.dft1, g + 1)
                if g >= 2:
                    act.wait_ge(S.dft2, g - 1)
                elif g == 0:
                    act.wait_ge(S.head_sum, HN["k2"] + 1)
                sc.activation(buf[4][:, 1024 + (g % 2) * 512:1536 + (g % 2) * 512], psum[:, 4 + g % 2, :], ACT.Copy)\
                  .then_inc(S.dft1_out, 1)
                act.wait_ge(S.dft2, g + 1)
                if g >= 2:
                    act.wait_ge(S.dft3, g - 1)
                sc.activation(hid_hi[:, g % 2, 0:T], psum[:, 6, 0:T], ACT.Copy).then_inc(S.mixed_hi, 1)
                act.wait_ge(S.dft3, g + 1)
                sc.activation(u_hi[:, g, 0:T], psum[:, 7, 0:T], ACT.Copy).then_inc(S.operand_hi, 1)
            pt = [buf[0][:, 0:1024], buf5[:, 1024:2048]]

            def na_exp(n):
                act.wait_ge(S.na_max, n + 1)
                e = na_slots[n % 4]
                sc.activation(e, e, ACT.Exp, bias=ty("na", 4 * (n % 4) + 1), accum_out=ty("na", 4 * (n % 4) + 2))\
                  .then_inc(S.na_e, 1)

            def na_turn(n):
                h, qt = n // 2, n % 2
                act.wait_ge(S.na_t, n + 1)
                if h >= 2:
                    act.wait_ge(S.na_o, h - 1)
                dst = pt[h % 2].rearrange("p (k q) -> p k q", k=4)[:, :, qt * P:(qt + 1) * P]
                sc.activation(dst, psum[:, 2 + qt, :].rearrange("p (k q) -> p k q", k=4), ACT.Copy)\
                  .then_inc(S.na_tout, 1)

            def na_hi(m):
                act.wait_ge(S.na_o, 2 * m + 2)
                sc.activation(u_hi[:, 4 + m, 0:T], psum[:, 4 + m % 2, 0:T], ACT.Copy).then_inc(S.operand_hi, 1)

            na_exp(0)
            for n in range(16):
                if n < 15:
                    na_exp(n + 1)
                na_turn(n)
                if n < 5:
                    pump_to(AT["woe"] + n)
                if n % 4 == 0 and n:
                    na_hi(n // 4 - 1)
            na_hi(3)
            pump_to(AT["mlp0"] + AHEAD - 1)
            shift_operand(0)
            for b in range(4):
                mlp_operand("woe", "G2", b)
            pump_to(AT["mlp0"] + AHEAD + 1)
            root(NRM["woe"])
            sqrelu("mlp0")

            norm_only("mlp0")
            shift_operand(1)
            v = ck(buf[3])
            for step in range(7):
                if step < 4:
                    for k in (2 * step, 2 * step + 1):
                        act.wait_ge(S.pool_norm, k + 1)
                        sc.activation(v[:, k, :], v[:, k, :], ACT.Identity, bias=part(1, 0, k)).then_inc(S.pool_u, 1)
                if 1 <= step < 5:
                    g = step - 1
                    act.wait_ge(S.pool_turned, g + 1)
                    sc.activation(buf[1][:, half(g)], psum[:, 4 + g, :], ACT.Copy).then_inc(S.pool_tok, 1)
                if 2 <= step < 6:
                    g = step - 2
                    act.wait_ge(S.pooled, g + 1)
                    sc.activation(u_hi[:, 2 * g:2 * g + 2, 0:T], bank2(4 + g), ACT.Copy).then_inc(S.pooled_hi, 1)
                if step >= 3:
                    mlp_operand("pool", "H2", step - 3)
                    pump_to(AT["mlp1"] + min(step + 1, 5))
            pump_to(AT["mlp1"] + AHEAD + 1)
            root(NRM["pool"])
            sqrelu("mlp1")
            for b in range(4):
                act.wait_ge(S.acc_read, 4 * RD["mlp1"] + b + 1)
                act.dma_start(out[:, half(b)], x_t[:, half(b)]).then_inc(S.out_done, 16)

        @block.vector
        def _(dve):
            ve = nc.vector
            nxt = [0]
            chain = [0]

            def link(ins):
                chain[0] += 1
                ins.then_inc(S.dve_chain, 1)
                dve.wait_ge(S.dve_chain, chain[0])

            def split_lo(c, i=0):
                dve.wait_ge(S.hi_ready, RING * i + c + 1)
                u = slice((c % RING) * UNIT, (c % RING + 1) * UNIT)
                ve.tensor_tensor(w_lo[:, u], raw[:, u], w_hi[:, u].bitcast(F32), ALU.subtract).then_inc(S.lo_ready, 1)

            def pump_to(last):
                while nxt[0] <= min(last, UNITS - 1):
                    split_lo(nxt[0])
                    nxt[0] += 1

            def acc_ready(name, b):
                dve.wait_ge(S.acc_ready, 4 * ACC[name] + b + 1)

            def inverse_root(m, r, y):
                link(ve.reciprocal(y, r))
                link(ve.scalar_tensor_tensor(r, y, -0.5, m, ALU.mult, ALU.mult))
                link(ve.tensor_tensor(r, r, y, ALU.mult))
                return ve.scalar_tensor_tensor(y, r, 1.5, y, ALU.add, ALU.mult)

            def rms(name):
                n = NRM[name]
                dve.wait_ge(S.ms_psum, n + 1)
                ve.tensor_scalar(ms[:, 0:T], psum[:, NORM_BANK.get(name, 7), 0:T], 1.0 / D, EPS, ALU.mult, ALU.add)\
                  .then_inc(S.ms_ready, 1)
                dve.wait_ge(S.root_ready, n + 1)
                link(inverse_root(ms[:, 0:T], root_t[:, 0:T], rstd[:, :]))

            def update_x(name, coef=None, banks=range(4)):
                for b in banks:
                    acc_ready(name, b)
                    if coef is None or isinstance(coef, float):
                        ins = ve.scalar_tensor_tensor(x_t[:, half(b)], psum[:, b, :], coef or 1.0, x_t[:, half(b)],
                                                      ALU.mult, ALU.add)
                    else:
                        for k in (2 * b, 2 * b + 1):
                            ins = ve.scalar_tensor_tensor(x[:, k, :], bank2(b)[:, k % 2, :], coef(k), x[:, k, :],
                                                          ALU.mult, ALU.add)
                    ins.then_inc(S.acc_read, 1)

            def gain_operand_lo(op, gain, first=0, end=NC):
                for k in range(first, end):
                    dve.wait_ge(S.operand_hi, NC * OPS[op] + k + 1)
                    ve.scalar_tensor_tensor(u_lo[:, k, 0:T], x[:, k, :], col(gain, k), u_hif[:, k, 0:T],
                                            ALU.mult, ALU.subtract).then_inc(S.operand_ready, 1)

            def update_and_operand(name, op, gain, coef):
                for b in range(5):
                    if b < 4:
                        acc_ready(name, b)
                        ve.scalar_tensor_tensor(x_t[:, half(b)], psum[:, b, :], coef, x_t[:, half(b)],
                                                ALU.mult, ALU.add).then_inc(S.acc_read, 1)
                    if b:
                        for k in (2 * b - 2, 2 * b - 1):
                            dve.wait_ge(S.operand_hi, NC * OPS[op] + k + 1)
                            ve.scalar_tensor_tensor(u_lo[:, k, 0:T], x[:, k, :], col(gain, k), u_hif[:, k, 0:T],
                                                    ALU.mult, ALU.subtract).then_inc(S.operand_ready, 1)

            def shift_operand(l):
                dve.wait_ge(S.shift_hi, l + 1)
                ve.tensor_tensor(u_lo[:, :, T:TS], part(l, 3).unsqueeze(2).broadcast_to([P, NC, 2]),
                                 u_hif[:, :, T:TS], ALU.subtract).then_inc(S.shift_lo, 1)

            def mlp_operand(op, gain, b):
                for k in (2 * b, 2 * b + 1):
                    dve.wait_ge(S.operand_hi, NC * OPS[op] + k + 1)
                    ve.scalar_tensor_tensor(u_lo[:, k, 0:T], x[:, k, :], ty(gain, k), u_hif[:, k, 0:T],
                                            ALU.mult, ALU.subtract).then_inc(S.operand_ready, 1)

            def normed_operand(op, gain, shift):
                v = ck(buf[3])
                for b in range(5):
                    if b < 4:
                        for k in (2 * b, 2 * b + 1):
                            ve.scalar_tensor_tensor(v[:, k, :], x[:, k, :], gain(k), rstd[:, :], ALU.mult, ALU.mult)\
                              .then_inc(S.full_ready, 1)
                    if b:
                        for k in (2 * b - 2, 2 * b - 1):
                            dve.wait_ge(S.operand_hi, NC * OPS[op] + k + 1)
                            ve.scalar_tensor_tensor(u_lo[:, k, 0:T], v[:, k, :], shift(k), u_hif[:, k, 0:T],
                                                    ALU.add, ALU.subtract).then_inc(S.operand_ready, 1)

            def swiglu(name):
                c0, h0, g0 = AT[name], STEPS[name], MODG * int(name[3])
                l, j0 = int(name[3]) // 2, 4 * MODG * (int(name[3]) % 2)

                def hidden(j, par, c, i=0, n_units=4):
                    dve.wait_ge(S.up_ready, h0 + j + 1)
                    ve.tensor_tensor(t2.rearrange("p (k t) -> p k t", k=2), bank2(4 + par), over2(rstd[:, :]),
                                     ALU.mult).then_inc(S.up_scaled, 1)
                    dve.wait_ge(S.gated, h0 + j + 1)
                    ve.tensor_tensor(h32[:, 0:T], sil, t2[:, T:2 * T], ALU.mult).then_inc(S.hid_f32, 1)
                    dve.wait_ge(S.hid_hi_ready, h0 + j + 1)
                    ve.tensor_tensor(hid_lo[:, par, 0:T], h32[:, 0:T], hid_hif[:, par, 0:T], ALU.subtract)\
                      .then_inc(S.hid_ready, 1)
                    for n in range(n_units):
                        split_lo(c + n, i)

                pump_to(c0 + 7)
                with dve.Fori(0, (FFS - 2) // 4) as i:
                    for s in range(4):
                        hidden(4 * i + s, s % 2, c0 + 8 + 4 * s, 2 * i)
                        if s == 2:
                            modulation(l, j0 + 4 * i, g0 + i)
                hidden(FFS - 2, 0, c0 + FFU - 2)
                nxt[0] = c0 + FFU + 2
                pump_to(c0 + FFU + 3)
                hidden(FFS - 1, 1, None, n_units=0)

            def last_modulation(f):
                modulation(f // 2, 4 * MODG * (f % 2) + 4 * MODG - 4, MODG * (f + 1) - 1)

            def modulation(l, j, g):
                dve.wait_ge(S.mod_turned, g + 1)
                where = bass.ds(j, 4) if not isinstance(j, int) else slice(j, j + 4)
                ve.tensor_reduce(mod[:, l, where, :], psum[:, 7, 0:16].rearrange("p (m t c) -> p m c t", m=4, t=2),
                                 AX_X, ALU.add).then_inc(S.mod_read, 1)

            def modulation_bias(l):
                dve.wait_ge(S.mod_read, 2 * MODG * (l + 1))
                bias = prm[:, COL["bmod"] + 48 * l:COL["bmod"] + 48 * (l + 1)].unsqueeze(2).broadcast_to([P, 48, 2])
                link(ve.tensor_tensor(mod[:, l, :, :], mod[:, l, :, :], bias, ALU.add))

            def scale_gain(dst, l, n, gain, c=0):
                link(ve.scalar_tensor_tensor(ty(dst, n=NC), part(l, n, c=c), 1.0, col(gain, n=NC), ALU.add, ALU.mult))

            def sqrelu(name):
                c0, h0 = AT[name], STEPS[name]
                assert nxt[0] == c0 + AHEAD + 2

                def hidden(j, par, c, i=0):
                    dve.wait_ge(S.up_ready, h0 + j + 1)
                    ve.tensor_copy(ty("s", n=2).unsqueeze(2), psum[:, 4 + 2 * par:6 + 2 * par, T:T + 1])
                    ve.tensor_tensor(t2.rearrange("p (k t) -> p k t", k=2), psum[:, 4 + 2 * par:6 + 2 * par, 0:T],
                                     over2(rstd[:, :]), ALU.mult).then_inc(S.up_scaled, 1)
                    dve.wait_ge(S.relu_done, h0 - STEPS["mlp0"] + j + 1)
                    ve.tensor_tensor(h32, t2, t2, ALU.mult).then_inc(S.hid_f32, 1)
                    dve.wait_ge(S.hid_hi_ready, h0 + j + 1)
                    ve.tensor_tensor(hid_lo[:, par, :], h32, hid_hif[:, par, :], ALU.subtract).then_inc(S.hid_ready, 1)
                    for n in range(4):
                        split(c + n, i)

                last = min(c0 + 4 * MLS - 2 + AHEAD, UNITS)

                def split(c, i):
                    if not isinstance(i, int) or c < last:
                        split_lo(c, i)

                with dve.Fori(0, (MLS - 2) // 2) as i:
                    for s in range(2):
                        hidden(2 * i + s, s, c0 + 2 + 4 * s + AHEAD, i)
                hidden(MLS - 2, 0, c0 + 4 * MLS - 6 + AHEAD)
                hidden(MLS - 1, 1, c0 + 4 * MLS - 2 + AHEAD)
                nxt[0] = last

            def head_norm(name, t, chunks, w, gain, b0, between=lambda: None):
                n = HN[name]
                dve.wait_ge(S.head_sum, n + 1)
                ve.tensor_scalar(ms[0:16, 0:w], psum[0:16, HEAD_BANK[name], 0:w], 1.0 / HD, EPS, ALU.mult, ALU.add)\
                  .then_inc(S.head_ms, 1)
                dve.wait_ge(S.head_root, n + 1)
                inverse_root(ms[0:16, 0:w], root_t[0:16, 0:w], head_rs[0:16, 0:w]).then_inc(S.head_rs, 1)
                between()
                for b in range(chunks * w // 512):
                    dve.wait_ge(S.head_bc, HNP[name] + b + 1)
                    ve.scalar_tensor_tensor(t[:, half(b)], t[:, half(b)], col(gain), psum[:, b0 + b, :],
                                            ALU.mult, ALU.mult).then_inc(S.normed, 1)

            dve.wait_ge(S.cond_hi_ready, 1)
            ve.tensor_tensor(cond[:, :, 2:4], ty("cond", n=16).rearrange("p (k c) -> p k c", c=2), condf[:, :, 0:2],
                             ALU.subtract)\
              .then_inc(S.cond_ready, 1)
            link(ve.tensor_scalar(ty("relu", n=NC), col("lam", n=NC), -1.0, 0.0, ALU.mult, ALU.max))
            link(ve.tensor_scalar(ty("q", n=NC), col("lam", n=NC), 0.0, None, ALU.max))
            link(ve.tensor_tensor(ty("negabs", n=NC), ty("relu", n=NC), ty("q", n=NC), ALU.add))
            ve.tensor_scalar(ty("negabs", n=NC), ty("negabs", n=NC), -1.0, None, ALU.mult).then_inc(S.lam_abs, 1)

            pump_to(1)
            gain_operand_lo("ffn0", "ffn1_0", 0, 4)
            pump_to(3)
            gain_operand_lo("ffn0", "ffn1_0", 4)
            pump_to(AHEAD + 1)
            rms("start")
            swiglu("ffn0")

            update_and_operand("ffn0", "mix0", "mix_0", 0.5)
            last_modulation(0)
            link(ve.memset(pad[:, :, 0:CONV - 1], 0.0))
            pump_to(AT["rec"] + AHEAD - 1)
            rms("ffn0")
            pump_to(AT["rec"] + 7 + 3)
            dve.wait_ge(S.lam_exp, 1)
            e, den, q, q2, poly = (ty(n, n=NC) for n in ("e", "den", "q", "q2", "poly"))
            link(ve.tensor_scalar(den, e, 2.0, None, ALU.add))
            link(ve.reciprocal(den, den))
            link(ve.tensor_tensor(q, e, den, ALU.mult))
            link(ve.tensor_tensor(q2, q, q, ALU.mult))
            link(ve.tensor_scalar(poly, q2, 1.0 / 15, None, ALU.mult))
            for m in (13, 11, 9, 7, 5, 3):
                link(ve.scalar_tensor_tensor(poly, poly, 1.0 / m, q2, ALU.add, ALU.mult))
            link(ve.scalar_tensor_tensor(poly, poly, 1.0, q, ALU.add, ALU.mult))
            link(ve.scalar_tensor_tensor(poly, poly, 2.0, ty("relu", n=NC), ALU.mult, ALU.add))
            ve.tensor_scalar(ty("sp8", n=NC), poly, 8.0, None, ALU.mult).then_inc(S.lam_ready, 1)
            ve.tensor_scalar(ty("nsp8", n=NC), poly, -8.0, None, ALU.mult).then_inc(S.lam_ready, 1)
            for b in range(4):
                acc_ready("rec", b)
                ve.tensor_tensor(pad[:, 2 * b:2 * b + 2, CONV - 1:], bank2(b), over2(rstd[:, :]), ALU.mult)\
                  .then_inc(S.acc_read, 1)
            pump_to(AT["gate"] + 3)
            xc = ck(buf[0])

            def xc_lo(b):
                dve.wait_ge(S.xc_hi, b + 1)
                ve.tensor_tensor(u_lo[:, 2 * b:2 * b + 2, T:2 * T], xc[:, 2 * b:2 * b + 2, :],
                                 u_hif[:, 2 * b:2 * b + 2, T:2 * T], ALU.subtract).then_inc(S.xc_lo, 1)

            for b in range(4):
                base = 2 * (CONV - 1) * b
                for tap in range(1, CONV):
                    for kk in range(2):
                        if tap == 1:
                            dve.wait_ge(S.conv_first, 2 * b + kk + 1)
                        else:
                            dve.wait_ge(S.conv_tap, base + 2 * (tap - 2) + kk + 1)
                        k = 2 * b + kk
                        ve.scalar_tensor_tensor(xc[:, k, :], pad[:, k, tap:tap + T], col(f"cw{tap}", k), xc[:, k, :],
                                                ALU.mult, ALU.add).then_inc(S.conv_tap, 1)
                if b:
                    xc_lo(b - 1)
                pump_to(AT["gate"] + 4 + b)
            xc_lo(3)
            pump_to(AT["wout"] + 1)
            for b in range(4):
                dve.wait_ge(S.gates_read, NC + 2 * b + 2)
                ve.tensor_tensor(buf[3][:, half(b)], buf[3][:, half(b)], buf[0][:, half(b)], ALU.mult)\
                  .then_inc(S.mixed_in, 1)

            def mult_square(b):
                dve.wait_ge(S.lru_decay, 2 * b + 2)
                dve.wait_ge(S.mixed_in, b + 1)
                link(ve.tensor_tensor(buf[0][:, half(b)], buf[2][:, half(b)], buf[2][:, half(b)], ALU.mult))
                ve.scalar_tensor_tensor(buf[4][:, half(b)], buf[0][:, half(b)], 1.0, buf[4][:, half(b)],
                                        ALU.add, ALU.mult).then_inc(S.lru_m2, 1)

            def read_gate(b):
                acc_ready("gate", b)
                ve.tensor_tensor(ck(buf[1])[:, 2 * b:2 * b + 2, :], bank2(4 + b), over2(rstd[:, :]), ALU.mult)\
                  .then_inc(S.acc_read, 1)

            a, hs = ck(buf[2]), ck(buf[0])

            def recur(b):
                dve.wait_ge(S.lru_sqrt, b + 1)
                link(ve.tensor_tensor(buf[3][:, half(b)], buf[3][:, half(b)], buf[4][:, half(b)], ALU.mult))
                for k in (2 * b, 2 * b + 1):
                    ins = ve.tensor_tensor_scan(hs[:, k, :], a[:, k, :], ck(buf[3])[:, k, :], 0.0, ALU.mult, ALU.add)
                link(ins)

            def y_full(b):
                dve.wait_ge(S.gelu_done, b + 1)
                ve.tensor_tensor(buf[1][:, half(b)], buf[0][:, half(b)], buf[1][:, half(b)], ALU.mult)\
                  .then_inc(S.lru_y, 1)

            def y_lo(b):
                dve.wait_ge(S.operand_hi, NC * OPS["y"] + 2 * b + 2)
                ve.tensor_tensor(u_lo[:, 2 * b:2 * b + 2, 0:T], ck(buf[1])[:, 2 * b:2 * b + 2, :],
                                 u_hif[:, 2 * b:2 * b + 2, 0:T], ALU.subtract).then_inc(S.operand_ready, 2)

            for b in range(2):
                mult_square(b)
                read_gate(b)
            recur(0)
            mult_square(2)
            y_full(0)
            mult_square(3)
            y_lo(0)
            recur(1)
            y_full(1)
            read_gate(2)
            read_gate(3)
            y_lo(1)
            pump_to(AT["wout"] + 3)
            recur(2)
            y_full(2)
            pump_to(AT["wout"] + 5)
            recur(3)
            y_lo(2)
            y_full(3)
            y_lo(3)
            pump_to(AT["ffn1"] + AHEAD - 1)
            update_and_operand("wout", "ffn1", "ffn2_0", 1.0)
            pump_to(AT["ffn1"] + 7)
            rms("wout")
            swiglu("ffn1")

            update_and_operand("ffn1", "kv", "kv", 0.5)
            last_modulation(1)
            modulation_bias(0)
            pump_to(AT["k"] + AHEAD - 1)
            rms("ffn1")
            for dst, n, gain, c in (("G1", 1, "n1_0", 0), ("Gc", 1, "n1_0", 1), ("G2", 4, "n2_0", 0)):
                scale_gain(dst, 0, n, gain, c)
            pump_to(AT["v"] + 4)
            for b in range(4):
                acc_ready("k", b)
                ve.tensor_tensor(ck(buf[1])[:, 2 * b:2 * b + 2, :], bank2(b), over2(rstd[:, :]), ALU.mult)\
                  .then_inc(S.acc_read, 1)
            head_norm("k", buf[1], NC, T, "kg", 0)
            pump_to(AT["ffn2"] + AHEAD - 1)
            for b in range(4):
                acc_ready("v", b)
                ve.tensor_tensor(ck(buf[0])[:, 2 * b:2 * b + 2, :], bank2(4 + b), over2(rstd[:, :]), ALU.mult)\
                  .then_inc(S.acc_read, 1)
            gain_operand_lo("ffn2", "ffn1_1")
            for b in range(4):
                dve.wait_ge(S.v_turned, b + 1)
                ve.tensor_copy(buf[2][:, half(b)], psum[:, b, :]).then_inc(S.v_out, 1)
            pump_to(AT["ffn2"] + 7)
            dve.wait_ge(S.ms_psum, NRM["ctx"] + 1)
            ve.tensor_scalar(ms[:, T:2 * T], psum[:, 7, 0:T], 1.0 / D, EPS, ALU.mult, ALU.add).then_inc(S.ms_ready, 1)
            dve.wait_ge(S.root_ready, NRM["ctx"] + 1)
            rc = head_rs[:, T:2 * T]
            link(inverse_root(ms[:, T:2 * T], root_t[:, T:2 * T], rc))
            swiglu("ffn2")

            update_and_operand("ffn2", "mix1", "mix_1", 0.5)
            last_modulation(2)
            pump_to(AT["q"] + AHEAD - 1)
            rms("ffn2")
            pump_to(AT["q"] + 7)
            cx = ck(buf[3])
            for b in range(5):
                if b < 4:
                    for k in (2 * b, 2 * b + 1):
                        ve.scalar_tensor_tensor(cx[:, k, :], cx[:, k, :], ty("Gc", k), rc, ALU.mult, ALU.mult)\
                          .then_inc(S.ctx_full, 1)
                if b:
                    for k in (2 * b - 2, 2 * b - 1):
                        dve.wait_ge(S.ctx_hi, k + 1)
                        ve.scalar_tensor_tensor(u_lo[:, k, T:2 * T], cx[:, k, :], part(0, 0, k, 1),
                                                u_hif[:, k, T:2 * T], ALU.add, ALU.subtract).then_inc(S.ctx_lo, 1)
            for b in range(4):
                acc_ready("q", b)
                ve.tensor_tensor(ck(buf[0])[:, 2 * b:2 * b + 2, :], bank2(b), over2(rstd[:, :]), ALU.mult)\
                  .then_inc(S.acc_read, 1)
            pump_to(AT["q"] + 7 + 3)
            head_norm("q", buf[0], NC, T, "qg", 4, between=lambda: pump_to(AT["wo"] + 4))

            def by_head(t):
                return t.rearrange("p (h c) -> p h c", h=2)

            def mask_scores(g):
                dve.wait_ge(S.z_ready, g + 1)
                if g >= 4:
                    dve.wait_ge(S.o_ready, g - 3)
                if g == 0:
                    dve.wait_ge(S.mixer_consts_in, 16)
                b = 2 * (g % 2)
                ve.scalar_tensor_tensor(by_head(z_slots[g % 4]), psum[:, b:b + 2, 0:STICK], HD ** -0.5,
                                        stick.unsqueeze(1).broadcast_to([P, 2, STICK]), ALU.mult, ALU.add)\
                  .then_inc(S.z_masked, 1)

            def softplus(g):
                dve.wait_ge(S.l_ready, g + 1)
                d = sp_slots[g % 2]
                ve.scalar_tensor_tensor(d, z_slots[g % 4], 0.0, d, ALU.max, ALU.add).then_inc(S.sp_ready, 1)

            mask_scores(0)
            mask_scores(1)
            softplus(0)
            for g in range(NC + 1):
                if g:
                    dve.wait_ge(S.cum_ready, g)
                    z, b = by_head(z_slots[(g - 1) % 4]), 4 + 2 * ((g - 1) % 2)
                    ve.tensor_tensor(z, z, psum[:, b:b + 2, 0:STICK], ALU.subtract).then_inc(S.w_arg, 1)
                if g + 2 < NC:
                    mask_scores(g + 2)
                if g + 1 < NC:
                    softplus(g + 1)
                if g:
                    dve.wait_ge(S.operand_hi, NC * OPS["att"] + g)
                    ve.tensor_tensor(u_lo[:, g - 1, 0:T], psum[:, b, 0:T], u_hif[:, g - 1, 0:T], ALU.subtract)\
                      .then_inc(S.operand_ready, 1)
            pump_to(AT["ffn3"] + AHEAD - 1)
            update_and_operand("wo", "ffn3", "ffn2_1", 1.0)
            pump_to(AT["ffn3"] + 7)
            rms("wo")
            swiglu("ffn3")

            update_x("ffn3", 0.5)
            last_modulation(3)
            modulation_bias(1)
            pump_to(AT["k2"] + AHEAD - 1)
            rms("ffn3")
            normed_operand("even", lambda k: ty("G1", k), lambda k: part(0, 0, k))
            for dst, n, gain in (("H1", 1, "n1_1"), ("H2", 4, "n2_1")):
                scale_gain(dst, 1, n, gain)
            link(ve.tensor_tensor(ty("Gp", n=NC), part(1, 2), col("pscale", n=NC), ALU.mult))
            pump_to(AT["fq2"] + 1 + 2)
            for b in range(4):
                acc_ready("k2", b)
                ve.tensor_copy(buf[1][:, half(b)], psum[:, 4 + b, :]).then_inc(S.acc_read, 1)
            pump_to(AT["v2"] + 2)
            for b in range(4):
                acc_ready("fq2", b)
                ve.tensor_copy(buf[0][:, half(b)], psum[:, b, :]).then_inc(S.acc_read, 1)
            pump_to(AT["v2"] + 3)
            q2 = buf[0][:, 1024:2048]
            head_norm("q2", q2, 4, T, "qg2", 6)
            for b in range(4):
                acc_ready("v2", b)
                ve.tensor_copy(buf[2][:, half(b)], psum[:, b, :]).then_inc(S.acc_read, 1)
            head_norm("k2", buf[1], 4, 512, "kg2", 0, between=lambda: pump_to(AT["four"] + 1))
            tabs = [buf[2], buf[4]]

            def mask_table(n):
                dve.wait_ge(tab_in[n], 16)
                w = tabs[n][:, 0:TABW].rearrange("p (e c) -> p e c", c=HD)
                ve.tensor_tensor(w, w, colmask.unsqueeze(1).broadcast_to([P, TABW // HD, HD]), ALU.add)\
                  .then_inc(S.tab_ready, 1)

            for g in range(4):
                dve.wait_ge(S.mixed_hi, g + 1)
                ve.tensor_tensor(hid_lo[:, g % 2, 0:T], psum[:, 6, 0:T], hid_hif[:, g % 2, 0:T], ALU.subtract)\
                  .then_inc(S.mixed_lo, 1)
                dve.wait_ge(S.operand_hi, NC * OPS["mixed"] + g + 1)
                ve.tensor_tensor(u_lo[:, g, 0:T], psum[:, 7, 0:T], u_hif[:, g, 0:T], ALU.subtract)\
                  .then_inc(S.operand_ready, 1)
                if g == 2:
                    mask_table(0)
            def na_scores(n):
                h, qt = n // 2, n % 2
                s, z = na_slots[n % 4], NA_BANKS[n % 4]
                dve.wait_ge(S.na_z, n + 1)
                if n >= 4:
                    dve.wait_ge(S.na_t, n - 3)
                if h % 4 == 0:
                    dve.wait_ge(S.tab_ready, h // 4 + 1)
                at = (h % 4) * 6 * HD + (2 - 2 * qt) * HD
                ve.scalar_tensor_tensor(s[:, 0:T], psum[:, z, 0:T], HD ** -0.5, tabs[h // 4][:, at:at + T],
                                        ALU.mult, ALU.add)
                ve.tensor_scalar(s[:, T:2 * T], psum[:, z, T:2 * T], HD ** -0.5, None, ALU.mult)\
                  .then_inc(S.na_s, 1)
                dve.wait_ge(S.na_s, n + 1)
                a = 4 * (n % 4)
                link(ve.tensor_reduce(ty("na", a), s, AX_X, ALU.max))
                ve.tensor_scalar(ty("na", a + 1), ty("na", a), -1.0, None, ALU.mult).then_inc(S.na_max, 1)

            def na_normalise(n):
                s, a = na_slots[n % 4], 4 * (n % 4)
                dve.wait_ge(S.na_e, n + 1)
                link(ve.reciprocal(ty("na", a + 3), ty("na", a + 2)))
                ve.tensor_scalar(s, s, ty("na", a + 3), None, ALU.mult).then_inc(S.na_p, 1)

            def na_lo(m):
                dve.wait_ge(S.operand_hi, NC * OPS["mixed"] + 4 + m + 1)
                ve.tensor_tensor(u_lo[:, 4 + m, 0:T], psum[:, 4 + m % 2, 0:T], u_hif[:, 4 + m, 0:T],
                                 ALU.subtract).then_inc(S.operand_ready, 1)

            na_scores(0)
            na_scores(1)
            for n in range(16):
                if n < 14:
                    na_scores(n + 2)
                na_normalise(n)
                if 1 <= n < 6:
                    pump_to(AT["woe"] + n - 1)
                if n == 3:
                    mask_table(1)
                if n % 4 == 1 and n > 4:
                    na_lo(n // 4 - 1)
            na_lo(3)
            pump_to(AT["mlp0"] + AHEAD - 1)
            shift_operand(0)
            for b in range(5):
                if b < 4:
                    update_x("woe", lambda k: part(0, 2, k), [b])
                if b:
                    mlp_operand("mlp0", "G2", b - 1)
            pump_to(AT["mlp0"] + AHEAD + 1)
            rms("woe")
            sqrelu("mlp0")

            update_x("mlp0", lambda k: part(0, 5, k))
            rms("mlp0")
            shift_operand(1)
            for k in range(NC):
                ve.scalar_tensor_tensor(ck(buf[3])[:, k, :], x[:, k, :], ty("H1", k), rstd[:, :], ALU.mult, ALU.mult)\
                  .then_inc(S.pool_norm, 1)
            for g in range(5):
                if g < 4:
                    dve.wait_ge(S.pooled_hi, g + 1)
                    ve.tensor_tensor(u_lo[:, 2 * g:2 * g + 2, 0:T], bank2(4 + g), u_hif[:, 2 * g:2 * g + 2, 0:T],
                                     ALU.subtract).then_inc(S.pooled_lo, 1)
                if g:
                    update_x("pool", lambda k: ty("Gp", k), [g - 1])
                    pump_to(AT["mlp1"] + min(g + 2, 5))
                if g > 1:
                    mlp_operand("mlp1", "H2", g - 2)
            mlp_operand("mlp1", "H2", 3)
            pump_to(AT["mlp1"] + AHEAD + 1)
            rms("pool")
            sqrelu("mlp1")
            update_x("mlp1", lambda k: part(1, 5, k))

        @block.tensor
        def _(pe):
            te = nc.tensor

            def unit_ready(c, i=0):
                pe.wait_ge(S.lo_ready, RING * i + c + 1)

            def operand(name, k):
                pe.wait_ge(S.operand_ready, NC * OPS[name] + k + 1)

            def read(name, b):
                pe.wait_ge(S.acc_read, 4 * RD[name] + b + 1)

            def norm_sum(name):
                n = NRM[name]
                if name in PE_SUMS:
                    for k in range(NC):
                        pe.wait_ge(S.sq_ready, 4 * n + k // 2 + 1)
                        ins = te.matmul(psum[:, NORM_BANK.get(name, 7), 0:T], ones, buf[4][:, k * T:(k + 1) * T], start=k == 0,
                                        stop=k == NC - 1)
                    ins.then_inc(S.ms_psum, 1)
                    return
                pe.wait_ge(S.ssq_ready, POOL_SUMS[name] + 1)
                if n == 0:
                    pe.wait_ge(S.consts_in, 16)
                if name[:3] == "ffn":
                    pe.wait_ge(S.mod_read, MODG * (int(name[3]) + 1))
                te.matmul(psum[:, 7, 0:T], ones, buf[4][:, 0:T], start=True, stop=True).then_inc(S.ms_psum, 1)

            def product(dst, c, at, hi, lo, first, last):
                w = slice((c % RING) * UNIT + at, (c % RING) * UNIT + at + P)
                ins = te.matmul(dst, w_hi[:, w], hi, start=first, stop=False, skip_group_check=True)
                if begun[0] != c:
                    ins.then_inc(S.unit_used, 1)
                    begun[0] = c
                te.matmul(dst, w_hi[:, w], lo, start=False, stop=False, skip_group_check=True)
                return te.matmul(dst, w_lo[:, w], hi, start=False, stop=last, skip_group_check=True)

            begun = [-1]

            def all_k(c, i, dst, op=None, w=T):
                unit_ready(c, i)
                for k in range(NC):
                    if op:
                        operand(op, k)
                    ins = product(dst, c, k * P, u_hi[:, k, 0:w], u_lo[:, k, 0:w], k == 0, k == NC - 1)
                return ins

            def one_k(c, i, hi, lo, b0, first, last, free=None):
                unit_ready(c, i)
                for n in range(NC):
                    if free and n % 2 == 0:
                        free(n // 2)
                    ins = product(bank2(b0 + n // 2)[:, n % 2, :], c, n * P, hi, lo, first and n % 2 == 0, last)
                    if last and n % 2:
                        ins.then_inc(S.acc_ready, 1)

            def project(name, op, b0, free=None, hooks={}, first=0, end=NC, unit0=None):
                for k in range(first, end):
                    operand(op, k)
                    one_k((AT[name] if unit0 is None else unit0) + k - first, 0, u_hi[:, k, 0:T], u_lo[:, k, 0:T], b0, k == 0, k == NC - 1,
                          free if k == 0 else None)
                    if k in hooks:
                        hooks[k]()

            def diagonal_block(name, n, b0, t0):
                c = AT[name] + n // 2
                if n % 2 == 0:
                    unit_ready(c)
                for kk in range(2):
                    for mo in range(2):
                        k = 2 * n + kk
                        ins = product(bank2(b0 + n)[:, mo, :], c, ((n % 2) * 4 + kk * 2 + mo) * P,
                                      u_hi[:, k, t0:t0 + T], u_lo[:, k, t0:t0 + T], kk == 0 and mo == 0, kk == 1)
                ins.then_inc(S.acc_ready, 1)

            def modulate(c, i, q, g):
                unit_ready(c, i)
                if q == 0 and not (isinstance(g, int) and g == 0):
                    pe.wait_ge(S.mod_copied, g)
                if q == 0 and not isinstance(g, int):
                    pe.wait_ge(S.mod_read, g - 1)
                for kk in range(2):
                    at = slice((c % RING) * UNIT + kk * 512, (c % RING) * UNIT + (kk + 1) * 512)
                    k = 2 * q + kk
                    ins = te.matmul(psum[0:4, 6, :], cond[:, k, :], w_hi[:, at], start=k == 0, stop=False,
                                    skip_group_check=True)
                    if kk == 0:
                        ins.then_inc(S.unit_used, 1)
                    ins = te.matmul(psum[0:4, 6, :], cond[:, k, :], w_lo[:, at], start=False, stop=k == NC - 1,
                                    skip_group_check=True)
                if q == 3:
                    ins.then_inc(S.mod_rows, 1)

            def turn_modulation():
                for m in range(4):
                    ins = te.transpose(psum[:, 7, 4 * m:4 * m + 4], mod_rows[:, m * P:(m + 1) * P], ident[0:4, 0:4])
                ins.then_inc(S.mod_turned, 1)

            def up(c, i, j, par, h0, op=None, between=lambda: None):
                if not isinstance(j, int) or j >= 2:
                    pe.wait_ge(S.up_scaled, h0 + j - 1)
                all_k(c, i, bank2(4 + par)[:, 0, :], op)
                between()
                all_k(c + 1, i, bank2(4 + par)[:, 1, :]).then_inc(S.up_ready, 1)

            def swiglu(name, norm):
                c0, h0, g0 = AT[name], STEPS[name], MODG * int(name[3])

                def down(j, par, c, i=0, first=False, last=False):
                    pe.wait_ge(S.hid_ready, h0 + j + 1)
                    one_k(c, i, hid_hi[:, par, 0:T], hid_lo[:, par, 0:T], 0, first, last)

                if g0 == 0:
                    pe.wait_ge(S.cond_ready, 1)
                for q in range(4):
                    modulate(c0 + q, 0, q, g0)
                up(c0 + 4, 0, 0, 0, h0, name, between=lambda: norm_sum(norm))
                up(c0 + 6, 0, 1, 1, h0)
                pe.wait_ge(S.ms_ready, NRM[norm] + 1)
                down(0, 0, c0 + 8, first=True)
                with pe.Fori(0, (FFS - 2) // 4) as i:
                    for s in range(4):
                        j, c = 2 + 4 * i + s, c0 + 9 + 4 * s
                        up(c, 2 * i, j, s % 2, h0)
                        modulate(c + 2, 2 * i, s, g0 + i + 1)
                        if s == 0:
                            turn_modulation()
                        down(j - 1, 1 - s % 2, c + 3, 2 * i)
                down(FFS - 1, 1, c0 + FFU - 1, last=True)
                pe.wait_ge(S.mod_copied, g0 + MODG)
                pe.wait_ge(S.mod_read, g0 + MODG - 1)
                turn_modulation()

            def sqrelu(name, norm):
                c0, h0 = AT[name], STEPS[name]

                def up_pair(c, i, j, par, op=None, between=lambda: None):
                    if not isinstance(j, int) or j >= 2:
                        pe.wait_ge(S.up_scaled, h0 + j - 1)
                    all_k(c, i, psum[:, 4 + 2 * par, 0:TS], op, TS)
                    between()
                    all_k(c + 1, i, psum[:, 5 + 2 * par, 0:TS], w=TS).then_inc(S.up_ready, 1)

                def down(j, par, c, i=0, first=False, last=False):
                    pe.wait_ge(S.hid_ready, h0 + j + 1)
                    for n in range(2):
                        one_k(c + n, i, hid_hi[:, par, n * T:(n + 1) * T], hid_lo[:, par, n * T:(n + 1) * T], 0,
                              first and n == 0, last and n == 1)

                pe.wait_ge(S.shift_lo, 1 if name == "mlp0" else 2)
                up_pair(c0, 0, 0, 0, name, between=lambda: norm_sum(norm))
                pe.wait_ge(S.ms_ready, NRM[norm] + 1)
                up_pair(c0 + 2, 0, 1, 1)
                down(0, 0, c0 + 4, first=True)
                with pe.Fori(0, (MLS - 2) // 2) as i:
                    for s in range(2):
                        j, c = 2 + 2 * i + s, c0 + 6 + 4 * s
                        up_pair(c, i, j, s)
                        down(j - 1, 1 - s, c + 2, i)
                down(MLS - 1, 1, c0 + 4 * MLS - 2, last=True)

            def head_sums(name, sq, chunks, w, free):
                b = HEAD_BANK[name]
                free()
                if name == "k":
                    pe.wait_ge(S.mixer_consts_in, 16)
                for m in range(chunks):
                    pe.wait_ge(S.head_sq, HNP[name] + (m * w) // 512 + 1)
                    ins = te.matmul(psum[0:16, b, 0:w], headsum[:, m, :], sq[:, m * w:(m + 1) * w],
                                    start=m == 0, stop=m == chunks - 1)
                ins.then_inc(S.head_sum, 1)

            def head_spread(name, chunks, w, b0, free=lambda b: None):
                pe.wait_ge(S.head_rs, HN[name] + 1)
                per = 512 // w
                for m in range(chunks):
                    b = b0 + m // per
                    if m % per == 0:
                        free(m // per)
                    ins = te.matmul(psum[:, b, (m % per) * w:(m % per + 1) * w], headbc[:, m, :], head_rs[0:16, 0:w],
                                    start=m % per == 0, stop=True, skip_group_check=True)
                    if m % per == per - 1:
                        ins.then_inc(S.head_bc, 1)

            swiglu("ffn0", "start")

            project("rec", "mix0", 0, lambda b: read("ffn0", b), hooks={1: lambda: norm_sum("ffn0")})
            pe.wait_ge(S.ms_ready, NRM["ffn0"] + 1)
            project("gate", "mix0", 4, end=6)

            def xc_ready(n):
                pe.wait_ge(S.xc_lo, n + 1)

            def r_free(n):
                xc_ready(n)
                read("rec", n)

            def i_free(n):
                pe.wait_ge(S.gates_read, 2 * n + 2)

            for n in range(4):
                r_free(n)
                diagonal_block("r", n, 0, T)
            for n in range(4):
                i_free(n)
                diagonal_block("i", n, 0, T)
            project("gate", "mix0", 4, first=6, unit0=AT["gate_end"])
            pe.wait_ge(S.gates_read, 2 * NC)
            project("wout", "y", 0)
            swiglu("ffn1", "wout")

            def k_sums():
                head_sums("k", buf[4], NC, T, lambda: read("k", 0))

            def k_spread():
                head_spread("k", NC, T, 0, lambda b: read("k", b))

            project("k", "kv", 0, lambda b: read("ffn1", b), hooks={2: lambda: norm_sum("ffn1")})
            pe.wait_ge(S.ms_ready, NRM["ffn1"] + 1)
            project("v", "kv", 4, hooks={1: k_sums, 3: k_spread})
            v_raw = ck(buf[0])
            for b in range(4):
                pe.wait_ge(S.normed, HNP["k"] + b + 1)
                for m in range(4):
                    chunk = 4 * (b % 2) + m
                    read("v", chunk // 2)
                    ins = te.transpose(psum[:, b, m * P:(m + 1) * P], v_raw[:, chunk, (b // 2) * P:(b // 2 + 1) * P],
                                       ident)
                ins.then_inc(S.v_turned, 1)
            swiglu("ffn2", "ctx")

            project("q", "mix1", 0, lambda b: read("ffn2", b), hooks={1: lambda: norm_sum("ffn2")})
            qt_, kt_ = ck(buf[0]), ck(buf[1])
            pe.wait_ge(S.ms_ready, NRM["ffn2"] + 1)
            head_sums("q", buf[4], NC, T, lambda: None)
            head_spread("q", NC, T, 4)

            def scores(g):
                pe.wait_ge(S.normed, HNP["q"] + g // 2 + 1)
                if g < 2:
                    read("q", 3)
                else:
                    pe.wait_ge(S.z_masked, g - 1)
                for h in range(2):
                    b, p0 = 2 * (g % 2) + h, HD * h
                    te.matmul(psum[:, b, 0:T], kt_[p0:p0 + HD, g, 0:P], qt_[p0:p0 + HD, g, :], start=True, stop=True)
                    ins = te.matmul(psum[:, b, T:STICK], kt_[p0:p0 + HD, g, P:T], qt_[p0:p0 + HD, g, P:T],
                                    start=True, stop=True)
                ins.then_inc(S.z_ready, 1)

            def sums_after(g):
                pe.wait_ge(S.sp_ready, g + 1)
                if g < 2:
                    pe.wait_ge(S.normed, HNP["q"] + 4)
                else:
                    operand("att", g - 2)
                for h in range(2):
                    b, s = 4 + 2 * (g % 2) + h, sp_slots[g % 2][:, h * STICK:(h + 1) * STICK]
                    te.matmul(psum[:, b, 0:T], tri, s[:, 0:T], start=True, stop=False, skip_group_check=True)
                    te.matmul(psum[:, b, P:T], ones, s[:, T:STICK], start=False, stop=False, skip_group_check=True)
                    ins = te.matmul(psum[:, b, T:STICK], tri, s[:, T:STICK], start=False, stop=True,
                                    skip_group_check=True)
                ins.then_inc(S.cum_ready, 1)

            def attend(g):
                pe.wait_ge(S.w_ready, g + 1)
                for h in range(2):
                    p0, f = HD * h, (2 * g + h) * HD
                    w = z_slots[g % 4][:, h * STICK:(h + 1) * STICK]
                    dst = psum[p0:p0 + HD, 4 + 2 * (g % 2), 0:T]
                    te.matmul(dst, buf[2][:, f:f + HD], w[:, 0:T], start=True, stop=False, skip_group_check=True)
                    ins = te.matmul(dst[:, P:T], buf[2][:, D + f:D + f + HD], w[:, T:STICK], start=False, stop=True,
                                    skip_group_check=True)
                ins.then_inc(S.o_ready, 1)

            scores(0)
            scores(1)
            for g in range(NC + 1):
                if g + 2 < NC:
                    scores(g + 2)
                if g < NC:
                    sums_after(g)
                if g:
                    attend(g - 1)
            pe.wait_ge(S.z_masked, NC)
            project("wo", "att", 0)
            swiglu("ffn3", "wo")

            pe.wait_ge(S.ctx_lo, NC)
            for n in range(4):
                if n == 0:
                    unit_ready(AT["k2"] + 3)
                if n == 2:
                    pe.wait_ge(S.mod_copied, 4 * MODG)
                if n == 3:
                    pe.wait_ge(S.mod_read, 4 * MODG)
                for k in range(NC):
                    at = ((AT["k2"] + k // 2) % RING) * UNIT + ((k % 2) * 4 + n) * P
                    w, dst = slice(at, at + P), psum[:, 4 + n, T:2 * T]
                    te.matmul(dst, w_hi[:, w], u_hi[:, k, T:2 * T], start=k == 0, stop=False, skip_group_check=True)
                    te.matmul(dst, w_hi[:, w], u_lo[:, k, T:2 * T], start=False, stop=False, skip_group_check=True)
                    te.matmul(dst, w_lo[:, w], u_hi[:, k, T:2 * T], start=False, stop=False, skip_group_check=True)
                if n == 0:
                    norm_sum("ffn3")
            for k in range(NC):
                operand("even", k)
                for n in range(4):
                    ins = product(psum[:, 4 + n, 0:T], AT["k2"] + k // 2, ((k % 2) * 4 + n) * P, u_hi[:, k, 0:T],
                                  u_lo[:, k, 0:T], False, k == NC - 1)
                    if k == NC - 1:
                        ins.then_inc(S.acc_ready, 1)
            pe.wait_ge(S.ms_ready, NRM["ffn3"] + 1)
            project("fq2", "even", 0)
            for k in range(NC):
                c = AT["v2"] + k // 2
                if k % 2 == 0:
                    unit_ready(c)
                for n in range(4):
                    if k == 0:
                        read("fq2", n)
                    ins = product(psum[:, n, :], c, ((k % 2) * 4 + n) * P, u_hi[:, k, :], u_lo[:, k, :], k == 0,
                                  k == NC - 1)
                    if k == NC - 1:
                        ins.then_inc(S.acc_ready, 1)
            head_sums("q2", buf[4], 4, T, lambda: read("k2", 3))
            head_sums("k2", buf[4], 4, 512, lambda: None)
            head_spread("q2", 4, T, 6)
            pe.wait_ge(S.normed, HNP["q2"] + 2)
            f_raw = buf[0][:, 0:1024].rearrange("p (k t) -> p k t", k=4)
            for qt in range(2):
                for g in range(4):
                    ins = te.transpose(psum[:, 6 + qt, g * P:(g + 1) * P], f_raw[:, g, qt * P:(qt + 1) * P], ident)
                ins.then_inc(S.f_turned, 1)
            v2_raw = ck(buf[2], 4)
            read("v2", 3)
            for kt in range(4):
                for m in range(4):
                    ins = te.transpose(psum[:, kt, m * P:(m + 1) * P], v2_raw[:, m, kt * P:(kt + 1) * P], ident)
                ins.then_inc(S.v2_turned, 1)
            dftc = buf5[:, 1024:1024 + 2 * P]

            def token_dft(g):
                if g == 0:
                    pe.wait_ge(S.late_in, 16)
                    pe.wait_ge(S.f_out, 2)
                if g < 2:
                    pe.wait_ge(S.head_ms, HN["q2"] + 1 + g)
                else:
                    pe.wait_ge(S.dft1_out, g - 1)
                for qt in range(2):
                    at = qt * 512
                    ins = te.matmul(psum[:, 4 + g % 2, :], buf[4][:, at + g * P:at + (g + 1) * P],
                                    buf5[:, at:at + 512], start=qt == 0, stop=qt == 1)
                ins.then_inc(S.dft1, 1)

            token_dft(0)
            token_dft(1)
            head_spread("k2", 4, 512, 0, lambda b: pe.wait_ge(S.v2_out, b + 1))
            for g in range(4):
                if 1 <= g < 3:
                    token_dft(g + 1)
                ab = buf[4][:, 1024 + (g % 2) * 512:1536 + (g % 2) * 512]
                pe.wait_ge(S.dft1_out, g + 1)
                if g:
                    pe.wait_ge(S.mixed_lo, g)
                te.matmul(psum[:, 6, 0:T], dftc[:, 0:P], ab[:, 0:T], start=True, stop=False)
                te.matmul(psum[:, 6, 0:T], dftc[:, P:2 * P], ab[:, T:2 * T], start=False, stop=True)\
                  .then_inc(S.dft2, 1)
                pe.wait_ge(S.mixed_lo, g + 1)
                if g:
                    operand("mixed", g - 1)
                c = AT["four"] + g // 2
                unit_ready(c)
                product(psum[:, 7, 0:T], c, (g % 2) * P, hid_hi[:, g % 2, 0:T], hid_lo[:, g % 2, 0:T], True, True)\
                  .then_inc(S.dft3, 1)

            q2, k2 = ck(buf[0])[:, 4:8, :], ck(buf[1], 4)
            vt = ck(buf[3], 4)
            pt = [buf[0][:, 0:1024], buf5[:, 1024:2048]]

            def na_scores(n):
                h, qt = n // 2, n % 2
                m, p0 = h // 2, HD * (h % 2)
                if n == 0:
                    pe.wait_ge(S.normed, HNP["k2"] + 4)
                if n == 2:
                    operand("mixed", 3)
                if n >= 4:
                    pe.wait_ge(S.na_s, n - 3)
                te.matmul(psum[:, NA_BANKS[n % 4], :], q2[p0:p0 + HD, m, qt * P:(qt + 1) * P], k2[p0:p0 + HD, m, :],
                          start=True, stop=True).then_inc(S.na_z, 1)

            def na_turn(n):
                qt = n % 2
                p = na_slots[n % 4]
                pe.wait_ge(S.na_p, n + 1)
                if n >= 2:
                    pe.wait_ge(S.na_tout, n - 1)
                for kt in range(4):
                    ins = te.transpose(psum[:, 2 + qt, kt * P:(kt + 1) * P], p[:, kt * P:(kt + 1) * P], ident)
                ins.then_inc(S.na_t, 1)

            def na_attend(h):
                m, p0 = h // 2, HD * (h % 2)
                pe.wait_ge(S.na_tout, 2 * h + 2)
                if m >= 2:
                    operand("mixed", 4 + m - 2)
                w = pt[h % 2].rearrange("p (k q) -> p k q", k=4)
                for kt in range(4):
                    ins = te.matmul(psum[p0:p0 + HD, 4 + m % 2, 0:T], vt[:, kt, h * HD:(h + 1) * HD], w[:, kt, :],
                                    start=kt == 0, stop=kt == 3)
                ins.then_inc(S.na_o, 1)

            for n in range(3):
                na_scores(n)
            for n in range(16):
                if n < 13:
                    na_scores(n + 3)
                na_turn(n)
                if n % 2 == 0 and n:
                    na_attend(n // 2 - 1)
            na_attend(7)
            project("woe", "mixed", 0)
            sqrelu("mlp0", "woe")

            norm_sum("mlp0")
            for step in range(6):
                if step < 4:
                    g = step
                    pe.wait_ge(S.pool_u, 2 * g + 2)
                    if g == 3:
                        pe.wait_ge(S.ms_ready, NRM["mlp0"] + 1)
                    for qt in range(2):
                        for kk in range(2):
                            ins = te.transpose(psum[:, 4 + g, (2 * qt + kk) * P:(2 * qt + kk + 1) * P],
                                               ck(buf[3])[:, 2 * g + kk, qt * P:(qt + 1) * P], ident)
                    ins.then_inc(S.pool_turned, 1)
                if 1 <= step < 5:
                    g = step - 1
                    pe.wait_ge(S.pool_tok, g + 1)
                    if g == 0:
                        pe.wait_ge(S.poolmat_in, 16)
                    for kk in range(2):
                        for qt in range(2):
                            tok = buf[1][:, g * 512 + (2 * qt + kk) * P:g * 512 + (2 * qt + kk + 1) * P]
                            ins = te.matmul(bank2(4 + g)[:, kk, :], tok, buf[2][:, (4 * qt + g) * T:(4 * qt + g + 1) * T],
                                            start=kk == 0 and qt == 0, stop=qt == 1, skip_group_check=True)
                    ins.then_inc(S.pooled, 1)
                if step >= 2:
                    g = step - 2
                    pe.wait_ge(S.pooled_lo, g + 1)
                    if g == 0:
                        read("mlp0", 3)
                    diagonal_block("pool", g, 0, 0)
            sqrelu("mlp1", "pool")


def weight_stream(w):
    units = np.zeros((UNITS, P, UNIT), np.float32)

    def k_in(m):
        return m.reshape(-1, P, D)

    def n_out(m):
        return m.reshape(NC, P, -1, P).transpose(2, 1, 0, 3).reshape(-1, P, D)

    def blocks(m):
        return m.reshape(2, 2, 2, P, 2, P).transpose(0, 3, 1, 2, 4, 5).reshape(2, P, UNIT)

    def halves(m):
        return m.reshape(4, 2, P, 512).transpose(0, 2, 1, 3).reshape(4, P, UNIT)

    mods = w["w_mod_2"].reshape(2, 4, 2, P, 12, 512).transpose(0, 4, 1, 3, 2, 5).reshape(-1, P, UNIT)

    for f, (w13, w2) in enumerate([("ffn1_w13", "ffn1_w2"), ("ffn2_w13", "ffn2_w2")] * 2):
        l, c0 = f // 2, AT[f"ffn{f}"]
        u13, u2 = n_out(w[w13][l]), k_in(w[w2][l])
        m0 = 4 * MODG * f
        units[c0:c0 + 4] = mods[m0:m0 + 4]
        for j in range(FFS):
            c = c0 + 4 + 2 * j if j < 2 else c0 + 4 * j + 1
            units[c], units[c + 1] = u13[j], u13[FFS + j]
            if j > 1:
                units[c + 2] = mods[m0 + 2 + j]
            if j:
                units[c + (2 if j == 1 else 3)] = u2[j - 1]
        units[c0 + FFU - 1] = u2[FFS - 1]
    for m, name in enumerate(["mlp0", "mlp1"]):
        c0 = AT[name]
        u1, u2 = n_out(w["w_mlp1_2"][m]), k_in(w["w_mlp2_2"][m])
        for j in range(MLS):
            c = c0 + 4 * j - 2 * (j > 0)
            units[c:c + 2] = u1[2 * j:2 * j + 2]
            if j:
                units[c + 2:c + 4] = u2[2 * j - 2:2 * j]
        units[c0 + 4 * MLS - 2:c0 + 4 * MLS] = u2[2 * MLS - 2:]
    a_in, w_even, w_kv = w["a_w_in"][0], w["w_in_even_2"][0], w["w_kv"]
    gate = k_in(a_in[:, :D])
    units[AT["gate"]:AT["gate"] + 6], units[AT["gate_end"]:AT["gate_end"] + 2] = gate[:6], gate[6:]
    whole = {"rec": a_in[:, D:], "wout": w["a_w_out"][0], "k": w_kv[:, :D], "v": w_kv[:, D:],
             "q": w["b_w_q"][0], "wo": w["b_w_o"][0], "fq2": w_even[:, :D], "woe": w["w_out_even_2"][0]}
    for name, m in whole.items():
        units[AT[name]:AT[name] + 8] = k_in(m)
    for name, m in {"r": w["a_w_r"][0], "i": w["a_w_i"][0], "pool": w["w_pool_2"][0]}.items():
        units[AT[name]:AT[name] + 2] = blocks(m)
    units[AT["k2"]:AT["k2"] + 4] = halves(w_even[:, D:D + 512])
    units[AT["v2"]:AT["v2"] + 4] = halves(w_even[:, D + 512:])
    four = w["w_four_2"][0].transpose(1, 0, 2).reshape(P, 4 * P)
    units[AT["four"], :, :2 * P], units[AT["four"] + 1, :, :2 * P] = four[:, :2 * P], four[:, 2 * P:]
    return units.reshape(UNITS // 2, 2, P, UNIT).transpose(0, 2, 1, 3).reshape(UNITS // 2, P, 2 * UNIT)


def by_feature(v):
    return v.reshape(NC, P).T


def small_params(w):
    prm = np.zeros((P, NSMALL), np.float32)
    vectors = [w["ffn1_norm"][0], w["ffn1_norm"][1], w["mix_norm"][0], w["mix_norm"][1], w["kv_norm"],
               w["ffn2_norm"][0], w["ffn2_norm"][1], w["norm1_g_2"][0], w["norm1_g_2"][1], w["norm2_g_2"][0],
               w["norm2_g_2"][1], *w["a_conv_w"][0], w["a_conv_b"][0], w["a_b_r"][0], w["a_b_i"][0],
               w["a_lambda"][0], w["pool_scale_2"][0]]
    for n, v in enumerate(vectors):
        prm[:, NC * n:NC * (n + 1)] = by_feature(v)
    prm[:, COL["cond"]:COL["cond"] + 2 * NC:2] = by_feature(w["c_2"][0])
    prm[:, COL["cond"] + 1:COL["cond"] + 2 * NC:2] = by_feature(w["c_ctx_2"])
    prm[:, COL["bmod"]:COL["bmod"] + 96] = w["b_mod_2"].reshape(96, P).T
    for name, v in (("kg", w["k_norm"]), ("qg", w["q_norm"][0]), ("kg2", w["k_norm_g_2"][0]),
                    ("qg2", w["q_norm_g_2"][0])):
        prm[:HD, COL[name]] = v
        prm[HD:, COL[name]] = v
    return prm


def shape_constants():
    p = np.arange(P)
    cst = np.zeros((P, NCONST), np.float32)
    cst[:, CC["ident"]:CC["ident"] + P] = np.eye(P)
    cst[:, CC["ones"]:CC["ones"] + P] = 1.0
    cst[:, CC["tri"]:CC["tri"] + P] = p[:, None] >= p[None, :]
    for m in range(NC):
        for half in range(2):
            h = 2 * m + half
            cst[HD * half:HD * (half + 1), CC["headsum"] + 16 * m + h] = 1.0
            cst[h, CC["headbc"] + P * m + HD * half:CC["headbc"] + P * m + HD * (half + 1)] = 1.0
    diagonal = np.where(p[:, None] < p[None, :], 0.0, BIG)
    cst[:, CC["stick"]:CC["stick"] + P] = diagonal
    cst[:, CC["stick"] + T:CC["stick"] + STICK] = diagonal
    c = np.arange(64)
    start = np.clip(c - 8, 0, 48)
    window = (c[None, :] >= start[:, None]) & (c[None, :] < start[:, None] + 16)
    cst[:, CC["colmask"]:CC["colmask"] + HD] = np.tile(np.where(window, 0.0, BIG), (2, 1))
    late = np.zeros((P, NLATE), np.float32)
    t = np.arange(T)
    a = 2 * np.pi * (np.outer(t, t) % T) / T
    dft = np.concatenate([np.cos(a), np.sin(a)], 1)
    late[:, :1024] = dft.reshape(2, P, 512).transpose(1, 0, 2).reshape(P, 1024)
    a = 2 * np.pi * (np.outer(p, p) % P) / P
    late[:, 1024:] = np.concatenate([np.cos(a), -np.sin(a)], 1) / np.sqrt(T * P)
    pools = np.zeros((T, 4, T), np.float32)
    for g in range(4):
        w = 2 << g
        lo, hi = np.clip(t - w // 2, 0, T), np.clip(t + w - w // 2, 0, T)
        inside = (t[:, None] >= lo[None, :]) & (t[:, None] < hi[None, :])
        pools[:, g] = np.where(inside, 1.0 / (hi - lo)[None, :], 0.0) - np.eye(T)
    return cst, late, pools.reshape(2, P, 4 * T).transpose(1, 0, 2).reshape(P, 8 * T)


def bias_windows(rpb):
    wide = np.zeros((8, 15, 3 * 64), np.float32)
    wide[:, :, 64:64 + 31] = rpb
    tab = np.zeros((2, P, 4, 6, 64), np.float32)
    for c in range(64):
        at = 64 + 15 - c
        rows = wide[:, :, at:at + 64]
        tab[:, c] = rows[:, 5:11].reshape(2, 4, 6, 64)
        tab[:, 64 + c] = rows[:, 4:10].reshape(2, 4, 6, 64)
    return tab.reshape(2, P, TABW)


def kernel(**inputs):
    import concourse.bacc as bacc
    from concourse.bass_utils import run_bass_kernel_spmd

    w = {k: np.asarray(v) for k, v in inputs.items()}

    def tokens(v):
        return np.ascontiguousarray(v.reshape(T, NC, P).transpose(2, 1, 0).reshape(P, NC * T))

    cst, late, poolmat = shape_constants()
    arrays = {"stream": weight_stream(w), "x_in": tokens(w["x"][0]), "ctx_in": tokens(w["ctx_2"][0]),
              "small": small_params(w), "consts": cst, "late": late, "poolmat": poolmat, "tab": bias_windows(w["rpb_2"][0])}
    nc = bacc.Bacc("TRN2", target_bir_lowering=False, num_devices=1)
    args = {}
    for name, a in arrays.items():
        arrays[name] = np.ascontiguousarray(a)
        args[name] = nc.dram_tensor(name, a.shape, mybir.dt.from_np(a.dtype), kind="ExternalInput").ap()
    out = nc.dram_tensor("out", (P, NC * T), F32, kind="ExternalOutput").ap()
    build(nc, out=out, **args)
    got = run_bass_kernel_spmd(nc, [arrays], core_ids=[0]).results[0]["out"]
    return got.reshape(P, NC, T).transpose(2, 1, 0).reshape(1, T, D)
```
